# Optimizing a Trainium2 kernel written in Bass

```python
import jax, jax.numpy as jnp
from jax import lax
import numpy as np
import math

D_MODEL = 1024
BATCH = 1
SEQ = 512
DEPTH = 2

BRANCH_W = D_MODEL // 2
N_BRANCHES = 3
POOL_WINDOWS = (2, 4, 8, 16)
POOL_GROUPS = 4
POOL_GROUP_W = BRANCH_W // POOL_GROUPS
RET_HEADS = 4
RET_HEAD_DIM = BRANCH_W // RET_HEADS
RET_CHUNK = 128
ROPE_BASE = 10000.0
RWKV_HEAD_DIM = 64
RWKV_HEADS = BRANCH_W // RWKV_HEAD_DIM
RWKV_W_LORA = 64
RWKV_A_LORA = 64
RWKV_SHIFT_W = 3 * BRANCH_W + RWKV_W_LORA + RWKV_A_LORA
IN_SPLIT_SIZES = (BRANCH_W, BRANCH_W, BRANCH_W, BRANCH_W, BRANCH_W, BRANCH_W,
                  RWKV_SHIFT_W, BRANCH_W, N_BRANCHES * D_MODEL)
D_IN = sum(IN_SPLIT_SIZES)
NORM_EPS = 1e-6
RET_NORM_EPS = 1e-5
RWKV_NORM_EPS = 64e-5


def rms_norm(x, g):
    x32 = x.astype(jnp.float32)
    y = x32 * lax.rsqrt(jnp.mean(x32 * x32, axis=-1, keepdims=True) + NORM_EPS)
    return (y * g).astype(x.dtype)

def head_norm(x, eps):
    x32 = x.astype(jnp.float32)
    mu = jnp.mean(x32, axis=-1, keepdims=True)
    xc = x32 - mu
    var = jnp.mean(xc * xc, axis=-1, keepdims=True)
    return xc * lax.rsqrt(var + eps)

def causal_pool_mixer(u, pool_w, pool_scale):
    B, T, _ = u.shape
    u32 = u.astype(jnp.float32)
    cs_pad = jnp.pad(jnp.cumsum(u32, axis=1), ((0, 0), (1, 0), (0, 0)))
    t_idx = jnp.arange(T)
    outs = []
    for gi, w in enumerate(POOL_WINDOWS):
        sl = slice(gi * POOL_GROUP_W, (gi + 1) * POOL_GROUP_W)
        c = cs_pad[..., sl]
        lower = jnp.pad(c[:, :T + 1 - w], ((0, 0), (w - 1, 0), (0, 0)))
        win_sum = c[:, 1:] - lower
        count = jnp.minimum(t_idx + 1, w).astype(jnp.float32)[None, :, None]
        outs.append(win_sum / count - u32[..., sl])
    d = jnp.stack(outs, axis=2).astype(u.dtype)
    y = jnp.einsum('btgc,gcd->btgd', d, pool_w).reshape(B, T, BRANCH_W)
    return y * pool_scale

def rotary(x, positions):
    half = x.shape[-1] // 2
    freqs = ROPE_BASE ** (-jnp.arange(half, dtype=jnp.float32) / half)
    ang = positions.astype(jnp.float32)[..., None] * freqs
    cos = jnp.cos(ang)[:, :, None, :]
    sin = jnp.sin(ang)[:, :, None, :]
    x32 = x.astype(jnp.float32)
    x1, x2 = x32[..., :half], x32[..., half:]
    return jnp.concatenate([x1 * cos - x2 * sin, x1 * sin + x2 * cos], axis=-1)

def retention(q, k, v, positions, ret_norm_g):
    dtype = q.dtype
    B, T, _ = q.shape
    H, dh, C = RET_HEADS, RET_HEAD_DIM, RET_CHUNK
    N = T // C
    qh = rotary(q.reshape(B, T, H, dh), positions)
    kh = rotary(k.reshape(B, T, H, dh), positions) * (dh ** -0.5)
    vh = v.reshape(B, T, H, dh).astype(jnp.float32)

    def to_chunks(a):
        return a.reshape(B, N, C, H, dh).transpose(0, 3, 1, 2, 4)

    qc, kc, vc = to_chunks(qh), to_chunks(kh), to_chunks(vh)
    log_gamma = jnp.log1p(-(2.0 ** (-5.0 - jnp.arange(H, dtype=jnp.float32))))
    i = jnp.arange(C, dtype=jnp.float32)
    diff = i[:, None] - i[None, :]
    decay_mask = jnp.where(diff >= 0,
                           jnp.exp(log_gamma[:, None, None] * jnp.maximum(diff, 0.0)),
                           0.0)
    scores = jnp.einsum('bhnid,bhnjd->bhnij', qc, kc) * decay_mask[None, :, None]
    o_intra = jnp.einsum('bhnij,bhnje->bhnie', scores, vc)
    k_tail = kc * jnp.exp(log_gamma[:, None] * (C - 1 - i))[None, :, None, :, None]
    kv = jnp.einsum('bhnjd,bhnje->bhnde', k_tail, vc)
    chunk_decay = jnp.exp(log_gamma * C)[None, :, None, None]

    def step(R, kv_n):
        return chunk_decay * R + kv_n, R

    _, R_prev = lax.scan(step, jnp.zeros((B, H, dh, dh), jnp.float32), jnp.moveaxis(kv, 2, 0))
    R_prev = jnp.moveaxis(R_prev, 0, 2)
    q_dec = qc * jnp.exp(log_gamma[:, None] * (i + 1.0))[None, :, None, :, None]
    o = o_intra + jnp.einsum('bhnid,bhnde->bhnie', q_dec, R_prev)
    o = o.transpose(0, 2, 3, 1, 4).reshape(B, T, H, dh)
    o = head_norm(o, RET_NORM_EPS).reshape(B, T, BRANCH_W) * ret_norm_g
    return o.astype(dtype)

def rwkv7_time_mix(p, shift_mu, w0, w2, a0, a2, k_k, k_a, r_k, ln_w, ln_b):
    dtype = p.dtype
    B, T, _ = p.shape
    H, N = RWKV_HEADS, RWKV_HEAD_DIM
    p_prev = jnp.pad(p[:, :-1], ((0, 0), (1, 0), (0, 0)))
    p = p + (p_prev - p) * shift_mu
    split_pts = (BRANCH_W, BRANCH_W + RWKV_W_LORA, 2 * BRANCH_W + RWKV_W_LORA,
                 3 * BRANCH_W + RWKV_W_LORA)
    r, wl, k, v, al = jnp.split(p, split_pts, axis=-1)
    w = -jax.nn.softplus(-(w0 + jnp.tanh(wl) @ w2)) - 0.5
    decay = jnp.exp(-jnp.exp(w.astype(jnp.float32)))
    a = jax.nn.sigmoid(a0 + al @ a2)

    def heads(z):
        return z.reshape(B, T, H, N).astype(jnp.float32)

    kk = heads(k * k_k)
    kk = kk / jnp.maximum(jnp.sqrt(jnp.sum(kk * kk, axis=-1, keepdims=True)), 1e-12)
    k = k * (1.0 + (a - 1.0) * k_a)
    r_h, k_h, v_h, a_h, w_h = heads(r), heads(k), heads(v), heads(a), heads(decay)
    xs = tuple(jnp.moveaxis(z, 1, 0) for z in (r_h, w_h, k_h, v_h, -kk, kk * a_h))

    def step(S, inp):
        r_t, w_t, k_t, v_t, a_t, b_t = inp
        sa = jnp.einsum('bhvk,bhk->bhv', S, a_t)
        S = (S * w_t[:, :, None, :] + sa[..., None] * b_t[:, :, None, :]
             + v_t[..., None] * k_t[:, :, None, :])
        return S, jnp.einsum('bhvk,bhk->bhv', S, r_t)

    _, y = lax.scan(step, jnp.zeros((B, H, N, N), jnp.float32), xs)
    y = jnp.moveaxis(y, 0, 1)
    y = head_norm(y, RWKV_NORM_EPS).reshape(B, T, BRANCH_W) * ln_w + ln_b
    bonus = jnp.sum(r_h * k_h * r_k, axis=-1, keepdims=True) * v_h
    y = y + bonus.reshape(B, T, BRANCH_W)
    return y.astype(dtype)

def hybrid_layer(x, c_act, positions, norm_g, w_ada, b_ada, w_in, pool_w, pool_scale,
                 ret_norm_g, shift_mu, w0, w2, a0, a2, k_k, k_a, r_k, ln_w, ln_b,
                 w_branch, w_out):
    B, T, D = x.shape
    mod = c_act @ w_ada + b_ada
    shift, scale, gate = jnp.split(mod[:, None, :], 3, axis=-1)
    h = rms_norm(x, norm_g) * (1.0 + scale) + shift
    proj = h @ w_in
    points = np.cumsum(IN_SPLIT_SIZES)[:-1].tolist()
    pool_u, pool_g, q, k, v, ret_g, rw, rw_g, gate_logits = jnp.split(proj, points, axis=-1)
    o_pool = causal_pool_mixer(pool_u, pool_w, pool_scale) * jax.nn.silu(pool_g)
    o_ret = retention(q, k, v, positions, ret_norm_g) * jax.nn.silu(ret_g)
    o_rwkv = rwkv7_time_mix(rw, shift_mu, w0, w2, a0, a2, k_k, k_a, r_k,
                            ln_w, ln_b) * jax.nn.silu(rw_g)
    branches = jnp.stack([o_pool, o_ret, o_rwkv], axis=2)
    y = jnp.einsum('btnw,nwd->btnd', branches, w_branch)
    gates = jax.nn.sigmoid(gate_logits.reshape(B, T, N_BRANCHES, D))
    merged = jnp.sum(gates * y, axis=2)
    return x + gate * (merged @ w_out)

def first_inputs(seed: int = 0) -> dict:
    key = jax.random.key(seed)
    ks = jax.random.split(key, 24)
    L, D, W = DEPTH, D_MODEL, BRANCH_W
    nrm = jax.random.normal
    f32 = jnp.float32
    return {
        "x": nrm(ks[0], (BATCH, SEQ, D), f32),
        "c": nrm(ks[1], (BATCH, D), f32),
        "positions": jnp.broadcast_to(jnp.arange(SEQ, dtype=jnp.int32), (BATCH, SEQ)),
        "norm_g": 1.0 + 0.05 * nrm(ks[2], (L, D), f32),
        "w_ada": 0.5 * D ** -0.5 * nrm(ks[3], (L, D, 3 * D), f32),
        "b_ada": 0.01 * nrm(ks[4], (L, 3 * D), f32),
        "w_in": D ** -0.5 * nrm(ks[5], (L, D, D_IN), f32),
        "pool_w": POOL_GROUP_W ** -0.5 * nrm(ks[6], (L, POOL_GROUPS, POOL_GROUP_W, POOL_GROUP_W), f32),
        "pool_scale": 1.0 + 0.1 * nrm(ks[7], (L, W), f32),
        "ret_norm_g": 1.0 + 0.05 * nrm(ks[8], (L, W), f32),
        "rwkv_shift_mu": jax.random.uniform(ks[9], (L, RWKV_SHIFT_W), f32),
        "rwkv_w0": jax.random.uniform(ks[10], (L, W), f32, -6.0, 1.0),
        "rwkv_w2": 0.5 * RWKV_W_LORA ** -0.5 * nrm(ks[11], (L, RWKV_W_LORA, W), f32),
        "rwkv_a0": 0.1 * nrm(ks[12], (L, W), f32),
        "rwkv_a2": 0.5 * RWKV_A_LORA ** -0.5 * nrm(ks[13], (L, RWKV_A_LORA, W), f32),
        "rwkv_k_k": 0.85 + 0.05 * nrm(ks[14], (L, W), f32),
        "rwkv_k_a": 1.0 + 0.05 * nrm(ks[15], (L, W), f32),
        "rwkv_r_k": 0.1 * nrm(ks[16], (L, RWKV_HEADS, RWKV_HEAD_DIM), f32),
        "rwkv_ln_w": 1.0 + 0.05 * nrm(ks[17], (L, W), f32),
        "rwkv_ln_b": 0.01 * nrm(ks[18], (L, W), f32),
        "w_branch": W ** -0.5 * nrm(ks[19], (L, N_BRANCHES, W, D), f32),
        "w_out": D ** -0.5 * nrm(ks[20], (L, D, D), f32),
        "final_g": 1.0 + 0.05 * nrm(ks[21], (D,), f32),
    }

def first_block(x, c, positions, norm_g, w_ada, b_ada, w_in, pool_w, pool_scale, ret_norm_g,
              rwkv_shift_mu, rwkv_w0, rwkv_w2, rwkv_a0, rwkv_a2, rwkv_k_k, rwkv_k_a,
              rwkv_r_k, rwkv_ln_w, rwkv_ln_b, w_branch, w_out, final_g):
    c_act = jax.nn.silu(c)
    for l in range(DEPTH):
        x = hybrid_layer(x, c_act, positions, norm_g[l], w_ada[l], b_ada[l], w_in[l],
                         pool_w[l], pool_scale[l], ret_norm_g[l], rwkv_shift_mu[l],
                         rwkv_w0[l], rwkv_w2[l], rwkv_a0[l], rwkv_a2[l], rwkv_k_k[l],
                         rwkv_k_a[l], rwkv_r_k[l], rwkv_ln_w[l], rwkv_ln_b[l],
                         w_branch[l], w_out[l])
    return rms_norm(x, final_g)


D_MIX = D_MODEL
HEAD_DIM = 64
D_SC = D_MIX // 4
D_ATT = D_MIX // 2
D_CC = D_MIX // 4
N_Q_HEADS = D_ATT // HEAD_DIM
N_KV_HEADS = 2
GQA_GROUP = N_Q_HEADS // N_KV_HEADS
SC_WIDTH = 3
CC_WIDTH = 31
WINDOW = 128
BLOCK = 128
ROPE_THETA = 10000.0
D_FF = 2816
LN_EPS = 1e-5
ALPHA = (2.0 * DEPTH) ** 0.25
BETA = (8.0 * DEPTH) ** -0.25
IN_SIZES = (D_SC, D_SC, D_SC, N_Q_HEADS * HEAD_DIM, N_KV_HEADS * HEAD_DIM, N_KV_HEADS * HEAD_DIM, D_CC, D_CC)
D_IN_2 = sum(IN_SIZES)
IN_OFFSETS = tuple(int(v) for v in np.cumsum(IN_SIZES)[:-1])


def layer_norm(x, g, b):
    xf = x.astype(jnp.float32)
    mu = jnp.mean(xf, axis=-1, keepdims=True)
    var = jnp.mean(jnp.square(xf - mu), axis=-1, keepdims=True)
    y = (xf - mu) * lax.rsqrt(var + LN_EPS)
    return (y * g.astype(jnp.float32) + b.astype(jnp.float32)).astype(x.dtype)

def swiglu(x, w_gu, w_down):
    g, u = jnp.split(x @ w_gu, 2, axis=-1)
    return (jax.nn.silu(g) * u) @ w_down

def depthwise_conv(x, w):
    k = w.shape[0]
    pad = (k - 1) // 2
    return lax.conv_general_dilated(
        x, w[:, None, :].astype(x.dtype), window_strides=(1,), padding=[(pad, pad)],
        dimension_numbers=("NWC", "WIO", "NWC"), feature_group_count=x.shape[-1])

def rope(x, positions):
    half = HEAD_DIM // 2
    inv_freq = ROPE_THETA ** (-jnp.arange(half, dtype=jnp.float32) / half)
    ang = positions.astype(jnp.float32)[:, None] * inv_freq[None, :]
    cos = jnp.cos(ang)[None, :, None, :]
    sin = jnp.sin(ang)[None, :, None, :]
    xf = x.astype(jnp.float32)
    x1, x2 = xf[..., :half], xf[..., half:]
    return jnp.concatenate([x1 * cos - x2 * sin, x2 * cos + x1 * sin], axis=-1).astype(x.dtype)

def banded_window_attention(q, k, v, sink):
    b, s = q.shape[0], q.shape[1]
    nb = s // BLOCK
    qb = q.reshape(b, nb, BLOCK, N_KV_HEADS, GQA_GROUP, HEAD_DIM)

    def band(t):
        tp = jnp.pad(t, ((0, 0), (BLOCK, BLOCK), (0, 0), (0, 0)))
        parts = [tp[:, o * BLOCK:o * BLOCK + s].reshape(b, nb, BLOCK, N_KV_HEADS, HEAD_DIM) for o in range(3)]
        return jnp.concatenate(parts, axis=2)

    kb, vb = band(k), band(v)
    scores = jnp.einsum("bnqkgd,bnskd->bnkgqs", qb, kb).astype(jnp.float32) * (HEAD_DIM ** -0.5)
    qpos = jnp.arange(s).reshape(nb, BLOCK)
    kpos = jnp.arange(nb)[:, None] * BLOCK - BLOCK + jnp.arange(3 * BLOCK)[None, :]
    valid = (jnp.abs(qpos[:, :, None] - kpos[:, None, :]) <= WINDOW) \
        & (kpos >= 0)[:, None, :] & (kpos < s)[:, None, :]
    scores = jnp.where(valid[None, :, None, None], scores, -1e30)
    sink_f = sink.astype(jnp.float32).reshape(N_KV_HEADS, GQA_GROUP)[None, None, :, :, None]
    m = jnp.maximum(jnp.max(scores, axis=-1), sink_f)
    p = jnp.exp(scores - m[..., None])
    denom = jnp.sum(p, axis=-1) + jnp.exp(sink_f - m)
    o = jnp.einsum("bnkgqs,bnskd->bnqkgd", p.astype(v.dtype), vb).astype(jnp.float32)
    o = o / jnp.transpose(denom, (0, 1, 4, 2, 3))[..., None]
    return o.reshape(b, s, D_ATT).astype(q.dtype)

def hybrid_mixer(x, w_in, sc_conv_w, attn_sink, cc_conv_w, cc_conv_b, cc_ln_g, cc_ln_b, w_out):
    b, s, _ = x.shape
    positions = jnp.arange(s)
    z = x @ w_in
    sc_b, sc_c, sc_h, q, k, v, cc_a, cc_gate = jnp.split(z, IN_OFFSETS, axis=-1)
    y_sc = sc_b * depthwise_conv(sc_c * sc_h, sc_conv_w)
    q = rope(q.reshape(b, s, N_Q_HEADS, HEAD_DIM), positions)
    k = rope(k.reshape(b, s, N_KV_HEADS, HEAD_DIM), positions)
    v = v.reshape(b, s, N_KV_HEADS, HEAD_DIM)
    y_att = banded_window_attention(q, k, v, attn_sink)
    u = cc_a * jax.nn.sigmoid(cc_gate)
    u = depthwise_conv(u, cc_conv_w) + cc_conv_b
    y_cc = jax.nn.silu(layer_norm(u, cc_ln_g, cc_ln_b))
    return jnp.concatenate([y_sc, y_att, y_cc], axis=-1) @ w_out

def second_inputs(seed: int = 0) -> dict:
    key = jax.random.key(seed)
    ks = jax.random.split(key, 24)
    f32 = jnp.float32

    def nrm(k, shape, scale):
        return jax.random.normal(k, shape, f32) * scale

    def gain(k, n):
        return 1.0 + 0.02 * jax.random.normal(k, (DEPTH, n), f32)

    return {
        "x": jax.random.normal(ks[0], (BATCH, SEQ, D_MODEL), f32),
        "ffn1_w_gu": nrm(ks[1], (DEPTH, D_MODEL, 2 * D_FF), D_MODEL ** -0.5),
        "ffn1_w_down": nrm(ks[2], (DEPTH, D_FF, D_MODEL), BETA * D_FF ** -0.5),
        "ln1_g": gain(ks[3], D_MODEL),
        "ln1_b": nrm(ks[4], (DEPTH, D_MODEL), 0.02),
        "w_in": nrm(ks[5], (DEPTH, D_MODEL, D_IN_2), D_MODEL ** -0.5),
        "sc_conv_w": nrm(ks[6], (DEPTH, SC_WIDTH, D_SC), SC_WIDTH ** -0.5),
        "attn_sink": nrm(ks[7], (DEPTH, N_Q_HEADS), 0.5),
        "cc_conv_w": nrm(ks[8], (DEPTH, CC_WIDTH, D_CC), CC_WIDTH ** -0.5),
        "cc_conv_b": nrm(ks[9], (DEPTH, D_CC), 0.02),
        "cc_ln_g": gain(ks[10], D_CC),
        "cc_ln_b": nrm(ks[11], (DEPTH, D_CC), 0.02),
        "w_out": nrm(ks[12], (DEPTH, D_MIX, D_MODEL), BETA * D_MIX ** -0.5),
        "ln2_g": gain(ks[13], D_MODEL),
        "ln2_b": nrm(ks[14], (DEPTH, D_MODEL), 0.02),
        "ffn2_w_gu": nrm(ks[15], (DEPTH, D_MODEL, 2 * D_FF), D_MODEL ** -0.5),
        "ffn2_w_down": nrm(ks[16], (DEPTH, D_FF, D_MODEL), BETA * D_FF ** -0.5),
        "ln3_g": gain(ks[17], D_MODEL),
        "ln3_b": nrm(ks[18], (DEPTH, D_MODEL), 0.02),
    }

def second_block(x, ffn1_w_gu, ffn1_w_down, ln1_g, ln1_b, w_in, sc_conv_w, attn_sink, cc_conv_w,
              cc_conv_b, cc_ln_g, cc_ln_b, w_out, ln2_g, ln2_b, ffn2_w_gu, ffn2_w_down, ln3_g, ln3_b):
    for l in range(DEPTH):
        x = layer_norm(ALPHA * x + 0.5 * swiglu(x, ffn1_w_gu[l], ffn1_w_down[l]), ln1_g[l], ln1_b[l])
        x = layer_norm(ALPHA * x + hybrid_mixer(x, w_in[l], sc_conv_w[l], attn_sink[l], cc_conv_w[l],
                                                 cc_conv_b[l], cc_ln_g[l], cc_ln_b[l], w_out[l]),
                       ln2_g[l], ln2_b[l])
        x = layer_norm(ALPHA * x + 0.5 * swiglu(x, ffn2_w_gu[l], ffn2_w_down[l]), ln3_g[l], ln3_b[l])
    return x


def setup_inputs(seed=0):
    out = dict(first_inputs(seed))
    for name, value in second_inputs(seed + 1).items():
        if name != "x":
            out[name + "_2"] = value
    return out


def reference(
    x, c, positions, norm_g, w_ada, b_ada, w_in, pool_w, pool_scale, ret_norm_g, rwkv_shift_mu,
    rwkv_w0, rwkv_w2, rwkv_a0, rwkv_a2, rwkv_k_k, rwkv_k_a, rwkv_r_k, rwkv_ln_w, rwkv_ln_b,
    w_branch, w_out, final_g, ffn1_w_gu_2, ffn1_w_down_2, ln1_g_2, ln1_b_2, w_in_2, sc_conv_w_2,
    attn_sink_2, cc_conv_w_2, cc_conv_b_2, cc_ln_g_2, cc_ln_b_2, w_out_2, ln2_g_2, ln2_b_2,
    ffn2_w_gu_2, ffn2_w_down_2, ln3_g_2, ln3_b_2,
):
    x = first_block(
        x, c, positions, norm_g, w_ada, b_ada, w_in, pool_w, pool_scale, ret_norm_g,
        rwkv_shift_mu, rwkv_w0, rwkv_w2, rwkv_a0, rwkv_a2, rwkv_k_k, rwkv_k_a, rwkv_r_k,
        rwkv_ln_w, rwkv_ln_b, w_branch, w_out, final_g,
    )
    return second_block(
        x, ffn1_w_gu_2, ffn1_w_down_2, ln1_g_2, ln1_b_2, w_in_2, sc_conv_w_2, attn_sink_2,
        cc_conv_w_2, cc_conv_b_2, cc_ln_g_2, cc_ln_b_2, w_out_2, ln2_g_2, ln2_b_2, ffn2_w_gu_2,
        ffn2_w_down_2, ln3_g_2, ln3_b_2,
    )


_drawn_inputs = setup_inputs


def setup_inputs(seed=0):
    import zlib

    import numpy as np

    out = dict(_drawn_inputs(seed))
    spreads = {}
    factors = {'b_ada': 4.332,
     'pool_scale': 3.501,
     'ret_norm_g': 6.714,
     'rwkv_w2': 7.247,
     'rwkv_a0': 7.234,
     'rwkv_k_k': 4.161,
     'rwkv_k_a': 4.036,
     'rwkv_ln_w': 6.194,
     'rwkv_ln_b': 40.415,
     'attn_sink_2': 8.0,
     'cc_conv_b_2': 8.0,
     'cc_ln_g_2': 8.0,
     'cc_ln_b_2': 8.0}
    for name, (base, spread) in spreads.items():
        noise = np.random.default_rng([zlib.crc32(name.encode()), seed]).standard_normal(out[name].shape)
        drawn = base * np.exp(spread * noise) if base else spread * noise
        out[name] = __import__('jax').numpy.asarray(drawn.astype(out[name].dtype))
    for name, factor in factors.items():
        out[name] = (out[name] * factor).astype(out[name].dtype)
    return out
```

```python
from contextlib import ExitStack

import numpy as np
import concourse.bass as bass
from concourse import mybir

F32 = mybir.dt.float32
FR = mybir.dt.float32r
I32 = mybir.dt.int32
U32 = mybir.dt.uint32
ALU = mybir.AluOpType
ACT = mybir.ActivationFunctionType
AX = mybir.AxisListType

T = 512
D = 1024
DEPTH = 2
FF = 2816
NFF = FF // 128
RAW = 3
RING = 4
ALPHA = (2.0 * DEPTH) ** 0.25
KAPPA = float(np.exp(-0.5))
POOLW = (2, 4, 8, 16)


class Columns:

    def __init__(self):
        self.pieces = []
        self.at = {}

    def add(self, key, name, index, spans):
        self.at[key] = len(self.pieces)
        flat = [(name, index, s, n) for s, n in spans]
        col, room = [], 128
        for name_, ix, s, n in flat:
            while n:
                m = min(n, room)
                col.append((name_, ix, s, m))
                s, n, room = s + m, n - m, room - m
                if room == 0:
                    self.pieces.append(col)
                    col, room = [], 128


def columns():
    c = Columns()
    full = [(0, 512)]
    for l in range(DEPTH):
        c.add(("norm_g", l), "norm_g", (l,), [(0, 1024)])
        c.add(("b_ada", l), "b_ada", (l,), [(0, 2048)])
        c.add(("pool_scale", l), "pool_scale", (l,), full)
        c.add(("ret_g", l), "ret_norm_g", (l,), full)
        c.add(("mu_r", l), "rwkv_shift_mu", (l,), [(0, 512)])
        c.add(("mu_k", l), "rwkv_shift_mu", (l,), [(576, 512)])
        c.add(("mu_v", l), "rwkv_shift_mu", (l,), [(1088, 512)])
        c.add(("mu_wa", l), "rwkv_shift_mu", (l,), [(512, 64), (1600, 64)])
        for k, n in (("w0", "rwkv_w0"), ("a0", "rwkv_a0"), ("k_k", "rwkv_k_k"), ("k_a", "rwkv_k_a"),
                     ("r_k", "rwkv_r_k"), ("ln_w", "rwkv_ln_w"), ("ln_b", "rwkv_ln_b")):
            c.add((k, l), n, (l,), full)
        for k in ("ln1", "ln2", "ln3"):
            c.add((k + "g", l), k + "_g_2", (l,), [(0, 1024)])
            c.add((k + "b", l), k + "_b_2", (l,), [(0, 1024)])
        for j in range(3):
            c.add(("sc", l, j), "sc_conv_w_2", (l, j), [(0, 256)])
        for j in range(31):
            c.add(("cc", l, j), "cc_conv_w_2", (l, j), [(0, 256)])
        c.add(("cc_b", l), "cc_conv_b_2", (l,), [(0, 256)])
        c.add(("cc_lg", l), "cc_ln_g_2", (l,), [(0, 256)])
        c.add(("cc_lb", l), "cc_ln_b_2", (l,), [(0, 256)])
    c.add(("final_g",), "final_g", (), [(0, 1024)])
    c.add(("c",), "c", (0,), [(0, 1024)])
    return c


def constants():
    p = np.arange(128)
    i = np.arange(512)
    out = {}
    out["ident"] = np.eye(128, dtype=np.float32)
    out["blk64"] = (p[:, None] // 64 == p[None, :] // 64).astype(np.float32)
    out["mean256"] = np.full((128, 128), 1.0 / 256, np.float32)
    half = 64
    fr = (np.float32(10000.0) ** (-np.arange(half, dtype=np.float32) / half)).astype(np.float32)
    sign = np.where(p < 64, -1.0, 1.0).astype(np.float32)
    out["misc"] = np.stack([fr[p % 64], sign], 1).astype(np.float32)
    lg = np.log1p(-(2.0 ** (-5.0 - np.arange(4))))
    dm = np.zeros((128, 4, 512), np.float64)
    for h in range(4):
        d = i[None, :] - p[:, None]
        dm[:, h] = np.where(d >= 0, np.exp(lg[h] * np.maximum(d, 0)), 0) * 128.0 ** -0.5
    out["decay"] = dm.reshape(128, 2048).astype(np.float32)
    s, t = p[:, None], p[None, :]
    strict, incl = (s < t), (s <= t)
    out["gmask"] = np.concatenate([strict, incl, strict, incl], 1).astype(np.float32)
    out["m1"] = ((s // 2 == t // 2) & (s < t)).astype(np.float32)
    lm = []
    for n in (2, 4, 8, 16):
        x = (p[:, None] // (2 * n) == p[None, :] // (2 * n)) & (p[:, None] % (2 * n) >= n) & (p[None, :] % (2 * n) < n)
        lm += [x, x.T]
    out["lmask"] = np.concatenate(lm, 1).astype(np.uint32)
    out["reset"] = np.broadcast_to((i % 128 != 0).astype(np.float32), (128, 512)).copy()
    cnt = np.stack([1.0 / np.minimum(i + 1, w) for w in POOLW]).reshape(-1)
    out["invcnt"] = np.broadcast_to(cnt.astype(np.float32), (128, 2048)).copy()
    inv = (np.float32(10000.0) ** (-np.arange(32, dtype=np.float32) / 32)).astype(np.float32)
    ang = (i.astype(np.float32)[None, :] * inv[p % 32][:, None]).astype(np.float32).astype(np.float64)
    sg = np.where(p % 64 < 32, -1.0, 1.0)[:, None]
    out["rcos"] = np.cos(ang).astype(np.float32)
    out["rsin"] = (np.sin(ang) * sg).astype(np.float32)
    j = np.arange(384)[None, :] - 128
    out["amask"] = np.where(np.abs(p[:, None] - j) <= 128, 0.0, -1e30).astype(np.float32)
    return out


def pack_units(units, inputs):
    out = np.empty((len(units), 128, 1024), np.float32)
    for n, (name, index, pieces) in enumerate(units):
        w = inputs[name][index]
        at = 0
        for k, c, m in pieces:
            out[n, :, at:at + m] = w[k:k + 128, c:c + m]
            at += m
    return out


def t_pieces(col, k0=0, nk=8, groups=1):
    return tuple((k0 + 128 * k, col + 128 * g, 128) for g in range(groups) for k in range(nk))


def n_pieces(k, col):
    return ((k, col, 512), (k + 128, col, 512))


class Queue:

    def __init__(self, sem, serial):
        self.sem, self.serial = sem, serial
        self.n, self.seen, self.todo = 0, {}, []

    def wait(self, *tokens):
        for t in tokens:
            if isinstance(t, list):
                self.wait(*t)
            elif t is not None and self.seen.get(id(t[0]), 0) < t[1]:
                self.seen[id(t[0])] = t[1]
                self.todo.append(lambda e, t=t: e.wait_ge(t[0], t[1]))

    def __call__(self, fn, *tokens, signal=True):
        self.wait(*tokens)
        if self.serial and self.n:
            self.wait((self.sem, self.n))
        if not signal:
            self.todo.append(fn)
            return None
        self.n += 1
        self.todo.append(lambda e: fn(e).then_inc(self.sem, 1))
        return (self.sem, self.n)

    def last(self):
        return (self.sem, self.n) if self.n else None


class Slot:

    def __init__(self, t):
        self.t, self.free = t, []

    def done(self, *tokens):
        self.free = list(tokens)


class Rota:
    def __init__(self, tensors):
        self.slots = [Slot(t) for t in tensors]
        self.n = 0

    def take(self):
        s = self.slots[self.n % len(self.slots)]
        self.n += 1
        return s


class Program:
    def __init__(self, nc, A, n_units):
        self.nc, self.A = nc, A
        self.units = []
        self.colspec = columns()
        self.ctx = ExitStack()
        self.nsem = 0
        self.build(n_units)

    def sem(self, name):
        self.nsem += 1
        return self.ctx.enter_context(self.nc.semaphore(name))

    def alloc(self, ctx, name, width, dt=F32):
        return ctx.enter_context(self.nc.sbuf_tensor(name, [128, width], dt))

    def load(self, dst, src, *tokens):
        s = self.sem(f"ld{self.nsem}")
        self.SP.wait(*tokens)
        self.SP.todo.append(lambda e: e.dma_start(dst, src).then_inc(s, 16))
        return (s, 16)

    def col(self, key, j=0):
        c = self.colspec.at[key] + j
        return self.cols[:, c:c + 1]

    def fence(self):
        return [q.last() for q in (self.PE, self.V, self.S, self.G)]

    def fetch(self):
        n = self.n_fetched
        if n >= self.n_units:
            return
        self.n_fetched += 1
        r = n % RAW
        if n >= RAW:
            self.SP.wait(*self.split_tokens[n - RAW])
        src, dst, s = self.A["W"][n], self.raw[:, r * 1024:(r + 1) * 1024], self.s_raw[r]
        self.SP.todo.append(lambda e: e.dma_start(dst, src).then_inc(s, 16))

    def split_next(self):
        n = self.n_split
        self.n_split += 1
        r, k = n % RAW, n % RING
        landed = (self.s_raw[r], 16 * (n // RAW + 1))
        raw = self.raw[:, r * 1024:(r + 1) * 1024]
        hi, lo = self.whi[:, k * 1024:(k + 1) * 1024], self.wlo[:, k * 1024:(k + 1) * 1024]
        free = self.used[n - RING] if n >= RING else None
        t1 = self.S(lambda e: e.copy(hi, raw), landed, free)
        t2 = self.V(lambda e: e.tensor_tensor(lo, raw, hi.bitcast(F32), ALU.subtract), landed, free, t1)
        self.split_tokens[n] = [t1, t2]
        self.fetch()

    def unit(self, name, index, pieces):
        n = len(self.units)
        self.units.append((name, index, pieces))
        while self.n_split < self.n_units and self.n_split <= n + RING - 1:
            self.split_next()
        k = n % RING
        return (self.whi[:, k * 1024:(k + 1) * 1024], self.wlo[:, k * 1024:(k + 1) * 1024],
                self.split_tokens[n], n)

    def mm3(self, out, ah, al, bh, bl, first, last, *tokens, signal=None):
        def three(e):
            e.matmul(out, ah, bh, start=first, stop=False, skip_group_check=True)
            e.matmul(out, ah, bl, start=False, stop=False, skip_group_check=True)
            return e.matmul(out, al, bh, start=False, stop=last, skip_group_check=True)
        return self.PE(three, *tokens, signal=last if signal is None else signal)

    def gemm_t(self, name, index, col, xh, xl, ready, k0=0, nk=8, groups=1, pieces=None, rota=None):
        wh, wl, tok, n = self.unit(name, index, pieces or t_pieces(col, k0, nk, groups))
        out = []
        for g in range(groups):
            bank = (rota or self.pg).take()
            for k in range(nk):
                c = (g * nk + k) * 128
                t = self.mm3(bank.t[:, :], wh[:, c:c + 128], wl[:, c:c + 128], xh(k), xl(k),
                             k == 0, k == nk - 1, tok, bank.free, ready)
            out.append((bank, t))
        self.used[n] = t
        return out

    def gemm_n(self, name, index, k0s, col, xh, xl, ready, rota):
        banks = [rota.take() for _ in range(4)]
        toks = [None] * 4
        nk = len(k0s) * 2
        for ui, k0 in enumerate(k0s):
            wh, wl, tok, n = self.unit(name, index, n_pieces(k0, col))
            last = ui == len(k0s) - 1
            order = [(j, t) for t in range(4) for j in range(2)] if last else [(j, t) for j in range(2) for t in range(4)]
            for q, (j, t) in enumerate(order):
                k = 2 * ui + j
                w = wh[:, j * 512:(j + 1) * 512], wl[:, j * 512:(j + 1) * 512]
                fin = k == nk - 1
                a = self.mm3(banks[t].t[:, :], xh(k, t), xl(k, t), w[0], w[1], k == 0, fin,
                             tok, banks[t].free, ready, signal=fin or q == len(order) - 1)
                if fin:
                    toks[t] = a
                if q == len(order) - 1:
                    self.used[n] = a
        return list(zip(banks, toks))

    def split(self, src, hi, lo, *tokens):
        t1 = self.S(lambda e: e.copy(hi, src), *tokens)
        t2 = self.V(lambda e: e.tensor_tensor(lo, src, hi.bitcast(F32), ALU.subtract), t1, *tokens)
        return [t1, t2]

    def vtt(self, o, a, b, op, *tokens):
        return self.V(lambda e: e.tensor_tensor(o, a, b, op), *tokens)

    def vts(self, o, a, s1, s2, op0, op1, *tokens):
        if op1 is None:
            return self.V(lambda e: e.tensor_scalar(o, a, s1, None, op0), *tokens)
        return self.V(lambda e: e.tensor_scalar(o, a, s1, s2, op0, op1), *tokens)

    def stt(self, o, a, s, b, op0, op1, *tokens):
        return self.V(lambda e: e.scalar_tensor_tensor(out=o, in0=a, scalar=s, in1=b, op0=op0, op1=op1), *tokens)

    def act(self, o, a, f, *tokens, bias=0.0, scale=1.0):
        return self.S(lambda e: e.activation(o, a, f, bias=bias, scale=scale), *tokens)

    def rstd(self, o, var, mul, eps, *tokens):
        w = o.shape[1]
        self.G(lambda e: e.tensor_scalar(o, var, mul, eps, ALU.mult, ALU.add), *tokens)
        return self.G(lambda e: e.tensor_tensor(o, o, self.mhalf[:, 0:w], ALU.pow))

    def transpose4(self, ins, bank, *tokens):
        t = None
        for j, x in enumerate(ins):
            o = bank.t[:, j * 128:(j + 1) * 128]
            t = self.PE(lambda e, o=o, x=x: e.transpose(o, x, self.ident[:, :]), bank.free, *tokens,
                        signal=j == len(ins) - 1)
        return t

    def build(self, n_units):
        nc, A = self.nc, self.A
        self.n_units = n_units
        self.n_fetched = self.n_split = 0
        self.split_tokens, self.used = {}, {}
        ctx = self.ctx
        self.PE = Queue(self.sem("s_pe"), False)
        self.V = Queue(self.sem("s_dve"), True)
        self.S = Queue(self.sem("s_act"), True)
        self.G = Queue(self.sem("s_pool"), True)
        self.SP = Queue(None, False)
        self.s_raw = [self.sem(f"s_raw{i}") for i in range(RAW)]
        self.s_out = self.sem("s_out")
        a = lambda n, w, dt=F32: self.alloc(ctx, n, w, dt)
        self.raw = a("raw", RAW * 1024)
        self.whi, self.wlo = a("whi", RING * 1024, FR), a("wlo", RING * 1024, FR)
        self.xn = a("xn", 4096)
        self.hh, self.hl = a("hh", 4096, FR), a("hl", 4096, FR)
        self.cols = a("cols", len(self.colspec.pieces))
        self.ident = a("ident", 128)
        self.mhalf = a("mhalf", 16)
        self.stat = a("stat", 64)
        self.mod = a("mod", 32)
        self.bc = a("bc", 2048)
        self.tmp = Rota([a(f"tmp{i}", 512) for i in range(2)])
        banks = [ctx.enter_context(nc.psum_tensor(f"bank{i}", [128, 512], F32)) for i in range(8)]
        self.pg, self.ps = Rota(banks[:4]), Rota(banks[4:])

        ca = ExitStack()
        b = lambda n, w, dt=F32, c=ca: self.alloc(c, n, w, dt)
        co = ExitStack()
        self.oh, self.ol = b("oh", 2048, FR, co), b("ol", 2048, FR, co)
        co.close()
        co = ExitStack()
        self.G4 = b("G4", 2048, c=co)
        self.X, self.U, self.Y = b("X", 512, c=co), b("U", 512, c=co), b("Y", 512, c=co)
        self.W4, self.SA = b("W4", 256, c=co), b("SA", 256, c=co)
        co.close()
        self.RT = [b(f"RT{i}", 512) for i in range(8)]
        self.mrg = b("mrg", 4096)
        self.cosr, self.sinr = b("cosr", 512), b("sinr", 512)
        self.cact = b("cact", 16)
        self.w2a2 = b("w2a2", 512)
        self.blk64 = b("blk64", 128)
        self.misc = b("misc", 2)
        c1 = ExitStack()
        self.poolw = b("poolw", 512, c=c1)
        self.invcnt = b("invcnt", 2048, c=c1)
        self.decay = b("decay", 2048, c=c1)
        self.vret = b("vret", 2048, c=c1)
        self.qk = Rota([b(f"qk{i}", 1536, c=c1) for i in range(2)])
        self.pt = b("pt", 2048, c=c1)
        self.onat = b("onat", 512, c=c1)
        self.sgr = b("sgr", 512, c=c1)
        c1.close()
        cx = ExitStack()
        self.xs = b("xs", 4096, c=cx)
        self.crep_h, self.crep_l = b("crep_h", 1024, FR, cx), b("crep_l", 1024, FR, cx)
        self.crep = b("crep", 1024, c=cx)
        self.c2h, self.c2l = b("c2h", 16, FR, cx), b("c2l", 16, FR, cx)
        cx.close()
        c2 = ExitStack()
        self.AR = b("AR", 4096, c=c2)
        self.KH, self.BH = b("KH", 2048, c=c2), b("BH", 2048, c=c2)
        self.VN, self.VB = b("VN", 2048, c=c2), b("VB", 2048, c=c2)
        self.gmask, self.m1 = b("gmask", 512, c=c2), b("m1", 128, c=c2)
        self.lmask = b("lmask", 1024, U32, c2)
        self.em = b("em", 64, c=c2)
        self.st = b("st", 256, c=c2)
        c3 = ExitStack()
        self.PP = b("PP", 513, c=c3)
        self.reset = b("reset", 512, c=c3)
        self.wa = b("wa", 512, c=c3)
        c3.close()
        c4 = ExitStack()
        self.KN, self.BN = b("KN", 256, c=c4), b("BN", 256, c=c4)
        self.SP4 = b("SP4", 256, c=c4)
        self.YN, self.YQ = b("YN", 256, c=c4), b("YQ", 256, c=c4)
        self.hs = b("hs", 16, c=c4)
        c4.close()
        c2.close()
        c5 = ExitStack()
        self.mh, self.ml = b("mh", 4096, FR, c5), b("ml", 4096, FR, c5)
        c5.close()
        ca.close()

        cb = ExitStack()
        d = lambda n, w, dt=F32, c=cb: self.alloc(c, n, w, dt)
        cf = ExitStack()
        self.fh, self.fl = d("fh", NFF * 512, FR, cf), d("fl", NFF * 512, FR, cf)
        cf.close()
        cm = ExitStack()
        self.xh8, self.xl8 = d("xh8", 4096, FR, cm), d("xl8", 4096, FR, cm)
        self.qT = d("qT", 2048, c=cm)
        self.kT, self.kS = d("kT", 512, c=cm), d("kS", 512, c=cm)
        self.ks_layer, self.den_free, self.ao_free = None, [], []
        self.v2 = d("v2", 512, c=cm)
        self.rcos, self.rsin, self.amask = d("rcos", 512, c=cm), d("rsin", 512, c=cm), d("amask", 384, c=cm)
        self.mean256 = d("mean256", 128, c=cm)
        self.sink = d("sink", 8, c=cm)
        self.ccp = d("ccp", 1088, c=cm)
        self.scp = d("scp", 1088, c=cm)
        self.acc = d("acc", 1024, c=cm)
        self.pr = Rota([d(f"pr{i}", 384, c=cm) for i in range(2)])
        self.prT = Rota([d(f"prT{i}", 384, c=cm) for i in range(2)])
        self.ao = d("ao", 512, c=cm)
        self.sm = Rota([d(f"sm{i}", 8, c=cm) for i in range(2)])
        self.den = d("den", 16, c=cm)
        self.t3 = [d(f"tz{i}", 512, c=cm) for i in range(3)]
        cm.close()
        cb.close()

        self.k_cols = self.load(self.cols[:, :], A["cols"])
        for _ in range(RAW):
            self.fetch()
        self.k_id = self.load(self.ident[:, :], A["ident"])
        self.k_x = [self.load(self.xn[:, t * 1024:(t + 1) * 1024], A["x"][0, t * 128:(t + 1) * 128, :]) for t in range(4)]
        self.k_half = self.G(lambda e: e.memset(self.mhalf[:, :], -0.5))
        self.prepare_a()
        self.x_ready = [[k] for k in self.k_x]
        for l in range(DEPTH):
            self.layer_a(l)
        self.final_norm()
        for l in range(DEPTH):
            self.layer_b(l)
        self.finish()

    def run(self):
        assert len(self.units) == self.n_units, len(self.units)
        with self.ctx:
            block = self.ctx.enter_context(self.nc.Block())
            for reg, q in ((block.sync, self.SP), (block.gpsimd, self.G), (block.scalar, self.S),
                           (block.vector, self.V), (block.tensor, self.PE)):
                def body(e, q=q):
                    for f in q.todo:
                        f(e)
                reg(body)

    def x_tile(self, t):
        return self.xn[:, t * 1024:(t + 1) * 1024]

    def to_hT(self, blocks, ready, scale, bias):
        f = self.h_free
        toks = []
        for d in range(8):
            bank = self.ps.take()
            t = self.transpose4([blocks(j, d) for j in range(4)], bank, self.k_id, ready)
            tm = self.tmp.take()
            if bias is None:
                t1 = self.vts(tm.t[:, :], bank.t[:, :], scale(d), None, ALU.mult, None, t, tm.free)
            else:
                t1 = self.act(tm.t[:, :], bank.t[:, :], ACT.Identity, t, tm.free, bias=bias(d), scale=scale(d))
            bank.done(t1)
            k = self.split(tm.t[:, :], self.hh[:, d * 512:(d + 1) * 512], self.hl[:, d * 512:(d + 1) * 512], t1, f)
            tm.done(*k)
            toks += k
        self.h_ready = toks
        return toks

    def h_rhs(self, k):
        return self.hh[:, k * 512:(k + 1) * 512]

    def l_rhs(self, k):
        return self.hl[:, k * 512:(k + 1) * 512]

    def h_lhs(self, k, t):
        return self.hh[:, k * 512 + t * 128:k * 512 + (t + 1) * 128]

    def l_lhs(self, k, t):
        return self.hl[:, k * 512 + t * 128:k * 512 + (t + 1) * 128]

    def prepare_a(self):
        A = self.A
        self.h_free = []
        self.k_misc = [self.load(self.misc[:, :], A["misc"]), self.load(self.blk64[:, :], A["blk64"])]
        k_pos = self.load(self.xs[:, 0:512].bitcast(I32), A["positions"][0].partition_broadcast(128))
        x = [self.xs[:, i * 512:(i + 1) * 512] for i in range(6)]
        self.V(lambda e: e.tensor_copy(x[1], x[0].bitcast(I32)), k_pos)
        self.vts(x[1], x[1], self.misc[:, 0:1], None, ALU.mult, None, *self.k_misc)
        big = 12582912.0
        c1 = 6.28125
        c2 = float(np.float32(2 * np.pi - c1))
        c3 = float(2 * np.pi - c1 - float(np.float32(c2)))
        pi = 3.1415925
        for off, out in ((0.25, self.cosr), (0.0, self.sinr)):
            self.vts(x[2], x[1], float(1 / (2 * np.pi)), off, ALU.mult, ALU.add)
            self.vts(x[2], x[2], big, None, ALU.add, None)
            self.vts(x[2], x[2], big, None, ALU.subtract, None)
            self.stt(x[3], x[2], -c1, x[1], ALU.mult, ALU.add)
            self.stt(x[3], x[2], -c2, x[3], ALU.mult, ALU.add)
            self.stt(x[3], x[2], -c3, x[3], ALU.mult, ALU.add)
            self.vts(x[3], x[3], float(off * 2 * np.pi), pi, ALU.add, ALU.min)
            t = self.vts(x[3], x[3], -pi, None, ALU.max, None)
            t = self.act(out[:, :], x[3], ACT.Sin, t)
            self.V.wait(t)
        self.k_rot = self.vts(self.sinr[:, :], self.sinr[:, :], self.misc[:, 1:2], None, ALU.mult, None, t)
        cc = self.colspec.at[("c",)]
        t = self.act(self.cact[:, 8:16], self.cols[:, cc:cc + 8], ACT.Sigmoid, self.k_cols)
        self.k_cact = self.vtt(self.cact[:, 0:8], self.cols[:, cc:cc + 8], self.cact[:, 8:16], ALU.mult, t, self.k_cols)

    def modulation(self, l):
        A = self.A
        f = self.fence()
        c = self.cact[:, 0:8]
        t = self.V(lambda e: e.tensor_copy(self.crep[:, :].rearrange("p (k n) -> p k n", k=8),
                                           c.unsqueeze(2).broadcast_to([128, 8, 128])), f, self.k_cact)
        k1 = self.split(self.crep[:, :], self.crep_h[:, :], self.crep_l[:, :], t)
        bank = self.ps.take()
        for m in range(16):
            wh, wl, tok, n = self.unit("w_ada", (l,), t_pieces(128 * m))
            for k in range(8):
                t = self.mm3(bank.t[:, 2 * m:2 * m + 2], wh[:, k * 128:(k + 1) * 128], wl[:, k * 128:(k + 1) * 128],
                             self.crep_h[:, k * 128:k * 128 + 2], self.crep_l[:, k * 128:k * 128 + 2],
                             k == 0, k == 7, tok, bank.free, k1)
            self.used[n] = t
        ba = self.colspec.at[("b_ada", l)]
        ng = self.colspec.at[("norm_g", l)]
        t = self.vtt(self.mod[:, 0:16], bank.t[:, 0:32].rearrange("p (m two) -> p m two", two=2)[:, :, 0],
                     self.cols[:, ba:ba + 16], ALU.add, t, self.k_cols, f)
        bank.done(t)
        self.k_mod = self.stt(self.mod[:, 16:24], self.mod[:, 8:16], 1.0, self.cols[:, ng:ng + 8], ALU.add, ALU.mult)
        kb = self.load(self.bc[:, 0:1024], A["b_ada"][l, 2048:3072].partition_broadcast(128), f)
        self.k_gate = []
        for half in range(2):
            bank = self.ps.take()
            for ui in range(4):
                wh, wl, tok, n = self.unit("w_ada", (l,), n_pieces(256 * ui, 2048 + 512 * half))
                for j in range(2):
                    k = 2 * ui + j
                    t = self.mm3(bank.t[:, :], self.crep_h[:, k * 128:(k + 1) * 128], self.crep_l[:, k * 128:(k + 1) * 128],
                                 wh[:, j * 512:(j + 1) * 512], wl[:, j * 512:(j + 1) * 512],
                                 k == 0, k == 7, tok, bank.free, k1, signal=j == 1)
                self.used[n] = t
            g = self.bc[:, half * 512:(half + 1) * 512]
            t = self.vtt(g, bank.t[:, :], g, ALU.add, t, kb)
            bank.done(t)
            self.k_gate.append(t)
        self.k_crep = t

    def layer_a(self, l):
        A = self.A
        self.modulation(l)
        f = self.fence()
        tt = []
        for t in range(4):
            xt, xs = self.x_tile(t), self.xs[:, t * 1024:(t + 1) * 1024]
            tt.append(self.S(lambda e, xt=xt, xs=xs, t=t: e.activation(xs, xt, ACT.Square, accum_out=self.stat[:, t:t + 1]),
                             self.x_ready[t], f))
        r = self.rstd(self.stat[:, 4:8], self.stat[:, 0:4], 1.0 / D, 1e-6, tt[-1], f)
        k = []
        for t in range(4):
            k.append(self.vts(self.xs[:, t * 1024:(t + 1) * 1024], self.x_tile(t), self.stat[:, 4 + t:5 + t], None,
                              ALU.mult, None, r, tt[t]))
        self.h_free = f
        self.to_hT(lambda t, d: self.xs[:, t * 1024 + d * 128:t * 1024 + (d + 1) * 128], k + [self.k_mod],
                   lambda d: self.mod[:, 16 + d:17 + d], lambda d: self.mod[:, d:d + 1])
        self.proj = lambda col, **kw: self.gemm_t("w_in", (l,), col, self.h_rhs, self.l_rhs, self.h_ready, **kw)
        f = self.fence()
        self.k_pw = self.load(self.poolw[:, :].rearrange("p (g d) -> p g d", g=4),
                              A["pool_w"][l].rearrange("g c d -> c g d"), f)
        self.k_ic = self.load(self.invcnt[:, :], A["invcnt"], f)
        self.k_dc = self.load(self.decay[:, :], A["decay"], f)
        self.k_w2 = [self.load(self.w2a2[0:64, :], A["rwkv_w2"][l], f), self.load(self.w2a2[64:128, :], A["rwkv_a2"][l], f)]
        k = self.pool(l, f)
        self.branch(l, 0, k)
        k = self.retention(l, self.fence())
        self.branch(l, 1, k)
        k = self.rwkv(l)
        self.branch(l, 2, k)
        self.w_out(l)

    def silu(self, out, bank, tok, *free):
        t1 = self.act(out, bank.t[:, :], ACT.Sigmoid, tok, *free)
        t2 = self.vtt(out, bank.t[:, :], out, ALU.mult, t1, tok)
        bank.done(t1, t2)
        return t2

    def pool(self, l, f):
        ready = []
        o_free = f
        for g, w in enumerate(POOLW):
            (bank, t), = self.proj(g * 128)
            s = self.pt[:, 0:512], self.pt[:, 512:1024]
            u = self.pt[:, 1024:1536]
            t = self.S(lambda e, u=u, b=bank: e.copy(u, b.t[:, :]), t, f)
            bank.done(t)
            src, n = u, 1
            i = 0
            while n < w:
                dst = s[i]
                self.vtt(dst[:, n:512], src[:, n:512], src[:, 0:512 - n], ALU.add, t, f)
                self.V(lambda e, dst=dst, src=src, n=n: e.tensor_copy(dst[:, 0:n], src[:, 0:n]))
                src, n, i = dst, 2 * n, 1 - i
            dd = s[i]
            self.vtt(dd, src, self.invcnt[:, g * 512:(g + 1) * 512], ALU.mult, self.k_ic)
            t = self.vtt(dd, dd, u, ALU.subtract)
            pb = self.ps.take()
            tp = self.PE(lambda e, pb=pb, dd=dd, g=g: e.matmul(pb.t[:, :], self.poolw[:, g * 128:(g + 1) * 128], dd,
                                                              start=True, stop=True), t, self.k_pw, pb.free)
            self.V.wait(tp)
            (bank, t), = self.proj(512 + g * 128)
            sg = self.pt[:, 1536:2048]
            self.silu(sg, bank, t, f)
            t = self.stt(sg, pb.t[:, :], self.col(("pool_scale", l), g), sg, ALU.mult, ALU.mult, tp, self.k_cols)
            pb.done(t)
            ready += self.split(sg, self.oh[:, g * 512:(g + 1) * 512], self.ol[:, g * 512:(g + 1) * 512], t, o_free)
            self.S.wait(ready[-1])
            f = []
        return ready

    def branch(self, l, n, ready):
        f = self.fence()
        first = True
        self.k_mrg = []
        for m2 in range(4):
            gates = [self.proj(5248 + n * 1024 + (2 * m2 + i) * 128)[0] for i in range(2)]
            sg = []
            for bank, t in gates:
                tm = self.tmp.take()
                t = self.act(tm.t[:, :], bank.t[:, :], ACT.Sigmoid, t, tm.free)
                bank.done(t)
                sg.append((tm, t))
            ys = self.gemm_t("w_branch", (l, n), 256 * m2, lambda k: self.oh[:, k * 512:(k + 1) * 512],
                             lambda k: self.ol[:, k * 512:(k + 1) * 512], ready, nk=4, groups=2)
            for i, (bank, t) in enumerate(ys):
                m = 2 * m2 + i
                tm, t1 = sg[i]
                acc = self.mrg[:, m * 512:(m + 1) * 512]
                if n == 0:
                    t = self.vtt(acc, tm.t[:, :], bank.t[:, :], ALU.mult, t, t1, f)
                    bank.done(t)
                    tm.done(t)
                else:
                    t = self.vtt(tm.t[:, :], tm.t[:, :], bank.t[:, :], ALU.mult, t, t1)
                    bank.done(t)
                    t = self.vtt(acc, acc, tm.t[:, :], ALU.add)
                    tm.done(t)
                if n == 2:
                    self.k_mrg += self.split(acc, self.mh[:, m * 512:(m + 1) * 512], self.ml[:, m * 512:(m + 1) * 512], t, f)

    def rope(self, src, dst, sw, cos, sin, w, *tokens):
        t = None
        for p in range(0, 128, 2 * w):
            for a, b in ((p, p + w), (p + w, p)):
                t = self.G(lambda e, a=a, b=b: e.tensor_copy(sw[a:a + w, :], src[b:b + w, :]), *tokens)
        self.vtt(dst, src, cos, ALU.mult, t, *tokens)
        self.vtt(sw, sw, sin, ALU.mult, t)
        return self.vtt(dst, dst, sw, ALU.add)

    def retention(self, l, f):
        vb = self.gemm_n("w_in", (l,), [0, 256, 512, 768], 2048, self.h_lhs, self.l_lhs, self.h_ready, self.ps)
        kv = []
        for t, (bank, tok) in enumerate(vb):
            kv.append(self.S(lambda e, t=t, bank=bank: e.copy(self.vret[:, t * 512:(t + 1) * 512], bank.t[:, :]), tok, f))
            bank.done(kv[-1])
        ready = []
        pfree, nfree = f, f
        for s in self.qk.slots:
            s.done(*f)
        for h in range(4):
            rot = []
            for base in (1024, 1536):
                (bank, t), = self.proj(base + h * 128)
                s = self.qk.take()
                src, dst, sw = s.t[:, 0:512], s.t[:, 512:1024], s.t[:, 1024:1536]
                t = self.S(lambda e, src=src, bank=bank: e.copy(src, bank.t[:, :]), t, s.free)
                bank.done(t)
                rot.append((s, dst, self.rope(src, dst, sw, self.cosr[:, :], self.sinr[:, :], 64, t, s.free, self.k_rot)))
            (bank, tg), = self.proj(2560 + h * 128)
            (sq, q, tq), (sk, k, tk) = rot
            tp = []
            for j in range(4):
                pb = self.ps.take()
                n = 512 - 128 * j
                t = self.PE(lambda e, pb=pb, j=j, n=n, q=q, k=k: e.matmul(pb.t[:, 0:n], k[:, j * 128:(j + 1) * 128], q[:, j * 128:512],
                                                                          start=True, stop=True), pb.free, tq, tk)
                t = self.vtt(self.pt[:, j * 512:j * 512 + n], pb.t[:, 0:n], self.decay[:, h * 512:h * 512 + n], ALU.mult,
                             t, pfree, self.k_dc)
                pb.done(t)
                tp.append(t)
            sq.done(t)
            sk.done(t)
            ob = self.ps.take()
            for i in range(4):
                for j in range(i + 1):
                    t = self.PE(lambda e, i=i, j=j, ob=ob, h=h: e.matmul(
                        ob.t[:, i * 128:(i + 1) * 128], self.pt[:, j * 512 + (i - j) * 128:j * 512 + (i - j + 1) * 128],
                        self.vret[:, j * 512 + h * 128:j * 512 + (h + 1) * 128], start=j == 0, stop=j == i, skip_group_check=True),
                        ob.free, tp[j], kv[j], signal=i == j)
            pfree = [t]
            st = self.stat
            for i in range(4):
                self.V(lambda e, i=i, ob=ob: e.bn_stats(st[:, 16 + 6 * i:22 + 6 * i], ob.t[:, i * 128:(i + 1) * 128]), t)
                ts = self.V(lambda e, i=i: e.bn_aggr(st[:, 2 * i:2 * i + 2], st[:, 16 + 6 * i:22 + 6 * i]))
            r = self.rstd(st[:, 8:12], st[:, 0:8].rearrange("p (i two) -> p i two", two=2)[:, :, 1], 1.0, 1e-5, ts)
            for i in range(4):
                tn = self.vts(self.onat[:, i * 128:(i + 1) * 128], ob.t[:, i * 128:(i + 1) * 128], st[:, 2 * i:2 * i + 1],
                              st[:, 8 + i:9 + i], ALU.subtract, ALU.mult, r, nfree)
            ob.done(tn)
            tb = self.ps.take()
            t = self.transpose4([self.onat[:, i * 128:(i + 1) * 128] for i in range(4)], tb, tn, self.k_id)
            nfree = [t]
            self.silu(self.sgr[:, :], bank, tg, f)
            t = self.stt(self.sgr[:, :], tb.t[:, :], self.col(("ret_g", l), h), self.sgr[:, :], ALU.mult, ALU.mult, t)
            tb.done(t)
            ready += self.split(self.sgr[:, :], self.oh[:, h * 512:(h + 1) * 512], self.ol[:, h * 512:(h + 1) * 512], t, f)
            self.S.wait(ready[-1])
            self.V.wait(ready[-2])
        return ready

    def shifted(self, bank, tok, mu, out, f):
        t = self.S(lambda e, bank=bank: e.copy(self.PP[:, 1:513], bank.t[:, :]), tok, self.pp_free)
        bank.done(t)
        self.vtt(self.RT[7][:, :], self.PP[:, 0:512], self.PP[:, 1:513], ALU.subtract, t, f)
        t = self.stt(out, self.RT[7][:, :], mu, self.PP[:, 1:513], ALU.mult, ALU.add)
        self.pp_free = [t]
        return t

    def rwkv(self, l):
        A = self.A
        f = self.fence()
        k_rs = self.load(self.reset[:, :], A["reset"], f)
        k_gm = [self.load(self.gmask[:, :], A["gmask"], f), self.load(self.m1[:, :], A["m1"], f),
                self.load(self.lmask[:, :], A["lmask"], f)]
        self.pp_free = [self.V(lambda e: e.memset(self.PP[:, 0:1], 0.0), f)]
        pieces = tuple(x for k in range(8) for x in ((128 * k, 3584, 64), (128 * k, 4672, 64)))
        (bank, t), = self.proj(0, pieces=pieces)
        t = self.shifted(bank, t, self.col(("mu_wa", l)), self.wa[:, :], f)
        k_wa = self.act(self.wa[0:64, :], self.wa[0:64, :], ACT.Tanh, t)
        RT = [x[:, :] for x in self.RT]
        for p in range(4):
            mu = lambda n: self.col((n, l), p)
            pb = self.ps.take()
            t = self.PE(lambda e, pb=pb, p=p: e.matmul(pb.t[:, :], self.w2a2[0:64, p * 128:(p + 1) * 128], self.wa[0:64, :],
                                                       start=True, stop=True), pb.free, k_wa, self.k_w2)
            sg, cum = RT[0], RT[1]
            t = self.act(sg, pb.t[:, :], ACT.Sigmoid, t, f, bias=mu("w0"))
            pb.done(t)
            self.V(lambda e: e.tensor_tensor_scan(cum, self.reset[:, :], sg, 0.0, ALU.mult, ALU.add), t, k_rs)
            c4 = cum.rearrange("p (c n) -> p c n", c=4)
            e4 = self.em[:, 16 * p:16 * p + 16]
            self.V(lambda e, e4=e4: e.tensor_copy(e4[:, 12:16], c4[:, :, 63]))
            tm = self.vtt(e4[:, 8:12], c4[:, :, 127], e4[:, 12:16], ALU.subtract)
            tm = self.V(lambda e, e4=e4: e.tensor_copy(e4[:, 4:8], c4[:, :, 127]))
            self.vtt(c4, c4, e4[:, 12:16].unsqueeze(2).broadcast_to([128, 4, 128]), ALU.subtract)
            td = self.vtt(sg, cum, sg, ALU.subtract)
            te = self.act(e4[:, 0:4], e4[:, 12:16], ACT.Exp, td, scale=-KAPPA)
            te = self.act(e4[:, 4:12], e4[:, 4:12], ACT.Exp, scale=-KAPPA)
            E1, E2, E3 = RT[2], RT[1], RT[0]
            self.act(E1, cum, ACT.Exp, scale=-KAPPA)
            self.act(E3, sg, ACT.Exp, scale=-KAPPA)
            te = self.act(E2, cum, ACT.Exp, scale=KAPPA)
            (bank, t), = self.proj(3072 + p * 128)
            r = RT[3]
            self.shifted(bank, t, mu("mu_r"), r, f)
            AR = self.AR[:, p * 1024:(p + 1) * 1024]
            self.vtt(AR[:, 512:1024], r, E1, ALU.mult, te)
            (bank, t), = self.proj(3648 + p * 128)
            k = RT[4]
            tk = self.shifted(bank, t, mu("mu_k"), k, f)
            pb = self.ps.take()
            t = self.PE(lambda e, pb=pb, p=p: e.matmul(pb.t[:, :], self.w2a2[64:128, p * 128:(p + 1) * 128], self.wa[64:128, :],
                                                       start=True, stop=True), pb.free, k_wa, self.k_w2)
            a = RT[5]
            ta = self.act(a, pb.t[:, :], ACT.Sigmoid, t, bias=mu("a0"))
            pb.done(ta)
            q = RT[6]
            t = self.act(q, k, ACT.Square, tk, scale=mu("k_k"))
            pb = self.ps.take()
            t = self.PE(lambda e, pb=pb: e.matmul(pb.t[:, :], self.blk64[:, :], q, start=True, stop=True), pb.free, t, *self.k_misc)
            t = self.vts(q, pb.t[:, :], 1e-24, None, ALU.max, None, t)
            pb.done(t)
            t = self.act(q, q, ACT.Sqrt, t)
            self.V(lambda e: e.reciprocal(q, q), t)
            kk = q
            self.stt(kk, k, mu("k_k"), q, ALU.mult, ALU.mult)
            self.stt(AR[:, 0:512], kk, -1.0, E3, ALU.mult, ALU.mult)
            self.vtt(kk, kk, a, ALU.mult, ta)
            self.vtt(self.BH[:, p * 512:(p + 1) * 512], kk, E2, ALU.mult)
            self.vts(a, a, 1.0, mu("k_a"), ALU.subtract, ALU.mult)
            self.stt(k, a, 1.0, k, ALU.add, ALU.mult)
            self.vtt(self.KH[:, p * 512:(p + 1) * 512], k, E2, ALU.mult)
            t = self.stt(r, r, mu("r_k"), k, ALU.mult, ALU.mult)
            pb = self.ps.take()
            tb = self.PE(lambda e, pb=pb: e.matmul(pb.t[:, :], self.blk64[:, :], r, start=True, stop=True), pb.free, t)
            (bank, t), = self.proj(4160 + p * 128)
            v = RT[5]
            tv = self.shifted(bank, t, mu("mu_v"), v, f)
            b2 = self.ps.take()
            t2 = self.transpose4([v[:, c * 128:(c + 1) * 128] for c in range(4)], b2, tv, self.k_id)
            vn = self.VN[:, :].rearrange("p (c q n) -> p c q n", c=4, q=4)[:, :, p, :]
            t3 = self.S(lambda e, b2=b2, vn=vn: e.copy(vn, b2.t[:, :].rearrange("p (c n) -> p c n", c=4)), t2)
            b2.done(t3)
            t = self.vtt(self.VB[:, p * 512:(p + 1) * 512], pb.t[:, :], v, ALU.mult, tb)
            pb.done(t)
            self.S.wait(t)
            self.V.wait(t3, te, t2)
        self.k_gm = k_gm
        self.chunks(l)
        ready = []
        f = self.fence()
        for p in range(4):
            (bank, t), = self.proj(4736 + p * 128)
            tm = self.tmp.take()
            y = self.KH[:, p * 512:(p + 1) * 512]
            self.silu(tm.t[:, :], bank, t, tm.free)
            self.vtt(y, y, self.VB[:, p * 512:(p + 1) * 512], ALU.add, f)
            t = self.vtt(y, y, tm.t[:, :], ALU.mult)
            tm.done(t)
            ready += self.split(y, self.oh[:, p * 512:(p + 1) * 512], self.ol[:, p * 512:(p + 1) * 512], t, f)
        return ready

    def chunks(self, l):
        f = self.fence()
        for c in range(4):
            for g in range(2):
                self.chunk(l, c, g, f)
                f = []

    def chunk(self, l, c, g, f):
        cs = slice(c * 128, (c + 1) * 128)
        heads = [(4 * g + i, (4 * g + i) // 2, 64 * (i % 2)) for i in range(4)]
        G4, X, U, Y = self.G4, self.X, self.U, self.Y
        v4 = lambda x: x[:, :].rearrange("p (h n) -> p h n", h=4)
        pe_last = [self.PE.last()]
        for i, (h, p, q) in enumerate(heads):
            bank = self.ps.take()
            ar = self.AR[q:q + 64, p * 1024:(p + 1) * 1024].rearrange("p (two n) -> p two n", two=2)[:, :, cs]
            for j, KB in enumerate((self.BH, self.KH)):
                o = bank.t[:, 256 * j:256 * j + 256].rearrange("p (two n) -> p two n", two=2)
                t = self.PE(lambda e, o=o, KB=KB, ar=ar, p=p, q=q: e.matmul(
                    o, KB[q:q + 64, p * 512 + c * 128:p * 512 + (c + 1) * 128], ar, start=True, stop=True, skip_group_check=True),
                    bank.free, f, signal=j == 1)
            t = self.vtt(G4[:, i * 512:(i + 1) * 512], bank.t[:, :], self.gmask[:, :], ALU.mult, t, f, pe_last, self.k_gm)
            bank.done(t)
        kn = []
        for KB, KN in ((self.BH, self.BN), (self.KH, self.KN)):
            bank = self.ps.take()
            tt = self.transpose4([KB[:, p * 512 + c * 128:p * 512 + (c + 1) * 128] for p in (2 * g, 2 * g + 1)], bank, self.k_id)
            kn.append(self.S(lambda e, KN=KN, bank=bank: e.copy(KN[:, :], bank.t[:, 0:256]), tt, pe_last, f))
            bank.done(kn[-1])
        ga = G4[:, :].rearrange("p (h n) -> p h n", h=4)[:, :, 0:128]
        self.vtt(v4(U), ga, self.m1[:, :].unsqueeze(1).broadcast_to([128, 4, 128]), ALU.mult)
        tu = self.vtt(v4(U), v4(U), self.ident[:, :].unsqueeze(1).broadcast_to([128, 4, 128]), ALU.add, self.k_id)
        bank = self.ps.take()
        t = self.transpose4([U[:, i * 128:(i + 1) * 128] for i in range(4)], bank, tu)
        tx = self.S(lambda e, bank=bank: e.copy(X[:, :], bank.t[:, :]), t, pe_last, f)
        bank.done(tx)

        def four(bank, lhs, rhs, *tokens):
            for i in range(4):
                t = self.PE(lambda e, i=i: e.matmul(bank.t[:, i * 128:(i + 1) * 128], lhs(i), rhs(i), start=True, stop=True,
                                                    skip_group_check=True), bank.free, *tokens, signal=i == 3)
            return t

        blk = lambda x: (lambda i: x[:, i * 128:(i + 1) * 128])
        for lv, n in enumerate((2, 4, 8, 16, 32, 64)):
            yb = self.ps.take()
            t = four(yb, lambda i: G4[:, i * 512:i * 512 + 128], blk(X), tx, tu)
            ty = self.S(lambda e, yb=yb: e.copy(Y[:, :], yb.t[:, :]), t)
            yb.done(ty)
            zb = None
            if n < 64:
                zb = self.ps.take()
                tz = four(zb, blk(U), blk(Y), ty)
            wb = self.ps.take()
            tw = four(wb, blk(Y), blk(U), ty)
            for b_, M, t, off in ((zb, X, None if zb is None else tz, 0), (wb, U, tw, 128)):
                if b_ is None:
                    continue
                if n < 32:
                    m = self.lmask[:, lv * 256 + off:lv * 256 + off + 128].unsqueeze(1).broadcast_to([128, 4, 128])
                    tc = self.V(lambda e, M=M, m=m, b_=b_: e.copy_predicated(v4(M), m, v4(b_.t)), t)
                else:
                    for s in range(0, 128, 2 * n):
                        a_, b2 = (s + n, s) if M is X else (s, s + n)
                        tc = self.V(lambda e, M=M, b_=b_, a_=a_, b2=b2, n=n: e.tensor_copy(
                            v4(M)[a_:a_ + n, :, b2:b2 + n], v4(b_.t)[a_:a_ + n, :, b2:b2 + n]), t)
                b_.done(tc)
                if M is X:
                    tx = tc
                else:
                    tu = tc
        em = self.em[:, 32 * g:32 * g + 32].rearrange("p (t j c) -> p t j c", t=2, j=4)
        bc = lambda j: em[:, :, j, c].unsqueeze(2).broadcast_to([128, 2, 64])
        st = self.st[:, g * 128:(g + 1) * 128].rearrange("p (t v) -> p t v", t=2)
        spt = self.SP4[:, :].rearrange("p (t j v) -> p t j v", t=2, j=2)
        ts = None
        if c == 0:
            self.V(lambda e: e.memset(self.SP4[:, :], 0.0), pe_last, f)
        else:
            for j in range(2):
                q = slice(64 * j, 64 * j + 64)
                ts = self.vtt(spt[q, :, j, :], st[q, :, :], bc(0)[q, :, :], ALU.mult, pe_last)
        wb = self.ps.take()
        vn = lambda h: self.VN[:, c * 512 + h * 64:c * 512 + (h + 1) * 64]

        def from_state(bank, j):
            for t in range(2):
                a = self.AR[:, (2 * g + t) * 1024 + j * 512 + c * 128:(2 * g + t) * 1024 + j * 512 + (c + 1) * 128]
                o = bank.t[:, t * 128:(t + 1) * 128]
                self.PE(lambda e, o=o, a=a, t=t: e.matmul(o, a, self.SP4[:, t * 128:(t + 1) * 128], start=t == 0, stop=False,
                                                          skip_group_check=True), ts, bank.free, signal=False)

        if c:
            from_state(wb, 0)
        for i, (h, p, q) in enumerate(heads):
            o = wb.t[:, i * 64:(i + 1) * 64]
            t = self.PE(lambda e, o=o, h=h, i=i: e.matmul(o, G4[:, i * 512 + 256:i * 512 + 384], vn(h), start=c == 0, stop=True,
                                                          skip_group_check=True), wb.free, signal=i == 3)
        t = self.S(lambda e, wb=wb: e.copy(self.W4[:, :], wb.t[:, 0:256]), t)
        wb.done(t)
        sb = self.ps.take()
        for i, (h, p, q) in enumerate(heads):
            t2 = self.PE(lambda e, i=i, sb=sb: e.matmul(sb.t[:, i * 64:(i + 1) * 64], U[:, i * 128:(i + 1) * 128],
                                                        self.W4[:, i * 64:(i + 1) * 64], start=True, stop=True, skip_group_check=True),
                         t, tu, sb.free, signal=i == 3)
        tsa = self.S(lambda e, sb=sb: e.copy(self.SA[:, :], sb.t[:, 0:256]), t2)
        sb.done(tsa)
        yb = self.ps.take()
        if c:
            from_state(yb, 1)
        for i, (h, p, q) in enumerate(heads):
            o = yb.t[:, i * 64:(i + 1) * 64]
            self.PE(lambda e, o=o, i=i: e.matmul(o, G4[:, i * 512 + 128:i * 512 + 256], self.SA[:, i * 64:(i + 1) * 64],
                                                 start=c == 0, stop=False, skip_group_check=True), tsa, yb.free, signal=False)
            t = self.PE(lambda e, o=o, h=h, i=i: e.matmul(o, G4[:, i * 512 + 384:i * 512 + 512], vn(h), start=False, stop=True,
                                                          skip_group_check=True), signal=i == 3)
        ty = t
        if c < 3:
            sb = self.ps.take()
            for i, (h, p, q) in enumerate(heads):
                o = sb.t[q:q + 64, (p - 2 * g) * 64:(p - 2 * g) * 64 + 64]
                for j, (KN, R) in enumerate(((self.BN, self.SA[:, i * 64:(i + 1) * 64]), (self.KN, vn(h)))):
                    t = self.PE(lambda e, o=o, KN=KN, R=R, i=i, j=j: e.matmul(o, KN[:, i * 64:(i + 1) * 64], R, start=j == 0, stop=j == 1,
                                                                              skip_group_check=True), kn, sb.free, signal=i == 3 and j == 1)
            sv = sb.t[:, 0:128].rearrange("p (t v) -> p t v", t=2)
            if c:
                sq = self.YQ[:, 0:128].rearrange("p (t v) -> p t v", t=2)
                self.vtt(st, st, bc(1), ALU.mult)
                t = self.vtt(sq, sv, bc(2), ALU.mult, t)
                self.vtt(st, st, sq, ALU.add)
            else:
                t = self.vtt(st, sv, bc(2), ALU.mult, t, f)
            sb.done(t)
        y4 = yb.t[:, 0:256].rearrange("p (h n) -> p h n", h=4)
        n4, q4 = (x[:, :].rearrange("p (h n) -> p h n", h=4) for x in (self.YN, self.YQ))
        hs = self.hs
        self.V(lambda e: e.tensor_reduce(hs[:, 0:4], y4, AX.X, ALU.add), ty)
        self.vts(hs[:, 0:4], hs[:, 0:4], 1.0 / 64, None, ALU.mult, None)
        t = self.vtt(n4, y4, hs[:, 0:4].unsqueeze(2).broadcast_to([128, 4, 64]), ALU.subtract, pe_last)
        yb.done(t)
        self.vtt(q4, n4, n4, ALU.mult)
        t = self.V(lambda e: e.tensor_reduce(hs[:, 4:8], q4, AX.X, ALU.add))
        r = self.rstd(hs[:, 8:12], hs[:, 4:8], 1.0 / 64, 64e-5, t)
        t = self.vtt(n4, n4, hs[:, 8:12].unsqueeze(2).broadcast_to([128, 4, 64]), ALU.mult, r)
        bank = self.ps.take()
        t = self.transpose4([self.YN[:, 0:128], self.YN[:, 128:256]], bank, t)
        for j in range(2):
            p = 2 * g + j
            tt = self.act(self.KH[:, p * 512 + c * 128:p * 512 + (c + 1) * 128], bank.t[:, j * 128:(j + 1) * 128], ACT.Identity, t,
                          bias=self.col(("ln_b", l), p), scale=self.col(("ln_w", l), p))
        bank.done(tt)

    def w_out(self, l):
        self.x_ready = [[] for _ in range(4)]
        for half in range(2):
            rota = (self.pg, self.ps)[half]
            out = self.gemm_n("w_out", (l,), [0, 256, 512, 768], 512 * half,
                              lambda k, t: self.mh[:, k * 512 + t * 128:k * 512 + (t + 1) * 128],
                              lambda k, t: self.ml[:, k * 512 + t * 128:k * 512 + (t + 1) * 128], self.k_mrg, rota)
            for t, (bank, tok) in enumerate(out):
                tm = self.tmp.take()
                a = self.vtt(tm.t[:, :], bank.t[:, :], self.bc[:, half * 512:(half + 1) * 512], ALU.mult, tok, tm.free, self.k_gate)
                bank.done(a)
                x = self.xn[:, t * 1024 + half * 512:t * 1024 + (half + 1) * 512]
                a = self.vtt(x, x, tm.t[:, :], ALU.add)
                tm.done(a)
                self.x_ready[t].append(a)

    def rows(self, g, b):
        f = self.fence()
        k = [self.load(self.bc[:, 0:1024], g.partition_broadcast(128), f)]
        if b is not None:
            k.append(self.load(self.bc[:, 1024:2048], b.partition_broadcast(128), f))
        return k

    def final_norm(self):
        kb = self.rows(self.A["final_g"], None)
        f = self.fence()
        for t in range(4):
            xt = self.x_tile(t)
            s = self.V(lambda e, xt=xt, t=t: e.tensor_tensor_reduce(self.bc[:, 1024:2048], xt, xt, 1.0, 0.0, ALU.mult, ALU.add,
                                                                    self.stat[:, t:t + 1]), self.x_ready[t], f)
        r = self.rstd(self.stat[:, 4:8], self.stat[:, 0:4], 1.0 / D, 1e-6, s)
        k = [self.vts(self.x_tile(t), self.x_tile(t), self.stat[:, 4 + t:5 + t], None, ALU.mult, None, r) for t in range(4)]
        self.h_free = f
        self.to_hT(lambda t, d: self.xn[:, t * 1024 + d * 128:t * 1024 + (d + 1) * 128], k,
                   lambda d: self.col(("final_g",), d), None)
        tp = self.PE.last()
        self.x_ready = []
        for t in range(4):
            xt = self.x_tile(t)
            self.x_ready.append([self.G(lambda e, xt=xt: e.tensor_tensor(xt, xt, self.bc[:, 0:1024], ALU.mult), tp, kb, k)])

    def layer_norm(self, l, name, eps, out=False):
        A = self.A
        kb = self.rows(A[name + "_g_2"][l], A[name + "_b_2"][l])
        f = self.fence()
        st = self.stat
        k = []
        for t in range(4):
            xt = self.x_tile(t)
            for hf in range(2):
                s = self.V(lambda e, xt=xt, hf=hf: e.bn_stats(st[:, 16 + 6 * hf:22 + 6 * hf], xt[:, hf * 512:(hf + 1) * 512]),
                           self.x_ready[t])
            s = self.V(lambda e, t=t: e.bn_aggr(st[:, 4 * t:4 * t + 2], st[:, 16:28]))
            r = self.rstd(st[:, 4 * t + 2:4 * t + 3], st[:, 4 * t + 1:4 * t + 2], 1.0, eps, s)
            k.append(self.vts(xt, xt, st[:, 4 * t:4 * t + 1], st[:, 4 * t + 2:4 * t + 3], ALU.subtract, ALU.mult, r))
        tp = None
        if not out:
            self.h_free = f
            self.to_hT(lambda t, d: self.xn[:, t * 1024 + d * 128:t * 1024 + (d + 1) * 128], k,
                       lambda d: self.col((name + "g", l), d), lambda d: self.col((name + "b", l), d))
            tp = self.PE.last()
        self.x_ready = []
        for t in range(4):
            xt = self.x_tile(t)
            self.G(lambda e, xt=xt: e.tensor_tensor(xt, xt, self.bc[:, 0:1024], ALU.mult), tp, kb, k[t])
            self.x_ready.append([self.G(lambda e, xt=xt: e.tensor_tensor(xt, xt, self.bc[:, 1024:2048], ALU.add))])

    def ffn(self, l, name):
        f = self.fence()
        ready = []
        for m in range(NFF):
            (gb, tg), = self.gemm_t(name + "_w_gu_2", (l,), m * 128, self.h_rhs, self.l_rhs, self.h_ready)
            (ub, tu), = self.gemm_t(name + "_w_gu_2", (l,), FF + m * 128, self.h_rhs, self.l_rhs, self.h_ready)
            tm = self.tmp.take()
            t = self.act(tm.t[:, :], gb.t[:, :], ACT.Silu, tg, tm.free)
            gb.done(t)
            t = self.vtt(tm.t[:, :], tm.t[:, :], ub.t[:, :], ALU.mult, t, tu)
            ub.done(t)
            k = self.split(tm.t[:, :], self.fh[:, m * 512:(m + 1) * 512], self.fl[:, m * 512:(m + 1) * 512], t, f)
            tm.done(*k)
            ready += k
        self.project(name + "_w_down_2", l, [256 * i for i in range(11)],
                     self.fh, self.fl, [ready[-1], ready[-2]], 2 * ALPHA)

    def project(self, name, l, k0s, ah, al, ready, s):
        xr = [[] for _ in range(4)]
        for half in range(2):
            rota = (self.ps, self.pg)[half]
            out = self.gemm_n(name, (l,), k0s, 512 * half, lambda k, t: ah[:, k * 512 + t * 128:k * 512 + (t + 1) * 128],
                              lambda k, t: al[:, k * 512 + t * 128:k * 512 + (t + 1) * 128], ready, rota)
            for t, (bank, tok) in enumerate(out):
                x = self.xn[:, t * 1024 + half * 512:t * 1024 + (half + 1) * 512]
                a = self.stt(x, x, s, bank.t[:, :], ALU.mult, ALU.add, tok, self.x_ready[t])
                bank.done(a)
                xr[t].append(a)
        self.x_ready = xr

    def layer_b(self, l):
        self.ffn(l, "ffn1")
        self.layer_norm(l, "ln1", 4e-5)
        self.mixer(l)
        self.layer_norm(l, "ln2", 1e-5)
        self.ffn(l, "ffn2")
        self.layer_norm(l, "ln3", 4e-5, out=l == DEPTH - 1)

    def mixer(self, l):
        A = self.A
        f = self.fence()
        k_c = [self.load(self.rcos[:, :], A["rcos"], f), self.load(self.rsin[:, :], A["rsin"], f),
               self.load(self.amask[:, :], A["amask"], f), self.load(self.mean256[:, :], A["mean256"], f),
               self.load(self.sink[:, :], A["attn_sink_2"][l].partition_broadcast(128), f)]
        proj = lambda col, **kw: self.gemm_t("w_in_2", (l,), col, self.h_rhs, self.l_rhs, self.h_ready, **kw)
        z = [x[:, :] for x in self.t3]
        half = lambda x, j: x[:, j * 512:(j + 1) * 512]
        cp = self.ccp[:, :].rearrange("p (j n) -> p j n", j=2)
        sp = self.scp[:, :].rearrange("p (j n) -> p j n", j=2)
        self.V(lambda e: e.memset(self.ccp[:, :], 0.0), f)
        self.V(lambda e: e.memset(self.scp[:, :], 0.0), f)
        for j in range(2):
            (ba, ta), = proj(1536 + j * 128)
            (bg, tg), = proj(1792 + j * 128)
            t = self.act(z[0], bg.t[:, :], ACT.Sigmoid, tg, f, self.V.last())
            bg.done(t)
            t = self.vtt(cp[:, j, 15:527], ba.t[:, :], z[0], ALU.mult, t, ta)
            ba.done(t)
        rot = []
        for n in range(5):
            (b_, t), = proj(768 + n * 128)
            dst = half(self.qT, n) if n < 4 else self.kT[:, :]
            t = self.S(lambda e, b_=b_: e.copy(z[1], b_.t[:, :]), t, self.V.last())
            b_.done(t)
            rot.append(self.rope(z[1], dst, z[2], self.rcos[:, :], self.rsin[:, :], 32, t, k_c, f, self.V.last()))
            self.G.wait(rot[-1])
        wh, wl, tok, n = self.unit("w_in_2", (l,), t_pieces(1408))
        vk = self.ps.take()
        for t in range(4):
            for k in range(8):
                tv = self.mm3(vk.t[:, t * 128:(t + 1) * 128], self.h_lhs(k, t), self.l_lhs(k, t), wh[:, k * 128:(k + 1) * 128],
                              wl[:, k * 128:(k + 1) * 128], k == 0, k == 7, tok, vk.free, self.h_ready)
        self.used[n] = tv
        kv = self.S(lambda e: e.copy(self.v2[:, :], vk.t[:, :]), tv, f)
        vk.done(kv)
        ready = []
        for j in range(2):
            (bc_, tc), = proj(256 + j * 128)
            (bh, th), = proj(512 + j * 128)
            t = self.S(lambda e, bc_=bc_: e.copy(z[0], bc_.t[:, :]), tc, self.V.last())
            bc_.done(t)
            t = self.vtt(sp[:, j, 1:513], z[0], bh.t[:, :], ALU.mult, t, th)
            bh.done(t)
            (bb, tb), = proj(j * 128)
            self.vts(z[1], sp[:, j, 0:512], self.col(("sc", l, 0), j), None, ALU.mult, None)
            for w in (1, 2):
                self.stt(z[1], sp[:, j, w:w + 512], self.col(("sc", l, w), j), z[1], ALU.mult, ALU.add)
            t = self.vtt(z[1], z[1], bb.t[:, :], ALU.mult, tb)
            bb.done(t)
            k = self.split(z[1], half(self.xh8, j), half(self.xl8, j), t, f)
            self.V.wait(*k)
            ready += k
        for nb in range(4):
            k0, k1 = max(nb - 1, 0), min(nb + 2, 4)
            nk = k1 - k0
            mo = (k0 - nb + 1) * 128
            ob = self.ps.take()
            to = None
            dn = self.den
            for h in range(8):
                kvh = h // 4
                p, q = h // 2, 64 * (h % 2)
                sb = self.ps.take()
                if sb is ob:
                    sb = self.ps.take()
                kt = (self.kT if q == 64 * kvh else self.kS)
                t = self.PE(lambda e, sb=sb, p=p, q=q, kt=kt, nb=nb, nk=nk, k0=k0: e.matmul(
                    sb.t[:, 0:nk * 128], self.qT[q:q + 64, p * 512 + nb * 128:p * 512 + (nb + 1) * 128],
                    kt[q:q + 64, k0 * 128:(k0 + nk) * 128], start=True, stop=True), sb.free, rot, self.k_ks(l, rot, f))
                pr, sm = self.pr.take(), self.sm.take()
                P, s = pr.t[:, 0:nk * 128], sm.t
                self.V(lambda e, P=P, sb=sb, nk=nk, mo=mo, s=s: e.tensor_tensor_reduce(
                    P, sb.t[:, 0:nk * 128], self.amask[:, mo:mo + nk * 128], 1.0, -3e38, ALU.add, ALU.max, s[:, 0:1]),
                    t, pr.free, sm.free, k_c, f)
                sb.done(self.V.last())
                self.vts(s[:, 0:1], s[:, 0:1], 0.125, self.sink[:, h:h + 1], ALU.mult, ALU.max)
                self.vts(s[:, 1:2], s[:, 0:1], -1.0, None, ALU.mult, None)
                t = self.V.last()
                te = self.S(lambda e, P=P, s=s: e.activation(P, P, ACT.Exp, bias=s[:, 1:2], scale=0.125, accum_out=s[:, 2:3]), t)
                te = self.act(s[:, 3:4], self.sink[:, h:h + 1], ACT.Exp, bias=s[:, 1:2])
                td = self.G(lambda e, s=s, h=h: e.tensor_tensor(dn[:, h:h + 1], s[:, 2:3], s[:, 3:4], ALU.add), te, self.den_free)
                sm.done(td)
                tb = self.ps.take()
                if tb is ob:
                    tb = self.ps.take()
                t = self.transpose4([P[:, i * 128:(i + 1) * 128] for i in range(nk)], tb, te, self.k_id)
                pr.done(t)
                pT = self.prT.take()
                t = self.S(lambda e, pT=pT, tb=tb, nk=nk: e.copy(pT.t[:, 0:nk * 128], tb.t[:, 0:nk * 128]), t, pT.free)
                tb.done(t)
                for i in range(nk):
                    to = self.PE(lambda e, ob=ob, h=h, i=i, pT=pT, nk=nk, k0=k0, kvh=kvh: e.matmul(
                        ob.t[:, h * 64:(h + 1) * 64], pT.t[:, i * 128:(i + 1) * 128],
                        self.v2[:, (k0 + i) * 128 + kvh * 64:(k0 + i) * 128 + kvh * 64 + 64], start=i == 0, stop=i == nk - 1,
                        skip_group_check=True), t, kv, ob.free, signal=i == nk - 1)
                pT.done(to)
            self.V(lambda e: e.reciprocal(dn[:, 8:16], dn[:, 0:8]), td)
            t = self.vtt(self.ao[:, :].rearrange("p (h n) -> p h n", h=8), ob.t[:, :].rearrange("p (h n) -> p h n", h=8),
                         dn[:, 8:16].unsqueeze(2).broadcast_to([128, 8, 64]), ALU.mult, to, self.ao_free)
            self.den_free = [t]
            ob.done(t)
            tb = self.ps.take()
            t = self.transpose4([self.ao[:, i * 128:(i + 1) * 128] for i in range(4)], tb, t)
            self.ao_free = [t]
            v8 = lambda x: x[:, 1024:3072].rearrange("p (j n) -> p j n", j=4)[:, :, nb * 128:(nb + 1) * 128]
            k = self.split(tb.t[:, :].rearrange("p (j n) -> p j n", j=4), v8(self.xh8), v8(self.xl8), t, f)
            tb.done(*k)
            ready += k
        for j in range(2):
            ac = half(self.acc, j)
            self.vts(ac, cp[:, j, 0:512], self.col(("cc", l, 0), j), self.col(("cc_b", l), j), ALU.mult, ALU.add, f)
            for w in range(1, 31):
                t = self.stt(ac, cp[:, j, w:w + 512], self.col(("cc", l, w), j), ac, ALU.mult, ALU.add)
        mb = self.ps.take()
        for j in range(2):
            t2 = self.PE(lambda e, j=j: e.matmul(mb.t[:, :], self.mean256[:, :], half(self.acc, j), start=j == 0, stop=j == 1),
                         t, mb.free, k_c)
        for j in range(2):
            t = self.vtt(half(self.acc, j), half(self.acc, j), mb.t[:, :], ALU.subtract, t2)
        mb.done(t)
        vb = self.ps.take()
        for j in range(2):
            t3 = self.act(z[j], half(self.acc, j), ACT.Square, t)
        for j in range(2):
            t3 = self.PE(lambda e, j=j, t3=t3: e.matmul(vb.t[:, :], self.mean256[:, :], z[j], start=j == 0, stop=j == 1), t3, vb.free)
        t = self.vts(z[2], vb.t[:, :], 1e-5, None, ALU.add, None, t3)
        vb.done(t)
        t = self.act(z[2], z[2], ACT.Sqrt, t)
        self.V(lambda e: e.reciprocal(z[2], z[2]), t)
        for j in range(2):
            ac = half(self.acc, j)
            t = self.stt(ac, ac, self.col(("cc_lg", l), j), z[2], ALU.mult, ALU.mult)
            t = self.act(ac, ac, ACT.Silu, t, bias=self.col(("cc_lb", l), j))
            ready += self.split(ac, half(self.xh8, 6 + j), half(self.xl8, 6 + j), t, f)
        self.project("w_out_2", l, [0, 256, 512, 768], self.xh8, self.xl8, ready, ALPHA)

    def k_ks(self, l, rot, f):
        if self.ks_layer != l:
            self.ks_layer = l
            self.G(lambda e: e.tensor_copy(self.kS[0:64, :], self.kT[64:128, :]), rot, f)
            self.ks_tok = self.G(lambda e: e.tensor_copy(self.kS[64:128, :], self.kT[0:64, :]))
        return self.ks_tok

    def finish(self):
        n = 0
        for t in range(4):
            self.SP.wait(*self.x_ready[t])
            x = self.x_tile(t)
            o = self.A["out"][0, t * 128:(t + 1) * 128, :]
            self.SP.todo.append(lambda e, o=o, x=x: e.dma_start(o, x).then_inc(self.s_out, 16))
            n += 16
        self.SP.todo.append(lambda e: e.wait_ge(self.s_out, n))


N_UNITS = 0


def program(nc, A, n_units):
    p = Program(nc, A, n_units)
    p.run()
    return p


def unit_count():
    a = 24 + 65 + 12 + 8
    b = 2 * (2 * NFF + NFF) + 16 + 8
    return DEPTH * (a + b)


_DIRECT = ["x", "positions", "b_ada", "pool_w", "rwkv_w2", "rwkv_a2", "final_g", "attn_sink_2",
           "ln1_g_2", "ln1_b_2", "ln2_g_2", "ln2_b_2", "ln3_g_2", "ln3_b_2"]


def kernel(**inputs):
    import concourse.bacc as bacc
    from concourse.bass_utils import run_bass_kernel_spmd

    inputs = {k: np.asarray(v) for k, v in inputs.items()}
    nc = bacc.Bacc("TRN2", target_bir_lowering=False, num_devices=1)
    spec = columns()
    arrays = {}
    for name in _DIRECT:
        arrays[name] = np.ascontiguousarray(inputs[name])
    cols = np.empty((128, len(spec.pieces)), np.float32)
    flat = {}
    for j, col in enumerate(spec.pieces):
        at = 0
        for name, index, s, n in col:
            v = inputs[name][index].reshape(-1)
            cols[at:at + n, j] = v[s:s + n]
            at += n
    arrays["cols"] = cols
    arrays.update(constants())
    A = {}
    for name, a in arrays.items():
        A[name] = nc.dram_tensor(f"in_{name}", a.shape, mybir.dt.from_np(a.dtype), kind="ExternalInput").ap()
    nu = unit_count()
    A["W"] = nc.dram_tensor("in_W", (nu, 128, 1024), F32, kind="ExternalInput").ap()
    A["out"] = nc.dram_tensor("out", (1, T, D), F32, kind="ExternalOutput").ap()
    prog = program(nc, A, nu)
    arrays["W"] = pack_units(prog.units, inputs)
    r = run_bass_kernel_spmd(nc, [{f"in_{k}": v for k, v in arrays.items()}], core_ids=[0])
    return r.results[0]["out"]
```

```python
from contextlib import ExitStack
import itertools

import numpy as np
import concourse.bass as bass
from concourse import mybir

F32 = mybir.dt.float32
FR = mybir.dt.float32r
I32 = mybir.dt.int32
U32 = mybir.dt.uint32
ALU = mybir.AluOpType
ACT = mybir.ActivationFunctionType
AX = mybir.AxisListType

T = 512
D = 1024
DEPTH = 2
FF = 2816
NFF = FF // 128
RAW = 3
RING = 4
ALPHA = (2.0 * DEPTH) ** 0.25
KAPPA = float(np.exp(-0.5))
POOLW = (2, 4, 8, 16)


class Columns:

    def __init__(self):
        self.pieces = []
        self.at = {}

    def add(self, key, name, index, spans):
        self.at[key] = len(self.pieces)
        flat = [(name, index, s, n) for s, n in spans]
        col, room = [], 128
        for name_, ix, s, n in flat:
            while n:
                m = min(n, room)
                col.append((name_, ix, s, m))
                s, n, room = s + m, n - m, room - m
                if room == 0:
                    self.pieces.append(col)
                    col, room = [], 128


def columns():
    c = Columns()
    full = [(0, 512)]
    for l in range(DEPTH):
        c.add(("norm_g", l), "norm_g", (l,), [(0, 1024)])
        c.add(("b_ada", l), "b_ada", (l,), [(0, 2048)])
        c.add(("pool_scale", l), "pool_scale", (l,), full)
        c.add(("ret_g", l), "ret_norm_g", (l,), full)
        c.add(("mu_r", l), "rwkv_shift_mu", (l,), [(0, 512)])
        c.add(("mu_k", l), "rwkv_shift_mu", (l,), [(576, 512)])
        c.add(("mu_v", l), "rwkv_shift_mu", (l,), [(1088, 512)])
        c.add(("mu_wa", l), "rwkv_shift_mu", (l,), [(512, 64), (1600, 64)])
        for k, n in (("w0", "rwkv_w0"), ("a0", "rwkv_a0"), ("k_k", "rwkv_k_k"), ("k_a", "rwkv_k_a"),
                     ("r_k", "rwkv_r_k"), ("ln_w", "rwkv_ln_w"), ("ln_b", "rwkv_ln_b")):
            c.add((k, l), n, (l,), full)
        for k in ("ln1", "ln2", "ln3"):
            c.add((k + "g", l), k + "_g_2", (l,), [(0, 1024)])
            c.add((k + "b", l), k + "_b_2", (l,), [(0, 1024)])
        for j in range(3):
            c.add(("sc", l, j), "sc_conv_w_2", (l, j), [(0, 256)])
        for j in range(31):
            c.add(("cc", l, j), "cc_conv_w_2", (l, j), [(0, 256)])
        c.add(("cc_b", l), "cc_conv_b_2", (l,), [(0, 256)])
        c.add(("cc_lg", l), "cc_ln_g_2", (l,), [(0, 256)])
        c.add(("cc_lb", l), "cc_ln_b_2", (l,), [(0, 256)])
    c.add(("final_g",), "final_g", (), [(0, 1024)])
    c.add(("c",), "c", (0,), [(0, 1024)])
    return c


def constants():
    p = np.arange(128)
    i = np.arange(512)
    out = {}
    out["ident"] = np.eye(128, dtype=np.float32)
    out["blk64"] = (p[:, None] // 64 == p[None, :] // 64).astype(np.float32)
    out["mean256"] = np.full((128, 128), 1.0 / 256, np.float32)
    half = 64
    fr = (np.float32(10000.0) ** (-np.arange(half, dtype=np.float32) / half)).astype(np.float32)
    sign = np.where(p < 64, -1.0, 1.0).astype(np.float32)
    out["misc"] = np.stack([fr[p % 64], sign], 1).astype(np.float32)
    lg = np.log1p(-(2.0 ** (-5.0 - np.arange(4))))
    dm = np.zeros((128, 4, 512), np.float64)
    for h in range(4):
        d = i[None, :] - p[:, None]
        dm[:, h] = np.where(d >= 0, np.exp(lg[h] * np.maximum(d, 0)), 0) * 128.0 ** -0.5
    out["decay"] = dm.reshape(128, 2048).astype(np.float32)
    s, t = p[:, None], p[None, :]
    strict, incl = (s < t), (s <= t)
    out["gmask"] = np.concatenate([strict, incl, strict, incl], 1).astype(np.float32)
    out["m1"] = ((s // 2 == t // 2) & (s < t)).astype(np.float32)
    lm = []
    for n in (2, 4, 8, 16):
        x = (p[:, None] // (2 * n) == p[None, :] // (2 * n)) & (p[:, None] % (2 * n) >= n) & (p[None, :] % (2 * n) < n)
        lm.append(x.T)
    out["lmask"] = np.concatenate(lm, 1).astype(np.uint32)
    out["reset"] = np.broadcast_to((i % 128 != 0).astype(np.float32), (128, 512)).copy()
    cnt = np.stack([1.0 / np.minimum(i + 1, w) for w in POOLW]).reshape(-1)
    out["invcnt"] = np.broadcast_to(cnt.astype(np.float32), (128, 2048)).copy()
    inv = (np.float32(10000.0) ** (-np.arange(32, dtype=np.float32) / 32)).astype(np.float32)
    ang = (i.astype(np.float32)[None, :] * inv[p % 32][:, None]).astype(np.float32).astype(np.float64)
    sg = np.where(p % 64 < 32, -1.0, 1.0)[:, None]
    out["rcos"] = np.cos(ang).astype(np.float32)
    out["rsin"] = (np.sin(ang) * sg).astype(np.float32)
    j = np.arange(384)[None, :] - 128
    out["amask"] = np.where(np.abs(p[:, None] - j) <= 128, 0.0, -1e30).astype(np.float32)
    return out


def pack_units(units, inputs):
    out = np.empty((len(units), 128, 1024), np.float32)
    for n, (name, index, pieces) in enumerate(units):
        w = inputs[name][index]
        at = 0
        for k, c, m in pieces:
            out[n, :, at:at + m] = w[k:k + 128, c:c + m]
            at += m
    return out


def t_pieces(col, k0=0, nk=8, groups=1):
    return tuple((k0 + 128 * k, col + 128 * g, 128) for g in range(groups) for k in range(nk))


def n_pieces(k, col):
    return ((k, col, 512), (k + 128, col, 512))


class Queue:

    def __init__(self, sem, serial):
        self.sem, self.serial = sem, serial
        self.n, self.seen, self.todo = 0, {}, []

    def wait(self, *tokens):
        for t in tokens:
            if isinstance(t, list):
                self.wait(*t)
            elif t is not None and self.seen.get(id(t[0]), 0) < t[1]:
                self.seen[id(t[0])] = t[1]
                self.todo.append(lambda e, t=t: e.wait_ge(t[0], t[1]))

    def __call__(self, fn, *tokens, signal=True):
        self.wait(*tokens)
        if self.serial and self.n:
            self.wait((self.sem, self.n))
        if not signal:
            self.todo.append(fn)
            return None
        self.n += 1
        self.todo.append(lambda e: fn(e).then_inc(self.sem, 1))
        return (self.sem, self.n)

    def last(self):
        return (self.sem, self.n) if self.n else None


class Slot:

    def __init__(self, t):
        self.t, self.free, self.held = t, [], False

    def done(self, *tokens):
        self.free, self.held = list(tokens), False


class Rota:
    def __init__(self, tensors):
        self.slots = [t if isinstance(t, Slot) else Slot(t) for t in tensors]
        self.n = 0

    def take(self):
        s = self.slots[self.n % len(self.slots)]
        self.n += 1
        assert not s.held
        s.held = True
        return s


def mix(main, side, main_steps, side_steps):
    done = n = 0
    for _ in main:
        n += 1
        while done < side_steps and done * main_steps < n * side_steps:
            next(side, None)
            done += 1
    for _ in range(done, side_steps):
        next(side, None)


def drain(gen):
    for _ in gen:
        pass


def abreast(*gens):
    gens = list(gens)
    while gens:
        for g in list(gens):
            if next(g, "end") == "end":
                gens.remove(g)
        yield


class Program:

    def __init__(self, nc, A, plan=None):
        self.nc, self.A = nc, A
        self.plan = plan
        self.units, self.kinds = [], []
        self.colspec = columns()
        self.ctx = ExitStack()
        self.nsem = 0
        self.build()

    def sem(self, name):
        self.nsem += 1
        return self.ctx.enter_context(self.nc.semaphore(name))

    def alloc(self, ctx, name, width, dt=F32):
        return ctx.enter_context(self.nc.sbuf_tensor(name, [128, width], dt))

    def load(self, dst, src, *tokens):
        s = self.sem(f"ld{self.nsem}")
        self.SP.wait(*tokens)
        self.SP.todo.append(lambda e: e.dma_start(dst, src).then_inc(s, 16))
        return (s, 16)

    def col(self, key, j=0):
        c = self.colspec.at[key] + j
        return self.cols[:, c:c + 1]

    def fence(self):
        return [q.last() for q in (self.PE, self.V, self.S, self.G)]

    def fetch(self):
        n = self.n_fetched
        if self.plan is None or n >= len(self.plan):
            return
        self.n_fetched += 1
        r = n % RAW
        if n >= RAW:
            self.SP.wait(*self.raw_free[n - RAW])
        src, dst, s = self.A["W"][n], self.raw[:, r * 1024:(r + 1) * 1024], self.s_raw[r]
        self.SP.todo.append(lambda e: e.dma_start(dst, src).then_inc(s, 16))

    def raw_unit(self, n):
        r = n % RAW
        return self.raw[:, r * 1024:(r + 1) * 1024], (self.s_raw[r], 16 * (n // RAW + 1))

    def split_next(self):
        n = self.next_raw
        self.next_raw += 1
        i = self.n_split
        self.n_split += 1
        k = i % RING
        raw, landed = self.raw_unit(n)
        hi, lo = self.whi[:, k * 1024:(k + 1) * 1024], self.wlo[:, k * 1024:(k + 1) * 1024]
        free = self.used[i - RING] if i >= RING else None
        t1 = self.S(lambda e: e.copy(hi, raw), landed, free)
        t2 = self.V(lambda e: e.tensor_tensor(lo, raw, hi.bitcast(F32), ALU.subtract), landed, free, t1)
        self.split_tokens[i] = [t1, t2]
        self.raw_free[n] = [t1, t2]
        self.fetch()

    def ahead(self):
        if self.plan is None:
            return
        while self.next_raw < len(self.plan) and self.plan[self.next_raw] and \
                self.n_split <= self.n_taken + RING - 1 and \
                (self.n_split < RING or self.n_split - RING in self.used):
            self.split_next()

    def unit(self, name, index, pieces):
        self.units.append((name, index, pieces))
        self.kinds.append(True)
        i = self.n_taken
        if self.plan is None:
            self.split_tokens[i] = []
        self.ahead()
        self.n_taken += 1
        k = i % RING
        return (self.whi[:, k * 1024:(k + 1) * 1024], self.wlo[:, k * 1024:(k + 1) * 1024],
                self.split_tokens[i], i)

    def direct(self, name, index, pieces):
        n = len(self.units)
        self.units.append((name, index, pieces))
        self.kinds.append(False)
        assert self.plan is None or self.next_raw == n
        self.next_raw = n + 1
        return self.raw_unit(n) + (n,)

    def release(self, n, token):
        self.raw_free[n] = [token]
        self.fetch()
        self.ahead()

    def mm3(self, out, ah, al, bh, bl, first, last, *tokens, signal=None):
        def three(e):
            e.matmul(out, ah, bh, start=first, stop=False, skip_group_check=True)
            e.matmul(out, ah, bl, start=False, stop=False, skip_group_check=True)
            return e.matmul(out, al, bh, start=False, stop=last, skip_group_check=True)
        return self.PE(three, *tokens, signal=last if signal is None else signal)

    def gemm_t(self, name, index, col, xh, xl, ready, k0=0, nk=8, groups=1, pieces=None, rota=None):
        wh, wl, tok, n = self.unit(name, index, pieces or t_pieces(col, k0, nk, groups))
        out = []
        for g in range(groups):
            bank = (rota or self.pg).take()
            for k in range(nk):
                c = (g * nk + k) * 128
                t = self.mm3(bank.t[:, :], wh[:, c:c + 128], wl[:, c:c + 128], xh(k), xl(k),
                             k == 0, k == nk - 1, tok, bank.free, ready)
            out.append((bank, t))
        self.used[n] = t
        return out

    def gemm_n(self, *args, **kw):
        return list(self.gemm_tiles(*args, **kw))

    def gemm_tiles(self, name, index, k0s, col, xh, xl, ready, rota, late=1):
        banks = [rota.take() for _ in range(4)]
        nk = len(k0s) * 2
        held = []
        for ui, k0 in enumerate(k0s):
            u = self.unit(name, index, n_pieces(k0, col))
            held.append((ui,) + u)
            if 0 <= len(k0s) - late <= ui < len(k0s) - 1:
                continue
            if ui == len(k0s) - 1:
                order = [(h, j, t) for t in range(4) for h in held for j in range(2)]
            else:
                order = [(h, j, t) for h in held for j in range(2) for t in range(4)]
            for q, ((u_, wh, wl, tok, n), j, t) in enumerate(order):
                k = 2 * u_ + j
                fin = k == nk - 1
                end = q == len(order) - 1
                a = self.mm3(banks[t].t[:, :], xh(k, t), xl(k, t), wh[:, j * 512:(j + 1) * 512], wl[:, j * 512:(j + 1) * 512],
                             k == 0, fin, tok, banks[t].free, ready(k) if callable(ready) else ready, signal=fin or end)
                if fin and not end:
                    yield banks[t], a
            for h in held:
                self.used[h[4]] = a
            held = []
        yield banks[3], a

    def split(self, src, hi, lo, *tokens):
        t1 = self.S(lambda e: e.copy(hi, src), *tokens)
        t2 = self.V(lambda e: e.tensor_tensor(lo, src, hi.bitcast(F32), ALU.subtract), t1, *tokens)
        return [t1, t2]

    def vtt(self, o, a, b, op, *tokens):
        return self.V(lambda e: e.tensor_tensor(o, a, b, op), *tokens)

    def vts(self, o, a, s1, s2, op0, op1, *tokens):
        if op1 is None:
            return self.V(lambda e: e.tensor_scalar(o, a, s1, None, op0), *tokens)
        return self.V(lambda e: e.tensor_scalar(o, a, s1, s2, op0, op1), *tokens)

    def stt(self, o, a, s, b, op0, op1, *tokens):
        return self.V(lambda e: e.scalar_tensor_tensor(out=o, in0=a, scalar=s, in1=b, op0=op0, op1=op1), *tokens)

    def act(self, o, a, f, *tokens, bias=0.0, scale=1.0):
        return self.S(lambda e: e.activation(o, a, f, bias=bias, scale=scale), *tokens)

    def rstd(self, o, var, mul, eps, *tokens):
        w = o.shape[1]
        self.G(lambda e: e.tensor_scalar(o, var, mul, eps, ALU.mult, ALU.add), *tokens)
        return self.G(lambda e: e.tensor_tensor(o, o, self.mhalf[:, 0:w], ALU.pow))

    def transpose4(self, ins, bank, *tokens):
        t = None
        for j, x in enumerate(ins):
            o = bank.t[:, j * 128:(j + 1) * 128]
            t = self.PE(lambda e, o=o, x=x: e.transpose(o, x, self.ident[:, :]), bank.free, *tokens,
                        signal=j == len(ins) - 1)
        return t

    def build(self):
        nc, A = self.nc, self.A
        self.n_fetched = self.n_split = self.n_taken = self.next_raw = 0
        self.split_tokens, self.used, self.raw_free = {}, {}, {}
        ctx = self.ctx
        self.PE = Queue(self.sem("s_pe"), False)
        self.V = Queue(self.sem("s_dve"), True)
        self.S = Queue(self.sem("s_act"), True)
        self.G = Queue(self.sem("s_pool"), True)
        self.SP = Queue(None, False)
        self.s_raw = [self.sem(f"s_raw{i}") for i in range(RAW)]
        self.s_out = self.sem("s_out")
        a = lambda n, w, dt=F32: self.alloc(ctx, n, w, dt)
        self.raw = a("raw", RAW * 1024)
        self.whi, self.wlo = a("whi", RING * 1024, FR), a("wlo", RING * 1024, FR)
        self.hh, self.hl = a("hh", 4096, FR), a("hl", 4096, FR)
        self.cols = a("cols", len(self.colspec.pieces))
        self.ident = a("ident", 128)
        self.mhalf = a("mhalf", 16)
        self.stat = a("stat", 64)
        self.mod = [a(f"mod{l}", 24) for l in range(DEPTH)]
        self.cact = a("cact", 16)
        cr = ExitStack()
        self.xn = self.alloc(cr, "xn", 4096)
        cr.close()
        cr = ExitStack()
        set0 = self.chunk_set(cr, 0)
        cr.close()
        self.RT = [a(f"RT{i}", 512) for i in range(8)]
        self.tmp = Rota([a(f"tmp{i}", 512) for i in range(2)])
        banks = [ctx.enter_context(nc.psum_tensor(f"bank{i}", [128, 512], F32)) for i in range(8)]
        self.all4, self.ps = Rota(banks[:4]), Rota(banks[4:])
        self.main2, self.side2 = Rota(self.all4.slots[:2]), Rota(self.all4.slots[2:])
        self.pg = self.all4

        ca = ExitStack()
        b = lambda n, w, dt=F32, c=ca: self.alloc(c, n, w, dt)
        co = ExitStack()
        self.oh, self.ol = b("oh", 2048, FR, co), b("ol", 2048, FR, co)
        co.close()
        self.sg2 = b("sg2", 4096)
        self.mrg = b("mrg", 4096)
        self.blk64 = b("blk64", 128)
        self.misc = b("misc", 2)
        c1 = ExitStack()
        self.ph, self.pl = b("ph", 2048, FR, c1), b("pl", 2048, FR, c1)
        self.poolw = b("poolw", 512, c=c1)
        self.invcnt = b("invcnt", 2048, c=c1)
        self.decay = b("decay", 2048, c=c1)
        self.vret = b("vret", 2048, c=c1)
        self.qk = Rota([b(f"qk{i}", 1536, c=c1) for i in range(2)])
        self.pt = b("pt", 2048, c=c1)
        self.onat = b("onat", 512, c=c1)
        self.sgr = b("sgr", 512, c=c1)
        self.cosr, self.sinr = b("cosr", 512, c=c1), b("sinr", 512, c=c1)
        c1.close()
        cx = ExitStack()
        self.xs = b("xs", 4096, c=cx)
        cx.close()
        c2 = ExitStack()
        self.AR = b("AR", 4096, c=c2)
        self.KH, self.BH = b("KH", 2048, c=c2), b("BH", 2048, c=c2)
        self.VN, self.VB = b("VN", 2048, c=c2), b("VB", 2048, c=c2)
        self.gmask, self.m1 = b("gmask", 512, c=c2), b("m1", 128, c=c2)
        self.lmask = b("lmask", 512, U32, c2)
        self.em = b("em", 64, c=c2)
        self.st = b("st", 256, c=c2)
        c3 = ExitStack()
        self.PP = b("PP", 513, c=c3)
        self.reset = b("reset", 512, c=c3)
        self.wa = b("wa", 512, c=c3)
        self.w2a2 = b("w2a2", 512, c=c3)
        c3.close()
        c4 = ExitStack()
        self.sets = [set0, self.chunk_set(c4, 1)]
        for g, z in enumerate(self.sets):
            for n, w in (("KN", 256), ("BN", 256), ("YN", 256), ("SP", 256), ("hs", 12)):
                z[n] = b(f"{n}{g}", w, c=c4)
        c4.close()
        c4 = ExitStack()
        self.o2h, self.o2l = b("o2h", 2048, FR, c4), b("o2l", 2048, FR, c4)
        c4.close()
        c2.close()
        c5 = ExitStack()
        self.mh, self.ml = b("mh", 4096, FR, c5), b("ml", 4096, FR, c5)
        self.gate = b("gate", 1024, c=c5)
        self.crep = b("crep", 1024, c=c5)
        c5.close()
        ca.close()

        cb = ExitStack()
        d = lambda n, w, dt=F32, c=cb: self.alloc(c, n, w, dt)
        self.bc = d("bc", 2048)
        cf = ExitStack()
        self.fh, self.fl = d("fh", NFF * 512, FR, cf), d("fl", NFF * 512, FR, cf)
        cf.close()
        cm = ExitStack()
        self.xh8, self.xl8 = d("xh8", 4096, FR, cm), d("xl8", 4096, FR, cm)
        self.qT = d("qT", 2048, c=cm)
        self.kT, self.kS = d("kT", 512, c=cm), d("kS", 512, c=cm)
        self.v2 = d("v2", 512, c=cm)
        self.rcos, self.rsin, self.amask = d("rcos", 512, c=cm), d("rsin", 512, c=cm), d("amask", 384, c=cm)
        self.mean256 = d("mean256", 128, c=cm)
        self.sink = d("sink", 8, c=cm)
        self.ccp = d("ccp", 1088, c=cm)
        self.scp = d("scp", 1088, c=cm)
        self.acc = d("acc", 1024, c=cm)
        self.pr = Rota([d(f"pr{i}", 384, c=cm) for i in range(8)])
        self.prT = Rota([d(f"prT{i}", 384, c=cm) for i in range(3)])
        self.ao = Rota([d("ao0", 512, c=cm)])
        self.sm = Rota([d(f"sm{i}", 20, c=cm) for i in range(2)])
        self.rq = Rota([d(f"rq{i}", 1024, c=cm) for i in range(2)])
        self.t3 = [d(f"tz{i}", 512, c=cm) for i in range(2)]
        self.zc = d("zc", 1024, c=cm)
        cm.close()
        cb.close()

        self.k_cols = self.load(self.cols[:, :], A["cols"])
        for _ in range(RAW):
            self.fetch()
        self.k_id = self.load(self.ident[:, :], A["ident"])
        self.load_x(A["x"][0])
        self.k_half = self.G(lambda e: e.memset(self.mhalf[:, :], -0.5))
        self.k_xd = None
        self.prepare_a()
        drain(self.modulation(0))
        for l in range(DEPTH):
            self.layer_a(l)
        self.final_norm()
        for l in range(DEPTH):
            self.layer_b(l)
        self.finish()

    def chunk_set(self, ctx, g):
        z = {n: self.alloc(ctx, f"{n}{g}", w) for n, w in (("G4", 2048), ("X", 512), ("U", 512), ("Y", 512))}
        z["free"] = []
        return z

    def load_x(self, src, *tokens):
        self.x_ready = [[self.load(self.x_tile(t), src[t * 128:(t + 1) * 128, :], *tokens)] for t in range(4)]

    def run(self):
        with self.ctx:
            block = self.ctx.enter_context(self.nc.Block())
            for reg, q in ((block.sync, self.SP), (block.gpsimd, self.G), (block.scalar, self.S),
                           (block.vector, self.V), (block.tensor, self.PE)):
                def body(e, q=q):
                    for f in q.todo:
                        f(e)
                reg(body)

    def x_tile(self, t):
        return self.xn[:, t * 1024:(t + 1) * 1024]

    def to_hT(self, blocks, ready, scale, bias):
        f = self.h_free
        toks = []
        for d in range(8):
            bank = self.ps.take()
            t = self.transpose4([blocks(j, d) for j in range(4)], bank, self.k_id, ready)
            tm = self.tmp.take()
            if bias is None:
                t1 = self.vts(tm.t[:, :], bank.t[:, :], scale(d), None, ALU.mult, None, t, tm.free)
            else:
                t1 = self.act(tm.t[:, :], bank.t[:, :], ACT.Identity, t, tm.free, bias=bias(d), scale=scale(d))
            bank.done(t1)
            k = self.split(tm.t[:, :], self.hh[:, d * 512:(d + 1) * 512], self.hl[:, d * 512:(d + 1) * 512], t1, f)
            tm.done(*k)
            toks += k
        self.h_ready = toks
        return toks

    def h_rhs(self, k):
        return self.hh[:, k * 512:(k + 1) * 512]

    def l_rhs(self, k):
        return self.hl[:, k * 512:(k + 1) * 512]

    def h_lhs(self, k, t):
        return self.hh[:, k * 512 + t * 128:k * 512 + (t + 1) * 128]

    def l_lhs(self, k, t):
        return self.hl[:, k * 512 + t * 128:k * 512 + (t + 1) * 128]

    def prepare_a(self):
        A = self.A
        self.h_free = []
        self.k_misc = [self.load(self.misc[:, :], A["misc"]), self.load(self.blk64[:, :], A["blk64"])]
        k_pos = self.load(self.xs[:, 0:512].bitcast(I32), A["positions"][0].partition_broadcast(128))
        x = [self.xs[:, i * 512:(i + 1) * 512] for i in range(6)]
        self.V(lambda e: e.tensor_copy(x[1], x[0].bitcast(I32)), k_pos)
        self.vts(x[1], x[1], self.misc[:, 0:1], None, ALU.mult, None, *self.k_misc)
        big = 12582912.0
        c1 = 6.28125
        c2 = float(np.float32(2 * np.pi - c1))
        c3 = float(2 * np.pi - c1 - float(np.float32(c2)))
        pi = 3.1415925
        for off, out in ((0.25, x[4]), (0.0, x[5])):
            self.vts(x[2], x[1], float(1 / (2 * np.pi)), off, ALU.mult, ALU.add)
            self.vts(x[2], x[2], big, None, ALU.add, None)
            self.vts(x[2], x[2], big, None, ALU.subtract, None)
            self.stt(x[3], x[2], -c1, x[1], ALU.mult, ALU.add)
            self.stt(x[3], x[2], -c2, x[3], ALU.mult, ALU.add)
            self.stt(x[3], x[2], -c3, x[3], ALU.mult, ALU.add)
            self.vts(x[3], x[3], float(off * 2 * np.pi), pi, ALU.add, ALU.min)
            t = self.vts(x[3], x[3], -pi, None, ALU.max, None)
            t = self.act(out, x[3], ACT.Sin, t)
            self.V.wait(t)
        t = self.vts(x[5], x[5], self.misc[:, 1:2], None, ALU.mult, None, t)
        self.k_tab = [self.load(A["rot"][i], x[4 + i], t) for i in range(2)]
        cc = self.colspec.at[("c",)]
        t = self.act(self.cact[:, 8:16], self.cols[:, cc:cc + 8], ACT.Sigmoid, self.k_cols)
        self.k_cact = self.vtt(self.cact[:, 0:8], self.cols[:, cc:cc + 8], self.cact[:, 8:16], ALU.mult, t, self.k_cols)

    def modulation(self, l):
        bank = self.side2.take()
        for m in range(16):
            w, landed, n = self.direct("w_ada", (l,), t_pieces(128 * m))
            for k in range(8):
                t = self.PE(lambda e, m=m, k=k, w=w, bank=bank: e.matmul(
                    bank.t[:, m:m + 1], w[:, k * 128:(k + 1) * 128], self.cact[:, k:k + 1], start=k == 0, stop=k == 7,
                    skip_group_check=True), landed, bank.free, self.k_cact, signal=k == 7)
            self.release(n, t)
            if m % 4 == 3 and m < 15:
                o = self.mod[l][:, m - 3:m + 1]
                t = self.S(lambda e, o=o, m=m, bank=bank: e.copy(o, bank.t[:, m - 3:m + 1]), t)
                bank.done(t)
                bank = self.side2.take()
                yield
        t = self.S(lambda e, bank=bank: e.copy(self.mod[l][:, 12:16], bank.t[:, 12:16]), t)
        bank.done(t)
        ba = self.colspec.at[("b_ada", l)]
        ng = self.colspec.at[("norm_g", l)]
        mod = self.mod[l]
        self.vtt(mod[:, 0:16], mod[:, 0:16], self.cols[:, ba:ba + 16], ALU.add, t, self.k_cols)
        self.k_mod = self.stt(mod[:, 16:24], mod[:, 8:16], 1.0, self.cols[:, ng:ng + 8], ALU.add, ALU.mult)
        yield

    def gates(self, l, f):
        A = self.A
        t1 = self.V(lambda e: e.tensor_copy(self.crep[:, :].rearrange("p (k n) -> p k n", k=8),
                                            self.cact[:, 0:8].unsqueeze(2).broadcast_to([128, 8, 128])), f, self.k_cact)
        kb = self.load(self.gate[:, :], A["b_ada"][l, 2048:3072].partition_broadcast(128), f)
        self.k_gate = []
        for half in range(2):
            bank = self.pg.take()
            for ui in range(4):
                w, landed, n = self.direct("w_ada", (l,), n_pieces(256 * ui, 2048 + 512 * half))
                for j in range(2):
                    k = 2 * ui + j
                    t = self.PE(lambda e, w=w, k=k, j=j, bank=bank: e.matmul(
                        bank.t[:, :], self.crep[:, k * 128:(k + 1) * 128], w[:, j * 512:(j + 1) * 512],
                        start=k == 0, stop=k == 7), landed, bank.free, t1, signal=j == 1)
                self.release(n, t)
            g = self.gate[:, half * 512:(half + 1) * 512]
            t = self.vtt(g, bank.t[:, :], g, ALU.add, t, kb)
            bank.done(t)
            self.k_gate.append(t)

    def layer_a(self, l):
        A = self.A
        f = self.fence()
        tt = []
        for t in range(4):
            xt, xs = self.x_tile(t), self.xs[:, t * 1024:(t + 1) * 1024]
            tt.append(self.S(lambda e, xt=xt, xs=xs, t=t: e.activation(xs, xt, ACT.Square, accum_out=self.stat[:, t:t + 1]),
                             self.x_ready[t], f))
        r = self.rstd(self.stat[:, 4:8], self.stat[:, 0:4], 1.0 / D, 1e-6, tt[-1], f)
        k = []
        for t in range(4):
            k.append(self.vts(self.xs[:, t * 1024:(t + 1) * 1024], self.x_tile(t), self.stat[:, 4 + t:5 + t], None,
                              ALU.mult, None, r, tt[t]))
        self.h_free = f
        self.to_hT(lambda t, d: self.xs[:, t * 1024 + d * 128:t * 1024 + (d + 1) * 128], k + [self.k_mod],
                   lambda d: self.mod[l][:, 16 + d:17 + d], lambda d: self.mod[l][:, d:d + 1])
        self.proj = lambda col, **kw: self.gemm_t("w_in", (l,), col, self.h_rhs, self.l_rhs, self.h_ready, **kw)
        f = self.fence()
        self.k_pw = self.load(self.poolw[:, :].rearrange("p (g d) -> p g d", g=4),
                              A["pool_w"][l].rearrange("g c d -> c g d"), f)
        self.k_ic = self.load(self.invcnt[:, :], A["invcnt"], f)
        self.k_dc = self.load(self.decay[:, :], A["decay"], f)
        self.k_rot = [self.load(self.cosr[:, :], A["rot"][0], f, self.k_tab), self.load(self.sinr[:, :], A["rot"][1], f, self.k_tab)]
        k = self.pool(l, f)
        self.pg = self.main2
        side = self.branch(l, 0, k)
        self.ret_ready = []
        mix(self.retention(l, f), side, 16, 12)
        drain(side)
        side = self.branch(l, 1, self.ret_ready)
        self.prepare_rwkv(l)
        mix(self.rwkv(l), side, 20, 9)
        if l + 1 < DEPTH:
            side = itertools.chain(side, self.modulation(l + 1))
        side = itertools.chain(side, self.last_gates(l))
        mix(self.chunks(l), side, 115, 20)
        drain(side)
        self.pg = self.all4
        f = self.fence()
        self.load_x(A["x"][0] if l == 0 else A["xd"], f, self.k_xd)
        k = self.rwkv_out(l)
        self.gates(l, f)
        drain(self.branch(l, 2, k))
        self.w_out(l)

    def silu(self, out, bank, tok, *free):
        t1 = self.act(out, bank.t[:, :], ACT.Sigmoid, tok, *free)
        t2 = self.vtt(out, bank.t[:, :], out, ALU.mult, t1, tok)
        bank.done(t1, t2)
        return t2

    def pool(self, l, f):
        ready = []
        o_free = f
        for g, w in enumerate(POOLW):
            (bank, t), = self.proj(g * 128)
            s = self.pt[:, 0:512], self.pt[:, 512:1024]
            u = self.pt[:, 1024:1536]
            t = self.S(lambda e, u=u, b=bank: e.copy(u, b.t[:, :]), t, f)
            bank.done(t)
            src, n = u, 1
            i = 0
            while n < w:
                dst = s[i]
                self.vtt(dst[:, n:512], src[:, n:512], src[:, 0:512 - n], ALU.add, t, f)
                self.V(lambda e, dst=dst, src=src, n=n: e.tensor_copy(dst[:, 0:n], src[:, 0:n]))
                src, n, i = dst, 2 * n, 1 - i
            dd = s[i]
            self.vtt(dd, src, self.invcnt[:, g * 512:(g + 1) * 512], ALU.mult, self.k_ic)
            t = self.vtt(dd, dd, u, ALU.subtract)
            pb = self.ps.take()
            tp = self.PE(lambda e, pb=pb, dd=dd, g=g: e.matmul(pb.t[:, :], self.poolw[:, g * 128:(g + 1) * 128], dd,
                                                              start=True, stop=True), t, self.k_pw, pb.free)
            self.V.wait(tp)
            (bank, t), = self.proj(512 + g * 128)
            sg = self.pt[:, 1536:2048]
            self.silu(sg, bank, t, f)
            t = self.stt(sg, pb.t[:, :], self.col(("pool_scale", l), g), sg, ALU.mult, ALU.mult, tp, self.k_cols)
            pb.done(t)
            ready += self.split(sg, self.ph[:, g * 512:(g + 1) * 512], self.pl[:, g * 512:(g + 1) * 512], t, o_free)
            self.S.wait(ready[-1])
            f = []
        return ready

    def last_gates(self, l):
        f = [self.PE.last()]
        for m in range(8):
            (bank, t), = self.proj(5248 + 2048 + m * 128, rota=self.side2)
            yield
            t = self.act(self.sg2[:, m * 512:(m + 1) * 512], bank.t[:, :], ACT.Sigmoid, t, f)
            bank.done(t)
            self.k_sg2 = t

    def branch(self, l, n, ready):
        f = self.fence() if n != 1 else []
        oh, ol = ((self.ph, self.pl), (self.oh, self.ol), (self.o2h, self.o2l))[n]
        rota = self.side2 if n < 2 else self.all4
        self.k_mrg = []
        for m2 in range(4):
            sg = []
            for i in range(2):
                m = 2 * m2 + i
                if n == 2:
                    sg.append((self.sg2[:, m * 512:(m + 1) * 512], self.k_sg2, None))
                    continue
                (bank, t), = self.proj(5248 + n * 1024 + m * 128, rota=rota)
                yield
                tm = self.tmp.take()
                t = self.act(tm.t[:, :], bank.t[:, :], ACT.Sigmoid, t, tm.free)
                bank.done(t)
                sg.append((tm.t[:, :], t, tm))
            ys = self.gemm_t("w_branch", (l, n), 256 * m2, lambda k: oh[:, k * 512:(k + 1) * 512],
                             lambda k: ol[:, k * 512:(k + 1) * 512], ready, nk=4, groups=2, rota=rota)
            yield
            for i, (bank, t) in enumerate(ys):
                m = 2 * m2 + i
                s, t1, tm = sg[i]
                acc = self.mrg[:, m * 512:(m + 1) * 512]
                t = self.vtt(acc if n == 0 else s, s, bank.t[:, :], ALU.mult, t, t1, f)
                bank.done(t)
                if n:
                    t = self.vtt(acc, acc, s, ALU.add)
                if tm:
                    tm.done(t)
                if n == 2:
                    self.k_mrg += self.split(acc, self.mh[:, m * 512:(m + 1) * 512], self.ml[:, m * 512:(m + 1) * 512], t, f)

    def rope(self, src, dst, sw, cos, sin, w, *tokens):
        t = None
        for p in range(0, 128, 2 * w):
            for a, b in ((p, p + w), (p + w, p)):
                t = self.G(lambda e, a=a, b=b: e.tensor_copy(sw[a:a + w, :], src[b:b + w, :]), *tokens)
        self.vtt(dst, src, cos, ALU.mult, t, *tokens)
        self.vtt(sw, sw, sin, ALU.mult, t)
        return self.vtt(dst, dst, sw, ALU.add)

    def retention(self, l, f):
        vb = self.gemm_n("w_in", (l,), [0, 256, 512, 768], 2048, self.h_lhs, self.l_lhs, self.h_ready, self.ps)
        kv = []
        for t, (bank, tok) in enumerate(vb):
            kv.append(self.S(lambda e, t=t, bank=bank: e.copy(self.vret[:, t * 512:(t + 1) * 512], bank.t[:, :]), tok, f))
            bank.done(kv[-1])
        yield
        ready = self.ret_ready
        pfree, nfree = f, f
        for s in self.qk.slots:
            s.done(*f)
        for h in range(4):
            rot = []
            for base in (1024, 1536):
                (bank, t), = self.proj(base + h * 128)
                s = self.qk.take()
                src, dst, sw = s.t[:, 0:512], s.t[:, 512:1024], s.t[:, 1024:1536]
                t = self.S(lambda e, src=src, bank=bank: e.copy(src, bank.t[:, :]), t, s.free)
                bank.done(t)
                rot.append((s, dst, self.rope(src, dst, sw, self.cosr[:, :], self.sinr[:, :], 64, t, s.free, self.k_rot)))
                yield
            (bank, tg), = self.proj(2560 + h * 128)
            self.silu(self.sgr[:, :], bank, tg, f)
            yield
            (sq, q, tq), (sk, k, tk) = rot
            tp = []
            for j in range(4):
                pb = self.ps.take()
                n = 512 - 128 * j
                t = self.PE(lambda e, pb=pb, j=j, n=n, q=q, k=k: e.matmul(pb.t[:, 0:n], k[:, j * 128:(j + 1) * 128], q[:, j * 128:512],
                                                                          start=True, stop=True), pb.free, tq, tk)
                t = self.vtt(self.pt[:, j * 512:j * 512 + n], pb.t[:, 0:n], self.decay[:, h * 512:h * 512 + n], ALU.mult,
                             t, pfree, self.k_dc)
                pb.done(t)
                tp.append(t)
            sq.done(t)
            sk.done(t)
            ob = self.ps.take()
            for i in range(4):
                for j in range(i + 1):
                    t = self.PE(lambda e, i=i, j=j, ob=ob, h=h: e.matmul(
                        ob.t[:, i * 128:(i + 1) * 128], self.pt[:, j * 512 + (i - j) * 128:j * 512 + (i - j + 1) * 128],
                        self.vret[:, j * 512 + h * 128:j * 512 + (h + 1) * 128], start=j == 0, stop=j == i, skip_group_check=True),
                        ob.free, tp[j], kv[j], signal=i == j)
            pfree = [t]
            yield
            st = self.stat
            for i in range(4):
                self.V(lambda e, i=i, ob=ob: e.bn_stats(st[:, 16 + 6 * i:22 + 6 * i], ob.t[:, i * 128:(i + 1) * 128]), t)
                ts = self.V(lambda e, i=i: e.bn_aggr(st[:, 2 * i:2 * i + 2], st[:, 16 + 6 * i:22 + 6 * i]))
            r = self.rstd(st[:, 8:12], st[:, 0:8].rearrange("p (i two) -> p i two", two=2)[:, :, 1], 1.0, 1e-5, ts)
            for i in range(4):
                tn = self.vts(self.onat[:, i * 128:(i + 1) * 128], ob.t[:, i * 128:(i + 1) * 128], st[:, 2 * i:2 * i + 1],
                              st[:, 8 + i:9 + i], ALU.subtract, ALU.mult, r, nfree)
            ob.done(tn)
            tb = self.ps.take()
            t = self.transpose4([self.onat[:, i * 128:(i + 1) * 128] for i in range(4)], tb, tn, self.k_id)
            nfree = [t]
            yield
            t = self.stt(self.sgr[:, :], tb.t[:, :], self.col(("ret_g", l), h), self.sgr[:, :], ALU.mult, ALU.mult, t)
            tb.done(t)
            ready += self.split(self.sgr[:, :], self.oh[:, h * 512:(h + 1) * 512], self.ol[:, h * 512:(h + 1) * 512], t, f)
            self.S.wait(ready[-1])
            self.V.wait(ready[-2])

    def shifted(self, bank, tok, mu, out, f):
        t = self.S(lambda e, bank=bank: e.copy(self.PP[:, 1:513], bank.t[:, :]), tok, self.pp_free)
        bank.done(t)
        self.vtt(self.RT[7][:, :], self.PP[:, 0:512], self.PP[:, 1:513], ALU.subtract, t, f)
        t = self.stt(out, self.RT[7][:, :], mu, self.PP[:, 1:513], ALU.mult, ALU.add)
        self.pp_free = [t]
        return t

    def prepare_rwkv(self, l):
        A = self.A
        self.rw_f = f = self.fence()
        self.k_w2 = [self.load(self.w2a2[0:64, :], A["rwkv_w2"][l], f), self.load(self.w2a2[64:128, :], A["rwkv_a2"][l], f)]
        self.k_rs = self.load(self.reset[:, :], A["reset"], f)
        self.k_gm = [self.load(self.gmask[:, :], A["gmask"], f), self.load(self.m1[:, :], A["m1"], f),
                self.load(self.lmask[:, :], A["lmask"], f)]
        self.pp_free = [self.V(lambda e: e.memset(self.PP[:, 0:1], 0.0), f)]

    def rwkv(self, l):
        f, k_rs = self.rw_f, self.k_rs
        pieces = tuple(x for k in range(8) for x in ((128 * k, 3584, 64), (128 * k, 4672, 64)))
        (bank, t), = self.proj(0, pieces=pieces)
        t = self.shifted(bank, t, self.col(("mu_wa", l)), self.wa[:, :], f)
        k_wa = self.act(self.wa[0:64, :], self.wa[0:64, :], ACT.Tanh, t)
        RT = [x[:, :] for x in self.RT]
        yield
        for p in range(4):
            mu = lambda n: self.col((n, l), p)
            pb = self.ps.take()
            t = self.PE(lambda e, pb=pb, p=p: e.matmul(pb.t[:, :], self.w2a2[0:64, p * 128:(p + 1) * 128], self.wa[0:64, :],
                                                       start=True, stop=True), pb.free, k_wa, self.k_w2)
            sg, cum = RT[0], RT[1]
            t = self.act(sg, pb.t[:, :], ACT.Sigmoid, t, f, bias=mu("w0"))
            pb.done(t)
            self.V(lambda e: e.tensor_tensor_scan(cum, self.reset[:, :], sg, 0.0, ALU.mult, ALU.add), t, k_rs)
            c4 = cum.rearrange("p (c n) -> p c n", c=4)
            e4 = self.em[:, 16 * p:16 * p + 16]
            self.V(lambda e, e4=e4: e.tensor_copy(e4[:, 12:16], c4[:, :, 63]))
            tm = self.vtt(e4[:, 8:12], c4[:, :, 127], e4[:, 12:16], ALU.subtract)
            tm = self.V(lambda e, e4=e4: e.tensor_copy(e4[:, 4:8], c4[:, :, 127]))
            self.vtt(c4, c4, e4[:, 12:16].unsqueeze(2).broadcast_to([128, 4, 128]), ALU.subtract)
            td = self.vtt(sg, cum, sg, ALU.subtract)
            te = self.act(e4[:, 0:4], e4[:, 12:16], ACT.Exp, td, scale=-KAPPA)
            te = self.act(e4[:, 4:12], e4[:, 4:12], ACT.Exp, scale=-KAPPA)
            E1, E2, E3 = RT[2], RT[1], RT[0]
            self.act(E1, cum, ACT.Exp, scale=-KAPPA)
            self.act(E3, sg, ACT.Exp, scale=-KAPPA)
            te = self.act(E2, cum, ACT.Exp, scale=KAPPA)
            (bank, t), = self.proj(3072 + p * 128)
            yield
            r = RT[3]
            self.shifted(bank, t, mu("mu_r"), r, f)
            AR = self.AR[:, p * 1024:(p + 1) * 1024]
            self.vtt(AR[:, 512:1024], r, E1, ALU.mult, te)
            (bank, t), = self.proj(3648 + p * 128)
            yield
            k = RT[4]
            tk = self.shifted(bank, t, mu("mu_k"), k, f)
            pb = self.ps.take()
            t = self.PE(lambda e, pb=pb, p=p: e.matmul(pb.t[:, :], self.w2a2[64:128, p * 128:(p + 1) * 128], self.wa[64:128, :],
                                                       start=True, stop=True), pb.free, k_wa, self.k_w2)
            a = RT[5]
            ta = self.act(a, pb.t[:, :], ACT.Sigmoid, t, bias=mu("a0"))
            pb.done(ta)
            q = RT[6]
            t = self.act(q, k, ACT.Square, tk, scale=mu("k_k"))
            pb = self.ps.take()
            t = self.PE(lambda e, pb=pb: e.matmul(pb.t[:, :], self.blk64[:, :], q, start=True, stop=True), pb.free, t, *self.k_misc)
            yield
            t = self.vts(q, pb.t[:, :], 1e-24, None, ALU.max, None, t)
            pb.done(t)
            t = self.act(q, q, ACT.Sqrt, t)
            self.V(lambda e: e.reciprocal(q, q), t)
            kk = q
            self.stt(kk, k, mu("k_k"), q, ALU.mult, ALU.mult)
            self.stt(AR[:, 0:512], kk, -1.0, E3, ALU.mult, ALU.mult)
            self.vtt(kk, kk, a, ALU.mult, ta)
            self.vtt(self.BH[:, p * 512:(p + 1) * 512], kk, E2, ALU.mult)
            self.vts(a, a, 1.0, mu("k_a"), ALU.subtract, ALU.mult)
            self.stt(k, a, 1.0, k, ALU.add, ALU.mult)
            self.vtt(self.KH[:, p * 512:(p + 1) * 512], k, E2, ALU.mult)
            t = self.stt(r, r, mu("r_k"), k, ALU.mult, ALU.mult)
            pb = self.ps.take()
            tb = self.PE(lambda e, pb=pb: e.matmul(pb.t[:, :], self.blk64[:, :], r, start=True, stop=True), pb.free, t)
            (bank, t), = self.proj(4160 + p * 128)
            yield
            v = RT[5]
            tv = self.shifted(bank, t, mu("mu_v"), v, f)
            b2 = self.ps.take()
            t2 = self.transpose4([v[:, c * 128:(c + 1) * 128] for c in range(4)], b2, tv, self.k_id)
            vn = self.VN[:, :].rearrange("p (c q n) -> p c q n", c=4, q=4)[:, :, p, :]
            t3 = self.S(lambda e, b2=b2, vn=vn: e.copy(vn, b2.t[:, :].rearrange("p (c n) -> p c n", c=4)), t2)
            b2.done(t3)
            t = self.vtt(self.VB[:, p * 512:(p + 1) * 512], pb.t[:, :], v, ALU.mult, tb)
            pb.done(t)
            self.S.wait(t)
            self.V.wait(t3, te, t2)

    def rwkv_out(self, l):
        ready = []
        f = self.fence()
        for p in range(4):
            (bank, t), = self.proj(4736 + p * 128)
            tm = self.tmp.take()
            y = self.KH[:, p * 512:(p + 1) * 512]
            self.silu(tm.t[:, :], bank, t, tm.free)
            self.vtt(y, y, self.VB[:, p * 512:(p + 1) * 512], ALU.add, f)
            t = self.vtt(y, y, tm.t[:, :], ALU.mult)
            tm.done(t)
            ready += self.split(y, self.o2h[:, p * 512:(p + 1) * 512], self.o2l[:, p * 512:(p + 1) * 512], t, f)
        return ready

    def chunks(self, l):
        f = self.fence()
        for z in self.sets:
            z["free"] = f
        stream = lambda g: itertools.chain.from_iterable(self.chunk(l, c, g) for c in range(4))
        yield from abreast(stream(0), itertools.chain(range(13), stream(1)))

    def chunk(self, l, c, g):
        cs = slice(c * 128, (c + 1) * 128)
        heads = [(4 * g + i, (4 * g + i) // 2, 64 * (i % 2)) for i in range(4)]
        z = self.sets[g]
        free = z["free"]
        G4, X, U, Y = z["G4"], z["X"], z["U"], z["Y"]
        W4, SA, YQ = Y[:, 0:256], Y[:, 256:512], X[:, 0:256]
        v4 = lambda x: x[:, :].rearrange("p (h n) -> p h n", h=4)
        for i, (h, p, q) in enumerate(heads):
            bank = self.ps.take()
            ar = self.AR[q:q + 64, p * 1024:(p + 1) * 1024].rearrange("p (two n) -> p two n", two=2)[:, :, cs]
            for j, KB in enumerate((self.BH, self.KH)):
                o = bank.t[:, 256 * j:256 * j + 256].rearrange("p (two n) -> p two n", two=2)
                t = self.PE(lambda e, o=o, KB=KB, ar=ar, p=p, q=q: e.matmul(
                    o, KB[q:q + 64, p * 512 + c * 128:p * 512 + (c + 1) * 128], ar, start=True, stop=True, skip_group_check=True),
                    bank.free, free, signal=j == 1)
            t = self.vtt(G4[:, i * 512:(i + 1) * 512], bank.t[:, :], self.gmask[:, :], ALU.mult, t, free, self.k_gm)
            bank.done(t)
        yield
        kn = []
        for KB, KN in ((self.BH, z["BN"]), (self.KH, z["KN"])):
            bank = self.ps.take()
            tt = self.transpose4([KB[:, p * 512 + c * 128:p * 512 + (c + 1) * 128] for p in (2 * g, 2 * g + 1)], bank, self.k_id)
            kn.append(self.S(lambda e, KN=KN, bank=bank: e.copy(KN[:, :], bank.t[:, 0:256]), tt, free))
            bank.done(kn[-1])
        ga = G4[:, :].rearrange("p (h n) -> p h n", h=4)[:, :, 0:128]
        self.vtt(v4(U), ga, self.m1[:, :].unsqueeze(1).broadcast_to([128, 4, 128]), ALU.mult)
        tu = self.vtt(v4(U), v4(U), self.ident[:, :].unsqueeze(1).broadcast_to([128, 4, 128]), ALU.add, self.k_id)
        yield

        def four(bank, lhs, rhs, *tokens):
            for i in range(4):
                t = self.PE(lambda e, i=i: e.matmul(bank.t[:, i * 128:(i + 1) * 128], lhs(i), rhs(i), start=True, stop=True,
                                                    skip_group_check=True), bank.free, *tokens, signal=i == 3)
            return t

        blk = lambda x: (lambda i: x[:, i * 128:(i + 1) * 128])
        for lv, n in enumerate((2, 4, 8, 16, 32, 64)):
            bank = self.ps.take()
            t = self.transpose4([U[:, i * 128:(i + 1) * 128] for i in range(4)], bank, tu)
            tx = self.S(lambda e, bank=bank: e.copy(X[:, :], bank.t[:, :]), t, free)
            bank.done(tx)
            yield
            yb = self.ps.take()
            t = four(yb, lambda i: G4[:, i * 512:i * 512 + 128], blk(X), tx, tu)
            ty = self.S(lambda e, yb=yb: e.copy(Y[:, :], yb.t[:, :]), t)
            yb.done(ty)
            yield
            wb = self.ps.take()
            tw = four(wb, blk(Y), blk(U), ty)
            if n < 32:
                m = self.lmask[:, lv * 128:(lv + 1) * 128].unsqueeze(1).broadcast_to([128, 4, 128])
                tu = self.V(lambda e, m=m, wb=wb: e.copy_predicated(v4(U), m, v4(wb.t)), tw)
            else:
                for s in range(0, 128, 2 * n):
                    tu = self.V(lambda e, wb=wb, s=s, n=n: e.tensor_copy(
                        v4(U)[s:s + n, :, s + n:s + 2 * n], v4(wb.t)[s:s + n, :, s + n:s + 2 * n]), tw)
            wb.done(tu)
            yield
        em = self.em[:, 32 * g:32 * g + 32].rearrange("p (t j c) -> p t j c", t=2, j=4)
        bc = lambda j: em[:, :, j, c].unsqueeze(2).broadcast_to([128, 2, 64])
        st = self.st[:, g * 128:(g + 1) * 128].rearrange("p (t v) -> p t v", t=2)
        S0 = z["SP"]
        spt = S0[:, :].rearrange("p (t j v) -> p t j v", t=2, j=2)
        ts = None
        if c == 0:
            self.V(lambda e: e.memset(S0[:, :], 0.0), free)
        else:
            for j in range(2):
                q = slice(64 * j, 64 * j + 64)
                ts = self.vtt(spt[q, :, j, :], st[q, :, :], bc(0)[q, :, :], ALU.mult, free)
        vn = lambda h: self.VN[:, c * 512 + h * 64:c * 512 + (h + 1) * 64]

        def from_state(bank, j):
            for t in range(2):
                a = self.AR[:, (2 * g + t) * 1024 + j * 512 + c * 128:(2 * g + t) * 1024 + j * 512 + (c + 1) * 128]
                o = bank.t[:, t * 128:(t + 1) * 128]
                self.PE(lambda e, o=o, a=a, t=t: e.matmul(o, a, S0[:, t * 128:(t + 1) * 128], start=t == 0, stop=False,
                                                          skip_group_check=True), ts, bank.free, signal=False)

        wb = self.ps.take()
        if c:
            from_state(wb, 0)
        for i, (h, p, q) in enumerate(heads):
            o = wb.t[:, i * 64:(i + 1) * 64]
            t = self.PE(lambda e, o=o, h=h, i=i: e.matmul(o, G4[:, i * 512 + 256:i * 512 + 384], vn(h), start=c == 0, stop=True,
                                                          skip_group_check=True), wb.free, signal=i == 3)
        t = self.S(lambda e, wb=wb: e.copy(W4, wb.t[:, 0:256]), t)
        wb.done(t)
        yield
        sb = self.ps.take()
        for i, (h, p, q) in enumerate(heads):
            t2 = self.PE(lambda e, i=i, sb=sb: e.matmul(sb.t[:, i * 64:(i + 1) * 64], U[:, i * 128:(i + 1) * 128],
                                                        W4[:, i * 64:(i + 1) * 64], start=True, stop=True, skip_group_check=True),
                         t, tu, sb.free, signal=i == 3)
        tsa = self.S(lambda e, sb=sb: e.copy(SA, sb.t[:, 0:256]), t2)
        sb.done(tsa)
        yield
        if c < 3:
            sb = self.ps.take()
            for i, (h, p, q) in enumerate(heads):
                o = sb.t[q:q + 64, (p - 2 * g) * 64:(p - 2 * g) * 64 + 64]
                for j, (KN, R) in enumerate(((z["BN"], SA[:, i * 64:(i + 1) * 64]), (z["KN"], vn(h)))):
                    t = self.PE(lambda e, o=o, KN=KN, R=R, i=i, j=j: e.matmul(o, KN[:, i * 64:(i + 1) * 64], R, start=j == 0, stop=j == 1,
                                                                              skip_group_check=True), kn, tsa, sb.free, signal=i == 3 and j == 1)
            sv = sb.t[:, 0:128].rearrange("p (t v) -> p t v", t=2)
            if c:
                sq = YQ[:, 0:128].rearrange("p (t v) -> p t v", t=2)
                self.vtt(st, st, bc(1), ALU.mult)
                t = self.vtt(sq, sv, bc(2), ALU.mult, t)
                self.vtt(st, st, sq, ALU.add)
            else:
                t = self.vtt(st, sv, bc(2), ALU.mult, t, free)
            sb.done(t)
        yb = self.ps.take()
        if c:
            from_state(yb, 1)
        for i, (h, p, q) in enumerate(heads):
            o = yb.t[:, i * 64:(i + 1) * 64]
            self.PE(lambda e, o=o, i=i: e.matmul(o, G4[:, i * 512 + 128:i * 512 + 256], SA[:, i * 64:(i + 1) * 64],
                                                 start=c == 0, stop=False, skip_group_check=True), tsa, yb.free, signal=False)
            ty = self.PE(lambda e, o=o, h=h, i=i: e.matmul(o, G4[:, i * 512 + 384:i * 512 + 512], vn(h), start=False, stop=True,
                                                           skip_group_check=True), signal=i == 3)
        y4 = yb.t[:, 0:256].rearrange("p (h n) -> p h n", h=4)
        n4, q4 = z["YN"][:, :].rearrange("p (h n) -> p h n", h=4), YQ.rearrange("p (h n) -> p h n", h=4)
        hs = z["hs"]
        self.V(lambda e: e.tensor_reduce(hs[:, 0:4], y4, AX.X, ALU.add), ty)
        self.vts(hs[:, 0:4], hs[:, 0:4], 1.0 / 64, None, ALU.mult, None)
        t = self.vtt(n4, y4, hs[:, 0:4].unsqueeze(2).broadcast_to([128, 4, 64]), ALU.subtract, free)
        yb.done(t)
        self.vtt(q4, n4, n4, ALU.mult)
        t = self.V(lambda e: e.tensor_reduce(hs[:, 4:8], q4, AX.X, ALU.add))
        r = self.rstd(hs[:, 8:12], hs[:, 4:8], 1.0 / 64, 64e-5, t)
        yield
        t = self.vtt(n4, n4, hs[:, 8:12].unsqueeze(2).broadcast_to([128, 4, 64]), ALU.mult, r)
        bank = self.ps.take()
        t = self.transpose4([z["YN"][:, 0:128], z["YN"][:, 128:256]], bank, t)
        z["free"] = [t]
        for j in range(2):
            p = 2 * g + j
            tt = self.act(self.KH[:, p * 512 + c * 128:p * 512 + (c + 1) * 128], bank.t[:, j * 128:(j + 1) * 128], ACT.Identity, t,
                          bias=self.col(("ln_b", l), p), scale=self.col(("ln_w", l), p))
        bank.done(tt)

    def w_out(self, l):
        xr = self.x_ready
        self.x_ready = [[] for _ in range(4)]
        for half in range(2):
            rota = (self.all4, self.ps)[half]
            out = self.gemm_n("w_out", (l,), [0, 256, 512, 768], 512 * half,
                              lambda k, t: self.mh[:, k * 512 + t * 128:k * 512 + (t + 1) * 128],
                              lambda k, t: self.ml[:, k * 512 + t * 128:k * 512 + (t + 1) * 128], self.k_mrg, rota)
            for t, (bank, tok) in enumerate(out):
                tm = self.tmp.take()
                a = self.vtt(tm.t[:, :], bank.t[:, :], self.gate[:, half * 512:(half + 1) * 512], ALU.mult, tok, tm.free, self.k_gate)
                bank.done(a)
                x = self.xn[:, t * 1024 + half * 512:t * 1024 + (half + 1) * 512]
                a = self.vtt(x, x, tm.t[:, :], ALU.add, xr[t])
                tm.done(a)
                self.x_ready[t].append(a)
        if l + 1 < DEPTH:
            self.k_xd = [self.load(self.A["xd"][t * 128:(t + 1) * 128, :], self.x_tile(t), *self.x_ready[t]) for t in range(4)]

    def rows(self, g, b):
        f = self.fence()
        k = [self.load(self.bc[:, 0:1024], g.partition_broadcast(128), f)]
        if b is not None:
            k.append(self.load(self.bc[:, 1024:2048], b.partition_broadcast(128), f))
        return k

    def to_hT_tile(self, t, *tokens):
        k = []
        for d4 in range(2):
            bank = self.ps.take()
            a = self.transpose4([self.xn[:, t * 1024 + d * 128:t * 1024 + (d + 1) * 128] for d in range(4 * d4, 4 * d4 + 4)],
                                bank, self.k_id, *tokens)
            o = lambda x: x[:, d4 * 2048:(d4 + 1) * 2048].rearrange("p (d n) -> p d n", d=4)[:, :, t * 128:(t + 1) * 128]
            s = self.split(bank.t[:, :].rearrange("p (d n) -> p d n", d=4), o(self.hh), o(self.hl), a, self.h_free)
            bank.done(*s)
            k += s
        self.h_ready += k
        return a

    def final_norm(self):
        kb = self.rows(self.A["final_g"], None)
        self.h_free, self.h_ready = self.fence(), []
        for t in range(4):
            xt, ss, r = self.x_tile(t), self.stat[:, t:t + 1], self.stat[:, 4 + t:5 + t]
            s = self.V(lambda e, xt=xt, ss=ss: e.tensor_tensor_reduce(self.bc[:, 1024:2048], xt, xt, 1.0, 0.0, ALU.mult, ALU.add, ss),
                       self.x_ready[t], self.h_free)
            k = self.rstd(r, ss, 1.0 / D, 1e-6, s)
            k = self.stt(xt, xt, r, self.bc[:, 0:1024], ALU.mult, ALU.mult, k, kb)
            self.to_hT_tile(t, k)
            self.x_ready[t] = [k]

    def layer_norm(self, l, name, eps, halves, out=False):
        A = self.A
        st = self.stat
        late = None
        for t, (xt, k) in enumerate(halves):
            if late:
                self.to_hT_tile(*late)
            else:
                self.h_free, self.h_ready = self.h_last, []
            for hf in range(2):
                s = self.V(lambda e, xt=xt, hf=hf: e.bn_stats(st[:, 16 + 6 * hf:22 + 6 * hf], xt[:, hf * 512:(hf + 1) * 512]), k)
            s = self.V(lambda e, t=t: e.bn_aggr(st[:, 4 * t:4 * t + 2], st[:, 16:28]))
            r = self.rstd(st[:, 4 * t + 2:4 * t + 3], st[:, 4 * t + 1:4 * t + 2], 1.0, eps, s)
            self.stt(xt, xt, st[:, 4 * t:4 * t + 1], self.bc[:, 0:1024], ALU.subtract, ALU.mult, self.k_rows)
            k = self.stt(xt, xt, st[:, 4 * t + 2:4 * t + 3], self.bc[:, 1024:2048], ALU.mult, ALU.add, r)
            self.x_ready[t] = [k]
            if not out:
                late = (t, k)
        if late:
            self.to_hT_tile(*late)

    def ffn(self, l, name, ln):
        f = self.fence()
        ready = []
        for m in range(NFF):
            (gb, tg), = self.gemm_t(name + "_w_gu_2", (l,), m * 128, self.h_rhs, self.l_rhs, self.h_ready)
            (ub, tu), = self.gemm_t(name + "_w_gu_2", (l,), FF + m * 128, self.h_rhs, self.l_rhs, self.h_ready)
            tm = self.tmp.take()
            t = self.act(tm.t[:, :], gb.t[:, :], ACT.Silu, tg, tm.free)
            gb.done(t)
            t = self.vtt(tm.t[:, :], tm.t[:, :], ub.t[:, :], ALU.mult, t, tu)
            ub.done(t)
            k = self.split(tm.t[:, :], self.fh[:, m * 512:(m + 1) * 512], self.fl[:, m * 512:(m + 1) * 512], t, f)
            tm.done(*k)
            ready += k
        return self.project(name + "_w_down_2", l, [256 * i for i in range(11)],
                            self.fh, self.fl, lambda k: ready[2 * k:2 * k + 2], 2 * ALPHA, ln)

    def project(self, name, l, k0s, ah, al, ready, s, ln):
        self.h_last = [self.PE.last()]
        self.k_rows = self.rows(self.A[ln + "_g_2"][l], self.A[ln + "_b_2"][l])
        xr = [[] for _ in range(4)]
        for half in range(2):
            rota = (self.ps, self.all4)[half]
            out = self.gemm_tiles(name, (l,), k0s, 512 * half, lambda k, t: ah[:, k * 512 + t * 128:k * 512 + (t + 1) * 128],
                              lambda k, t: al[:, k * 512 + t * 128:k * 512 + (t + 1) * 128], ready, rota, late=(1, 3)[half])
            for t, (bank, tok) in enumerate(out):
                x = self.xn[:, t * 1024 + half * 512:t * 1024 + (half + 1) * 512]
                a = self.stt(x, x, s, bank.t[:, :], ALU.mult, ALU.add, tok, self.x_ready[t])
                bank.done(a)
                xr[t].append(a)
                if half:
                    yield self.x_tile(t), xr[t]

    def layer_b(self, l):
        self.layer_norm(l, "ln1", 4e-5, self.ffn(l, "ffn1", "ln1"))
        self.layer_norm(l, "ln2", 1e-5, self.mixer(l))
        self.layer_norm(l, "ln3", 4e-5, self.ffn(l, "ffn2", "ln3"), out=l == DEPTH - 1)

    def mixer(self, l):
        A = self.A
        f = self.fence()
        k_c = [self.load(self.rcos[:, :], A["rcos"], f), self.load(self.rsin[:, :], A["rsin"], f),
               self.load(self.amask[:, :], A["amask"], f), self.load(self.mean256[:, :], A["mean256"], f),
               self.load(self.sink[:, :], A["attn_sink_2"][l].partition_broadcast(128), f)]
        proj = lambda col, rota: self.gemm_t("w_in_2", (l,), col, self.h_rhs, self.l_rhs, self.h_ready, rota=rota)[0]
        z = [x[:, :] for x in self.t3]
        half = lambda x, j: x[:, j * 512:(j + 1) * 512]
        cp = self.ccp[:, :].rearrange("p (j n) -> p j n", j=2)
        self.V(lambda e: e.memset(self.ccp[:, :], 0.0), f)
        self.V(lambda e: e.memset(self.scp[:, :], 0.0), f)
        ready = [None] * 8
        zt = None
        for j in range(2):
            ba, ta = proj(1536 + j * 128, self.all4)
            bg, tg = proj(1792 + j * 128, self.all4)
            t = self.act(z[0], bg.t[:, :], ACT.Sigmoid, tg, f, zt)
            bg.done(t)
            zt = t = self.vtt(cp[:, j, 15:527], ba.t[:, :], z[0], ALU.mult, t, ta)
            ba.done(t)
        side = abreast(self.wide_conv(l, cp, half, ready, k_c, f), itertools.chain(range(3), self.short_conv(l, proj, half, ready, zt, f)))
        rot, swt = [], None
        for n in range(5):
            b_, t = proj(768 + n * 128, self.main2)
            r = self.rq.take()
            dst = half(self.qT, n) if n < 4 else self.kT[:, :]
            t = self.S(lambda e, b_=b_, r=r: e.copy(r.t[:, 0:512], b_.t[:, :]), t, r.free, f)
            b_.done(t)
            rot.append(self.rope(r.t[:, 0:512], dst, r.t[:, 512:1024], self.rcos[:, :], self.rsin[:, :], 32, t, k_c, f, r.free))
            r.done(rot[-1])
            next(side, None)
        self.G(lambda e: e.tensor_copy(self.kS[0:64, :], self.kT[64:128, :]), rot, f)
        rot.append(self.G(lambda e: e.tensor_copy(self.kS[64:128, :], self.kT[0:64, :])))
        wh, wl, tok, n = self.unit("w_in_2", (l,), t_pieces(1408))
        vk = self.ps.take()
        for t in range(4):
            for k in range(8):
                tv = self.mm3(vk.t[:, t * 128:(t + 1) * 128], self.h_lhs(k, t), self.l_lhs(k, t), wh[:, k * 128:(k + 1) * 128],
                              wl[:, k * 128:(k + 1) * 128], k == 0, k == 7, tok, vk.free, self.h_ready)
        self.used[n] = tv
        kv = self.S(lambda e: e.copy(self.v2[:, :], vk.t[:, :]), tv, f)
        vk.done(kv)
        mix(self.attention(rot, kv, ready, k_c, f), side, 17, 17)
        drain(side)
        yield from self.project("w_out_2", l, [0, 256, 512, 768], self.xh8, self.xl8, lambda k: ready[k], ALPHA, "ln2")

    def short_conv(self, l, proj, half, ready, zt, f):
        sp = self.scp[:, :].rearrange("p (j n) -> p j n", j=2)
        z = [x[:, :] for x in self.t3]
        for j in range(2):
            b_, t = proj(256 + j * 128, self.side2)
            yield
            t = self.S(lambda e, b_=b_: e.copy(z[0], b_.t[:, :]), t, zt)
            b_.done(t)
            b_, th = proj(512 + j * 128, self.side2)
            yield
            zt = self.vtt(sp[:, j, 1:513], z[0], b_.t[:, :], ALU.mult, t, th)
            b_.done(zt)
            self.vts(z[1], sp[:, j, 0:512], self.col(("sc", l, 0), j), None, ALU.mult, None)
            for w in (1, 2):
                self.stt(z[1], sp[:, j, w:w + 512], self.col(("sc", l, w), j), z[1], ALU.mult, ALU.add)
            b_, tb = proj(j * 128, self.side2)
            yield
            t = self.vtt(z[1], z[1], b_.t[:, :], ALU.mult, tb)
            b_.done(t)
            k = self.split(z[1], half(self.xh8, j), half(self.xl8, j), t, f)
            self.V.wait(*k)
            ready[j] = k

    def wide_conv(self, l, cp, half, ready, k_c, f):
        for j in range(2):
            ac = half(self.acc, j)
            self.vts(ac, cp[:, j, 0:512], self.col(("cc", l, 0), j), self.col(("cc_b", l), j), ALU.mult, ALU.add, f)
            for w in range(1, 31):
                t = self.stt(ac, cp[:, j, w:w + 512], self.col(("cc", l, w), j), ac, ALU.mult, ALU.add)
                if w % 5 == 0:
                    yield
        z = self.zc
        mb = self.side2.take()
        for j in range(2):
            t2 = self.PE(lambda e, j=j: e.matmul(mb.t[:, :], self.mean256[:, :], half(self.acc, j), start=j == 0, stop=j == 1),
                         t, mb.free, k_c)
        for j in range(2):
            t = self.vtt(half(self.acc, j), half(self.acc, j), mb.t[:, :], ALU.subtract, t2)
        mb.done(t)
        t3 = self.act(z[:, :], self.acc[:, :], ACT.Square, t, f)
        yield
        vb = self.side2.take()
        for j in range(2):
            t4 = self.PE(lambda e, j=j: e.matmul(vb.t[:, :], self.mean256[:, :], half(z, j), start=j == 0, stop=j == 1), t3, vb.free)
        t = self.vts(z[:, 0:512], vb.t[:, :], 1e-5, None, ALU.add, None, t4)
        vb.done(t)
        t = self.act(z[:, 0:512], z[:, 0:512], ACT.Sqrt, t)
        yield
        self.V(lambda e: e.reciprocal(z[:, 0:512], z[:, 0:512]), t)
        for j in range(2):
            ac = half(self.acc, j)
            t = self.stt(ac, ac, self.col(("cc_lg", l), j), z[:, 0:512], ALU.mult, ALU.mult)
            t = self.act(ac, ac, ACT.Silu, t, bias=self.col(("cc_lb", l), j))
            ready[6 + j] = self.split(ac, half(self.xh8, 6 + j), half(self.xl8, 6 + j), t, f)

    def attention(self, rot, kv, ready, k_c, f):
        outs = {}
        last = None
        parts = []

        def scores(nb, kvh):
            k0, nk = max(nb - 1, 0), min(nb + 2, 4) - max(nb - 1, 0)
            mo = (k0 - nb + 1) * 128
            sm = self.sm.take()
            s = sm.t
            P = []
            for i in range(4):
                h = 4 * kvh + i
                p, q = h // 2, 64 * (h % 2)
                sb, pr = self.ps.take(), self.pr.take()
                kt = self.kT if q == 64 * kvh else self.kS
                t = self.PE(lambda e, sb=sb, p=p, q=q, kt=kt: e.matmul(
                    sb.t[:, 0:nk * 128], self.qT[q:q + 64, p * 512 + nb * 128:p * 512 + (nb + 1) * 128],
                    kt[q:q + 64, k0 * 128:(k0 + nk) * 128], start=True, stop=True), sb.free, rot)
                P.append(pr)
                t = self.V(lambda e, pr=pr, sb=sb, i=i: e.tensor_tensor_reduce(
                    pr.t[:, 0:nk * 128], sb.t[:, 0:nk * 128], self.amask[:, mo:mo + nk * 128], 1.0, -3e38, ALU.add, ALU.max,
                    s[:, i:i + 1]), t, pr.free, sm.free, k_c, f)
                sb.done(t)
            sk = self.sink[:, 4 * kvh:4 * kvh + 4]
            self.stt(s[:, 0:4], s[:, 0:4], 0.125, sk, ALU.mult, ALU.max)
            self.vts(s[:, 4:8], s[:, 0:4], -1.0, None, ALU.mult, None)
            t = self.vtt(s[:, 8:12], sk, s[:, 0:4], ALU.subtract)
            te = []
            for i in range(4):
                x = P[i].t[:, 0:nk * 128]
                te.append(self.S(lambda e, x=x, i=i: e.activation(x, x, ACT.Exp, bias=s[:, 4 + i:5 + i], scale=0.125,
                                                                  accum_out=s[:, 12 + i:13 + i]), t))
            t = self.act(s[:, 8:12], s[:, 8:12], ACT.Exp)
            self.vtt(s[:, 8:12], s[:, 8:12], s[:, 12:16], ALU.add, t)
            t = self.V(lambda e: e.reciprocal(s[:, 16:20], s[:, 8:12]))
            return nb, kvh, k0, nk, sm, P, te, t

        def values(nb, kvh, k0, nk, sm, P, te, td):
            ob = self.main2.take()
            for i in range(4):
                h = 4 * kvh + i
                tb, pT = self.ps.take(), self.prT.take()
                t = self.transpose4([P[i].t[:, j * 128:(j + 1) * 128] for j in range(nk)], tb, te[i], self.k_id)
                P[i].done(t)
                t = self.S(lambda e, pT=pT, tb=tb: e.copy(pT.t[:, 0:nk * 128], tb.t[:, 0:nk * 128]), t, pT.free)
                tb.done(t)
                for j in range(nk):
                    to = self.PE(lambda e, h=h, j=j, pT=pT: e.matmul(
                        ob.t[:, h * 64:(h + 1) * 64], pT.t[:, j * 128:(j + 1) * 128],
                        self.v2[:, (k0 + j) * 128 + kvh * 64:(k0 + j) * 128 + kvh * 64 + 64], start=j == 0, stop=j == nk - 1,
                        skip_group_check=True), t, kv, ob.free, signal=j == nk - 1)
                pT.done(to)
            ao = self.ao.take() if kvh == 0 else outs["ao"]
            outs["ao"] = ao
            o = slice(kvh * 256, kvh * 256 + 256)
            t = self.vtt(ao.t[:, o].rearrange("p (h n) -> p h n", h=4), ob.t[:, o].rearrange("p (h n) -> p h n", h=4),
                         sm.t[:, 16:20].unsqueeze(2).broadcast_to([128, 4, 64]), ALU.mult, to, ao.free)
            sm.done(t)
            ob.done(t)
            if kvh == 0:
                return
            tb = self.ps.take()
            t = self.transpose4([ao.t[:, i * 128:(i + 1) * 128] for i in range(4)], tb, t)
            ao.done(t)
            v8 = lambda x: x[:, 1024:3072].rearrange("p (j n) -> p j n", j=4)[:, :, nb * 128:(nb + 1) * 128]
            k = self.split(tb.t[:, :].rearrange("p (j n) -> p j n", j=4), v8(self.xh8), v8(self.xl8), t, f)
            tb.done(*k)
            parts.extend(k)

        for nb in range(4):
            for kvh in range(2):
                now = scores(nb, kvh)
                yield
                if last:
                    values(*last)
                    yield
                last = now
        values(*last)
        for j in range(2, 6):
            ready[j] = parts

    def finish(self):
        n = 0
        for t in range(4):
            self.SP.wait(*self.x_ready[t])
            x = self.x_tile(t)
            o = self.A["out"][0, t * 128:(t + 1) * 128, :]
            self.SP.todo.append(lambda e, o=o, x=x: e.dma_start(o, x).then_inc(self.s_out, 16))
            n += 16
        self.SP.todo.append(lambda e: e.wait_ge(self.s_out, n))


def program(nc, A, plan=None):
    p = Program(nc, A, plan)
    if plan is not None:
        p.run()
    return p


_DIRECT = ["x", "positions", "b_ada", "pool_w", "rwkv_w2", "rwkv_a2", "final_g", "attn_sink_2",
           "ln1_g_2", "ln1_b_2", "ln2_g_2", "ln2_b_2", "ln3_g_2", "ln3_b_2"]


def kernel(**inputs):
    import concourse.bacc as bacc
    from concourse.bass_utils import run_bass_kernel_spmd

    inputs = {k: np.asarray(v) for k, v in inputs.items()}
    nc = bacc.Bacc("TRN2", target_bir_lowering=False, num_devices=1)
    spec = columns()
    arrays = {}
    for name in _DIRECT:
        arrays[name] = np.ascontiguousarray(inputs[name])
    cols = np.empty((128, len(spec.pieces)), np.float32)
    flat = {}
    for j, col in enumerate(spec.pieces):
        at = 0
        for name, index, s, n in col:
            v = inputs[name][index].reshape(-1)
            cols[at:at + n, j] = v[s:s + n]
            at += n
    arrays["cols"] = cols
    arrays.update(constants())

    def declare(nc, nu):
        A = {}
        for name, a in arrays.items():
            A[name] = nc.dram_tensor(f"in_{name}", a.shape, mybir.dt.from_np(a.dtype), kind="ExternalInput").ap()
        A["W"] = nc.dram_tensor("in_W", (nu, 128, 1024), F32, kind="ExternalInput").ap()
        A["out"] = nc.dram_tensor("out", (1, T, D), F32, kind="ExternalOutput").ap()
        A["rot"] = nc.dram_tensor("rot", (2, 128, 512), F32, kind="Internal").ap()
        A["xd"] = nc.dram_tensor("xd", (T, D), F32, kind="Internal").ap()
        return A

    draft = bacc.Bacc("TRN2", target_bir_lowering=False, num_devices=1)
    plan = program(draft, declare(draft, 1)).kinds
    prog = program(nc, declare(nc, len(plan)), plan)
    arrays["W"] = pack_units(prog.units, inputs)
    r = run_bass_kernel_spmd(nc, [{f"in_{k}": v for k, v in arrays.items()}], core_ids=[0])
    return r.results[0]["out"]
```

```python
from contextlib import ExitStack
import itertools

import numpy as np
import concourse.bass as bass
from concourse import mybir

F32 = mybir.dt.float32
FR = mybir.dt.float32r
I32 = mybir.dt.int32
U32 = mybir.dt.uint32
ALU = mybir.AluOpType
ACT = mybir.ActivationFunctionType
AX = mybir.AxisListType

T = 512
D = 1024
DEPTH = 2
FF = 2816
NFF = FF // 128
RAW = 3
RING = 4
ALPHA = (2.0 * DEPTH) ** 0.25
KAPPA = float(np.exp(-0.5))
POOLW = (2, 4, 8, 16)


class Columns:

    def __init__(self):
        self.pieces = []
        self.at = {}

    def add(self, key, name, index, spans):
        self.at[key] = len(self.pieces)
        flat = [(name, index, s, n) for s, n in spans]
        col, room = [], 128
        for name_, ix, s, n in flat:
            while n:
                m = min(n, room)
                col.append((name_, ix, s, m))
                s, n, room = s + m, n - m, room - m
                if room == 0:
                    self.pieces.append(col)
                    col, room = [], 128


def columns():
    c = Columns()
    full = [(0, 512)]
    for l in range(DEPTH):
        c.add(("norm_g", l), "norm_g", (l,), [(0, 1024)])
        c.add(("b_ada", l), "b_ada", (l,), [(0, 2048)])
        c.add(("pool_scale", l), "pool_scale", (l,), full)
        c.add(("ret_g", l), "ret_norm_g", (l,), full)
        c.add(("mu_r", l), "rwkv_shift_mu", (l,), [(0, 512)])
        c.add(("mu_k", l), "rwkv_shift_mu", (l,), [(576, 512)])
        c.add(("mu_v", l), "rwkv_shift_mu", (l,), [(1088, 512)])
        c.add(("mu_wa", l), "rwkv_shift_mu", (l,), [(512, 64), (1600, 64)])
        for k, n in (("w0", "rwkv_w0"), ("a0", "rwkv_a0"), ("k_k", "rwkv_k_k"), ("k_a", "rwkv_k_a"),
                     ("r_k", "rwkv_r_k"), ("ln_w", "rwkv_ln_w"), ("ln_b", "rwkv_ln_b")):
            c.add((k, l), n, (l,), full)
        for k in ("ln1", "ln2", "ln3"):
            c.add((k + "g", l), k + "_g_2", (l,), [(0, 1024)])
            c.add((k + "b", l), k + "_b_2", (l,), [(0, 1024)])
        for j in range(3):
            c.add(("sc", l, j), "sc_conv_w_2", (l, j), [(0, 256)])
        for j in range(31):
            c.add(("cc", l, j), "cc_conv_w_2", (l, j), [(0, 256)])
        c.add(("cc_b", l), "cc_conv_b_2", (l,), [(0, 256)])
        c.add(("cc_lg", l), "cc_ln_g_2", (l,), [(0, 256)])
        c.add(("cc_lb", l), "cc_ln_b_2", (l,), [(0, 256)])
    c.add(("final_g",), "final_g", (), [(0, 1024)])
    c.add(("c",), "c", (0,), [(0, 1024)])
    return c


def constants():
    p = np.arange(128)
    i = np.arange(512)
    out = {}
    out["ident"] = np.eye(128, dtype=np.float32)
    out["blk64"] = (p[:, None] // 64 == p[None, :] // 64).astype(np.float32)
    out["mean256"] = np.full((128, 128), 1.0 / 256, np.float32)
    half = 64
    fr = (np.float32(10000.0) ** (-np.arange(half, dtype=np.float32) / half)).astype(np.float32)
    sign = np.where(p < 64, -1.0, 1.0).astype(np.float32)
    out["misc"] = np.stack([fr[p % 64], sign], 1).astype(np.float32)
    lg = np.log1p(-(2.0 ** (-5.0 - np.arange(4))))
    dm = np.zeros((128, 4, 512), np.float64)
    for h in range(4):
        d = i[None, :] - p[:, None]
        dm[:, h] = np.where(d >= 0, np.exp(lg[h] * np.maximum(d, 0)), 0) * 128.0 ** -0.5
    out["decay"] = dm.reshape(128, 2048).astype(np.float32)
    s, t = p[:, None], p[None, :]
    strict, incl = (s < t), (s <= t)
    out["gmask"] = np.concatenate([strict, incl, strict, incl], 1).astype(np.float32)
    out["m1"] = ((s // 2 == t // 2) & (s < t)).astype(np.float32)
    lm = []
    for n in (2, 4, 8, 16):
        second = p % (2 * n) >= n
        lm.append((p[:, None] // (2 * n) == p[second][None, :] // (2 * n)) & ~second[:, None])
    out["lmask"] = np.concatenate(lm, 1).astype(np.uint32)
    out["reset"] = np.broadcast_to((i % 128 != 0).astype(np.float32), (128, 512)).copy()
    cnt = np.stack([1.0 / np.minimum(i + 1, w) for w in POOLW]).reshape(-1)
    out["invcnt"] = np.broadcast_to(cnt.astype(np.float32), (128, 2048)).copy()
    inv = (np.float32(10000.0) ** (-np.arange(32, dtype=np.float32) / 32)).astype(np.float32)
    ang = (i.astype(np.float32)[None, :] * inv[p % 32][:, None]).astype(np.float32).astype(np.float64)
    sg = np.where(p % 64 < 32, -1.0, 1.0)[:, None]
    out["rcos"] = np.cos(ang).astype(np.float32)
    out["rsin"] = (np.sin(ang) * sg).astype(np.float32)
    j = np.arange(384)[None, :] - 128
    out["amask"] = np.where(np.abs(p[:, None] - j) <= 128, 0.0, -1e30).astype(np.float32)
    return out


def pack_units(units, inputs):
    out = np.empty((len(units), 128, 1024), np.float32)
    for n, (name, index, pieces) in enumerate(units):
        w = inputs[name][index]
        at = 0
        for k, c, m in pieces:
            out[n, :, at:at + m] = w[k:k + 128, c:c + m]
            at += m
    return out


def t_pieces(col, k0=0, nk=8, groups=1):
    return tuple((k0 + 128 * k, col + 128 * g, 128) for g in range(groups) for k in range(nk))


def n_pieces(k, col):
    return ((k, col, 512), (k + 128, col, 512))


class Queue:

    def __init__(self, sem, serial):
        self.sem, self.serial = sem, serial
        self.n, self.seen, self.todo = 0, {}, []

    def wait(self, *tokens):
        for t in tokens:
            if isinstance(t, list):
                self.wait(*t)
            elif t is not None and self.seen.get(id(t[0]), 0) < t[1]:
                self.seen[id(t[0])] = t[1]
                self.todo.append(lambda e, t=t: e.wait_ge(t[0], t[1]))

    def __call__(self, fn, *tokens, signal=True):
        self.wait(*tokens)
        if self.serial and self.n:
            self.wait((self.sem, self.n))
        if not signal:
            self.todo.append(fn)
            return None
        self.n += 1
        self.todo.append(lambda e: fn(e).then_inc(self.sem, 1))
        return (self.sem, self.n)

    def last(self):
        return (self.sem, self.n) if self.n else None


class Slot:

    def __init__(self, t):
        self.t, self.free, self.held = t, [], False

    def done(self, *tokens):
        self.free, self.held = list(tokens), False


class Rota:
    def __init__(self, tensors):
        self.slots = [t if isinstance(t, Slot) else Slot(t) for t in tensors]
        self.n = 0

    def take(self):
        s = self.slots[self.n % len(self.slots)]
        self.n += 1
        assert not s.held
        s.held = True
        return s


def mix(main, side, main_steps, side_steps):
    done = n = 0
    for _ in main:
        n += 1
        while done < side_steps and done * main_steps < n * side_steps:
            next(side, None)
            done += 1
    for _ in range(done, side_steps):
        next(side, None)


def result(gen):
    while True:
        try:
            next(gen)
        except StopIteration as end:
            return end.value


def drain(gen):
    for _ in gen:
        pass


def abreast(*gens):
    gens = list(gens)
    while gens:
        for g in list(gens):
            if next(g, "end") == "end":
                gens.remove(g)
            else:
                yield


class Program:

    def __init__(self, nc, A, plan=None):
        self.nc, self.A = nc, A
        self.plan = plan
        self.units, self.kinds = [], []
        self.colspec = columns()
        self.ctx = ExitStack()
        self.nsem = 0
        self.build()

    def sem(self, name):
        self.nsem += 1
        return self.ctx.enter_context(self.nc.semaphore(name))

    def alloc(self, ctx, name, width, dt=F32):
        return ctx.enter_context(self.nc.sbuf_tensor(name, [128, width], dt))

    def load(self, dst, src, *tokens):
        s = self.sem(f"ld{self.nsem}")
        q = self.G if tokens else self.SP
        q.wait(*tokens)
        q.todo.append(lambda e: e.dma_start(dst, src).then_inc(s, 16))
        return (s, 16)

    def col(self, key, j=0):
        c = self.colspec.at[key] + j
        return self.cols[:, c:c + 1]

    def fence(self):
        return [q.last() for q in (self.PE, self.V, self.S, self.G)]

    def fetch(self):
        n = self.n_fetched
        if self.plan is None or n >= len(self.plan):
            return
        self.n_fetched += 1
        r = n % RAW
        if n >= RAW:
            self.SP.wait(*self.raw_free[n - RAW])
        src, dst, s = self.A["W"][n], self.raw[:, r * 1024:(r + 1) * 1024], self.s_raw[r]
        self.SP.todo.append(lambda e: e.dma_start(dst, src).then_inc(s, 16))

    def raw_unit(self, n):
        r = n % RAW
        return self.raw[:, r * 1024:(r + 1) * 1024], (self.s_raw[r], 16 * (n // RAW + 1))

    def split_next(self):
        n = self.next_raw
        self.next_raw += 1
        i = self.n_split
        self.n_split += 1
        k = i % RING
        raw, landed = self.raw_unit(n)
        hi, lo = self.whi[:, k * 1024:(k + 1) * 1024], self.wlo[:, k * 1024:(k + 1) * 1024]
        free = self.used[i - RING] if i >= RING else None
        t1 = self.S(lambda e: e.copy(hi, raw), landed, free)
        t2 = self.V(lambda e: e.tensor_tensor(lo, raw, hi.bitcast(F32), ALU.subtract), landed, free, t1)
        self.split_tokens[i] = [t1, t2]
        self.raw_free[n] = [t1, t2]
        self.fetch()

    def ahead(self):
        if self.plan is None:
            return
        while self.next_raw < len(self.plan) and self.plan[self.next_raw] and \
                self.n_split <= self.n_taken + RING - 1 and \
                (self.n_split < RING or self.n_split - RING in self.used):
            self.split_next()

    def unit(self, name, index, pieces):
        self.units.append((name, index, pieces))
        self.kinds.append(True)
        i = self.n_taken
        if self.plan is None:
            self.split_tokens[i] = []
        self.ahead()
        self.n_taken += 1
        k = i % RING
        return (self.whi[:, k * 1024:(k + 1) * 1024], self.wlo[:, k * 1024:(k + 1) * 1024],
                self.split_tokens[i], i)

    def direct(self, name, index, pieces):
        n = len(self.units)
        self.units.append((name, index, pieces))
        self.kinds.append(False)
        assert self.plan is None or self.next_raw == n
        self.next_raw = n + 1
        return self.raw_unit(n) + (n,)

    def release(self, n, token):
        self.raw_free[n] = [token]
        self.fetch()
        self.ahead()

    def mm3(self, out, ah, al, bh, bl, first, last, *tokens, signal=None):
        def three(e):
            e.matmul(out, ah, bh, start=first, stop=False, skip_group_check=True)
            e.matmul(out, ah, bl, start=False, stop=False, skip_group_check=True)
            return e.matmul(out, al, bh, start=False, stop=last, skip_group_check=True)
        return self.PE(three, *tokens, signal=last if signal is None else signal)

    def gemm_t(self, *args, **kw):
        return result(self.gemm_steps(*args, **kw))

    def gemm_steps(self, name, index, col, xh, xl, ready, k0=0, nk=8, groups=1, pieces=None, rota=None):
        wh, wl, tok, n = self.unit(name, index, pieces or t_pieces(col, k0, nk, groups))
        out = []
        for g in range(groups):
            bank = (rota or self.pg).take()
            for k in range(nk):
                c = (g * nk + k) * 128
                t = self.mm3(bank.t[:, :], wh[:, c:c + 128], wl[:, c:c + 128], xh(k), xl(k),
                             k == 0, k == nk - 1, tok, bank.free, ready(k) if callable(ready) else ready)
                if k == nk - 1 and g == groups - 1:
                    self.used[n] = t
                yield
            out.append((bank, t))
        return out

    def gemm_halves(self, name, index, cols):
        jobs = [self.unit(name, index, t_pieces(c)) + (self.all4.take(),) for c in cols]
        out = []
        for hf in range(2):
            if hf:
                self.turn_rest()
            for wh, wl, tok, n, bank in jobs:
                o = bank.t[:, 256 * hf:256 * hf + 256]
                for k in range(8):
                    c = slice(128 * k, 128 * k + 128)
                    x = slice(512 * k + 256 * hf, 512 * k + 256 * hf + 256)
                    t = self.mm3(o, wh[:, c], wl[:, c], self.hh[:, x], self.hl[:, x], k == 0, k == 7, tok, bank.free,
                                 self.h_tiles[2 * hf], self.h_tiles[2 * hf + 1])
                if hf:
                    self.used[n] = t
                    out.append((bank, t))
        return out

    def turn_rest(self):
        for p in self.pending:
            self.to_hT_tile(*p)
        self.pending = []

    def gemm_n(self, *args, **kw):
        return list(self.gemm_tiles(*args, **kw))

    def gemm_tiles(self, name, index, k0s, col, xh, xl, ready, rota, late=1):
        banks = [rota.take() for _ in range(4)]
        nk = len(k0s) * 2
        held = []
        for ui, k0 in enumerate(k0s):
            u = self.unit(name, index, n_pieces(k0, col))
            held.append((ui,) + u)
            if 0 <= len(k0s) - late <= ui < len(k0s) - 1:
                continue
            if ui == len(k0s) - 1:
                order = [(h, j, t) for t in range(4) for h in held for j in range(2)]
            else:
                order = [(h, j, t) for h in held for j in range(2) for t in range(4)]
            for q, ((u_, wh, wl, tok, n), j, t) in enumerate(order):
                k = 2 * u_ + j
                fin = k == nk - 1
                end = q == len(order) - 1
                a = self.mm3(banks[t].t[:, :], xh(k, t), xl(k, t), wh[:, j * 512:(j + 1) * 512], wl[:, j * 512:(j + 1) * 512],
                             k == 0, fin, tok, banks[t].free, ready(k) if callable(ready) else ready, signal=fin or end)
                if fin and not end:
                    yield banks[t], a
            for h in held:
                self.used[h[4]] = a
            held = []
        yield banks[3], a

    def split(self, src, hi, lo, *tokens):
        t1 = self.S(lambda e: e.copy(hi, src), *tokens)
        t2 = self.V(lambda e: e.tensor_tensor(lo, src, hi.bitcast(F32), ALU.subtract), t1, *tokens)
        return [t1, t2]

    def vtt(self, o, a, b, op, *tokens):
        return self.V(lambda e: e.tensor_tensor(o, a, b, op), *tokens)

    def vts(self, o, a, s1, s2, op0, op1, *tokens):
        if op1 is None:
            return self.V(lambda e: e.tensor_scalar(o, a, s1, None, op0), *tokens)
        return self.V(lambda e: e.tensor_scalar(o, a, s1, s2, op0, op1), *tokens)

    def stt(self, o, a, s, b, op0, op1, *tokens):
        return self.V(lambda e: e.scalar_tensor_tensor(out=o, in0=a, scalar=s, in1=b, op0=op0, op1=op1), *tokens)

    def act(self, o, a, f, *tokens, bias=0.0, scale=1.0):
        return self.S(lambda e: e.activation(o, a, f, bias=bias, scale=scale), *tokens)

    def rstd(self, o, var, mul, eps, *tokens):
        w = o.shape[1]
        self.G(lambda e: e.tensor_scalar(o, var, mul, eps, ALU.mult, ALU.add), *tokens)
        return self.G(lambda e: e.tensor_tensor(o, o, self.mhalf[:, 0:w], ALU.pow))

    def transpose4(self, ins, bank, *tokens):
        t = None
        for j, x in enumerate(ins):
            o = bank.t[:, j * 128:(j + 1) * 128]
            t = self.PE(lambda e, o=o, x=x: e.transpose(o, x, self.ident[:, :]), bank.free, *tokens,
                        signal=j == len(ins) - 1)
        return t

    def build(self):
        nc, A = self.nc, self.A
        self.n_fetched = self.n_split = self.n_taken = self.next_raw = 0
        self.split_tokens, self.used, self.raw_free = {}, {}, {}
        ctx = self.ctx
        self.PE = Queue(self.sem("s_pe"), False)
        self.V = Queue(self.sem("s_dve"), True)
        self.S = Queue(self.sem("s_act"), True)
        self.G = Queue(self.sem("s_pool"), True)
        self.SP = Queue(None, False)
        self.s_raw = [self.sem(f"s_raw{i}") for i in range(RAW)]
        self.s_out = self.sem("s_out")
        a = lambda n, w, dt=F32: self.alloc(ctx, n, w, dt)
        self.raw = a("raw", RAW * 1024)
        self.whi, self.wlo = a("whi", RING * 1024, FR), a("wlo", RING * 1024, FR)
        self.hh, self.hl = a("hh", 4096, FR), a("hl", 4096, FR)
        self.cols = a("cols", len(self.colspec.pieces))
        self.ident = a("ident", 128)
        self.mhalf = a("mhalf", 16)
        self.stat = a("stat", 64)
        self.mod = [a(f"mod{l}", 24) for l in range(DEPTH)]
        self.cact = a("cact", 16)
        cr = ExitStack()
        self.xn = self.alloc(cr, "xn", 4096)
        cr.close()
        cr = ExitStack()
        set0 = self.chunk_set(cr, 0)
        cr.close()
        self.RT = [a(f"RT{i}", 512) for i in range(8)]
        self.tmp = Rota([a(f"tmp{i}", 512) for i in range(2)])
        banks = [ctx.enter_context(nc.psum_tensor(f"bank{i}", [128, 512], F32)) for i in range(8)]
        self.all4, self.ps = Rota(banks[:4]), Rota(banks[4:])
        self.main2, self.side2 = Rota(self.all4.slots[:2]), Rota(self.all4.slots[2:])
        self.pg = self.all4

        ca = ExitStack()
        b = lambda n, w, dt=F32, c=ca: self.alloc(c, n, w, dt)
        co = ExitStack()
        self.oh, self.ol = b("oh", 2048, FR, co), b("ol", 2048, FR, co)
        co.close()
        self.sg2 = b("sg2", 4096)
        self.mrg = b("mrg", 4096)
        self.blk64 = b("blk64", 128)
        self.misc = b("misc", 2)
        c1 = ExitStack()
        self.ph, self.pl = b("ph", 2048, FR, c1), b("pl", 2048, FR, c1)
        self.poolw = b("poolw", 512, c=c1)
        self.invcnt = b("invcnt", 2048, c=c1)
        self.decay = b("decay", 2048, c=c1)
        self.vret = b("vret", 2048, c=c1)
        self.qk = Rota([b(f"qk{i}", 1536, c=c1) for i in range(2)])
        self.pt = b("pt", 2048, c=c1)
        self.onat = b("onat", 512, c=c1)
        self.sgr = b("sgr", 512, c=c1)
        self.cosr, self.sinr = b("cosr", 512, c=c1), b("sinr", 512, c=c1)
        c1.close()
        cx = ExitStack()
        self.xs = b("xs", 4096, c=cx)
        cx.close()
        c2 = ExitStack()
        self.AR = b("AR", 4096, c=c2)
        self.KH, self.BH = b("KH", 2048, c=c2), b("BH", 2048, c=c2)
        self.VN, self.VB = b("VN", 2048, c=c2), b("VB", 2048, c=c2)
        self.gmask, self.m1 = b("gmask", 512, c=c2), b("m1", 128, c=c2)
        self.lmask = b("lmask", 256, U32, c2)
        self.em = b("em", 64, c=c2)
        self.st = b("st", 256, c=c2)
        c3 = ExitStack()
        self.PP = b("PP", 513, c=c3)
        self.reset = b("reset", 512, c=c3)
        self.wa = b("wa", 512, c=c3)
        self.w2a2 = b("w2a2", 512, c=c3)
        c3.close()
        c4 = ExitStack()
        self.sets = [set0, self.chunk_set(c4, 1)]
        for g, z in enumerate(self.sets):
            for n, w in (("KN", 256), ("BN", 256), ("YN", 256), ("SP", 256), ("hs", 12)):
                z[n] = b(f"{n}{g}", w, c=c4)
        c4.close()
        c4 = ExitStack()
        self.o2h, self.o2l = b("o2h", 2048, FR, c4), b("o2l", 2048, FR, c4)
        c4.close()
        c2.close()
        c5 = ExitStack()
        self.mh, self.ml = b("mh", 4096, FR, c5), b("ml", 4096, FR, c5)
        self.gate = b("gate", 1024, c=c5)
        self.crep = b("crep", 1024, c=c5)
        c5.close()
        ca.close()

        cb = ExitStack()
        d = lambda n, w, dt=F32, c=cb: self.alloc(c, n, w, dt)
        self.bc = d("bc", 2048)
        cf = ExitStack()
        self.fh, self.fl = d("fh", NFF * 512, FR, cf), d("fl", NFF * 512, FR, cf)
        cf.close()
        cm = ExitStack()
        self.xh8, self.xl8 = d("xh8", 4096, FR, cm), d("xl8", 4096, FR, cm)
        self.qT = d("qT", 2048, c=cm)
        self.kT, self.kS = d("kT", 512, c=cm), d("kS", 512, c=cm)
        self.v2 = d("v2", 512, c=cm)
        self.rcos, self.rsin, self.amask = d("rcos", 512, c=cm), d("rsin", 512, c=cm), d("amask", 384, c=cm)
        self.mean256 = d("mean256", 128, c=cm)
        self.sink = d("sink", 8, c=cm)
        self.ccp = d("ccp", 1088, c=cm)
        self.scp = d("scp", 1088, c=cm)
        self.acc = d("acc", 1024, c=cm)
        self.pr = Rota([d(f"pr{i}", 384, c=cm) for i in range(8)])
        self.prT = Rota([d(f"prT{i}", 384, c=cm) for i in range(3)])
        self.ao = Rota([d("ao0", 512, c=cm)])
        self.sm = Rota([d(f"sm{i}", 20, c=cm) for i in range(2)])
        self.rq = Rota([d(f"rq{i}", 1024, c=cm) for i in range(2)])
        self.t3 = [d(f"tz{i}", 512, c=cm) for i in range(2)]
        self.zc = d("zc", 1024, c=cm)
        cm.close()
        cb.close()

        self.k_cols = self.load(self.cols[:, :], A["cols"])
        for _ in range(RAW):
            self.fetch()
        self.k_id = self.load(self.ident[:, :], A["ident"])
        cc = self.colspec.at[("c",)]
        t = self.act(self.cact[:, 8:16], self.cols[:, cc:cc + 8], ACT.Sigmoid, self.k_cols)
        self.k_cact = self.vtt(self.cact[:, 0:8], self.cols[:, cc:cc + 8], self.cact[:, 8:16], ALU.mult, t, self.k_cols)
        self.k_half = self.G(lambda e: e.memset(self.mhalf[:, :], -0.5))
        self.k_xd = None
        first = self.modulation(0)
        for _ in range(10):
            next(first)
        self.load_x(A["x"][0])
        self.prepare_a()
        for _ in range(22):
            next(first)
        k = self.norm_x()
        drain(first)
        for l in range(DEPTH):
            self.layer_a(l, self.norm_x() if l else k)
        self.final_norm()
        for l in range(DEPTH):
            self.layer_b(l)
        self.finish()

    def chunk_set(self, ctx, g):
        z = {n: self.alloc(ctx, f"{n}{g}", w) for n, w in (("G4", 2048), ("X", 512), ("U", 512), ("Y", 512))}
        z["free"] = []
        return z

    def load_x(self, src, *tokens):
        self.x_ready = [[self.load(self.x_tile(t), src[t * 128:(t + 1) * 128, :], *tokens)] for t in range(4)]

    def run(self):
        with self.ctx:
            block = self.ctx.enter_context(self.nc.Block())
            for reg, q in ((block.sync, self.SP), (block.gpsimd, self.G), (block.scalar, self.S),
                           (block.vector, self.V), (block.tensor, self.PE)):
                def body(e, q=q):
                    for f in q.todo:
                        f(e)
                reg(body)

    def x_tile(self, t):
        return self.xn[:, t * 1024:(t + 1) * 1024]

    def to_hT(self, blocks, ready, scale, bias):
        f = self.h_free
        parts = [None] * 8

        def rest(d, tm, t1, t2):
            lo, hi = self.hl[:, d * 512:(d + 1) * 512], self.hh[:, d * 512:(d + 1) * 512]
            t3 = self.vtt(lo, tm.t[:, :], hi.bitcast(F32), ALU.subtract, t1, t2, f)
            tm.done(t2, t3)
            parts[d] = [t2, t3]

        late = None
        for d in range(8):
            bank = self.ps.take()
            t = self.transpose4([blocks(j, d) for j in range(4)], bank, self.k_id, ready)
            tm = self.tmp.take()
            if d % 2:
                t1 = self.vts(tm.t[:, :], bank.t[:, :], scale(d), bias(d), ALU.mult, ALU.add, t, tm.free)
            else:
                t1 = self.act(tm.t[:, :], bank.t[:, :], ACT.Identity, t, tm.free, bias=bias(d), scale=scale(d))
            bank.done(t1)
            if late:
                rest(*late)
            hi = self.hh[:, d * 512:(d + 1) * 512]
            t2 = self.S(lambda e, hi=hi, tm=tm: e.copy(hi, tm.t[:, :]), t1, f)
            late = (d, tm, t1, t2)
        rest(*late)
        self.h_ready = lambda k: parts[k]

    def h_rhs(self, k):
        return self.hh[:, k * 512:(k + 1) * 512]

    def l_rhs(self, k):
        return self.hl[:, k * 512:(k + 1) * 512]

    def h_lhs(self, k, t):
        return self.hh[:, k * 512 + t * 128:k * 512 + (t + 1) * 128]

    def l_lhs(self, k, t):
        return self.hl[:, k * 512 + t * 128:k * 512 + (t + 1) * 128]

    def prepare_a(self):
        A = self.A
        self.h_free = []
        self.k_misc = [self.load(self.misc[:, :], A["misc"]), self.load(self.blk64[:, :], A["blk64"])]
        k_pos = self.load(self.xs[:, 0:512].bitcast(I32), A["positions"][0].partition_broadcast(128))
        x = [self.xs[:, i * 512:(i + 1) * 512] for i in range(6)]
        self.V(lambda e: e.tensor_copy(x[1], x[0].bitcast(I32)), k_pos)
        self.vts(x[1], x[1], self.misc[:, 0:1], None, ALU.mult, None, *self.k_misc)
        big = 12582912.0
        c1 = 6.28125
        c2 = float(np.float32(2 * np.pi - c1))
        c3 = float(2 * np.pi - c1 - float(np.float32(c2)))
        pi = 3.1415925
        for off, out in ((0.25, x[4]), (0.0, x[5])):
            self.vts(x[2], x[1], float(1 / (2 * np.pi)), off, ALU.mult, ALU.add)
            self.vts(x[2], x[2], big, None, ALU.add, None)
            self.vts(x[2], x[2], big, None, ALU.subtract, None)
            self.stt(x[3], x[2], -c1, x[1], ALU.mult, ALU.add)
            self.stt(x[3], x[2], -c2, x[3], ALU.mult, ALU.add)
            self.stt(x[3], x[2], -c3, x[3], ALU.mult, ALU.add)
            self.vts(x[3], x[3], float(off * 2 * np.pi), pi, ALU.add, ALU.min)
            t = self.vts(x[3], x[3], -pi, None, ALU.max, None)
            t = self.act(out, x[3], ACT.Sin, t)
            self.V.wait(t)
        t = self.vts(x[5], x[5], self.misc[:, 1:2], None, ALU.mult, None, t)
        self.k_tab = [self.load(A["rot"][i], x[4 + i], t) for i in range(2)]

    def modulation(self, l):
        for q in range(4):
            bank = self.side2.take()
            for ui in range(4):
                w, landed, n = self.direct("w_ada", (l,), n_pieces(256 * ui, 512 * q))
                for j in range(2):
                    k = 2 * ui + j
                    t = self.PE(lambda e, k=k, j=j, w=w, bank=bank: e.matmul(
                        bank.t[0:1, :], self.cact[:, k:k + 1], w[:, j * 512:(j + 1) * 512], start=k == 0, stop=k == 7),
                        landed, bank.free, self.k_cact, signal=j == 1)
                    if j == 0:
                        yield
                if ui == 3 and l == 0:
                    row, used = self.tmp.take(), t
                    t = self.S(lambda e, row=row, bank=bank: e.copy(row.t[0:1, :], bank.t[0:1, :]), t, row.free)
                    bank.done(t)
                    self.release(n, used)
                else:
                    self.release(n, t)
                yield
            if l:
                row = self.tmp.take()
                t = self.S(lambda e, row=row, bank=bank: e.copy(row.t[0:1, :], bank.t[0:1, :]), t, row.free)
                bank.done(t)
            yield
            yield
            bank = self.side2.take()
            for i in range(4):
                tc = self.PE(lambda e, i=i, row=row, bank=bank: e.matmul(
                    bank.t[:, i:i + 1], row.t[0:1, i * 128:(i + 1) * 128], self.ident[0:1, 0:1], start=True, stop=True,
                    skip_group_check=True), t, bank.free, self.k_id, signal=i == 3)
            row.done(tc)
            o = self.mod[l][:, 4 * q:4 * q + 4]
            t = self.S(lambda e, o=o, bank=bank: e.copy(o, bank.t[:, 0:4]), tc)
            bank.done(t)
        ba = self.colspec.at[("b_ada", l)]
        ng = self.colspec.at[("norm_g", l)]
        mod = self.mod[l]
        self.vtt(mod[:, 0:16], mod[:, 0:16], self.cols[:, ba:ba + 16], ALU.add, t, self.k_cols)
        self.k_mod = self.stt(mod[:, 16:24], mod[:, 8:16], 1.0, self.cols[:, ng:ng + 8], ALU.add, ALU.mult)
        yield

    def gates(self, l, f):
        A = self.A
        t1 = self.V(lambda e: e.tensor_copy(self.crep[:, :].rearrange("p (k n) -> p k n", k=8),
                                            self.cact[:, 0:8].unsqueeze(2).broadcast_to([128, 8, 128])), f, self.k_cact)
        kb = self.load(self.gate[:, :], A["b_ada"][l, 2048:3072].partition_broadcast(128), f)
        self.k_gate = []
        for half in range(2):
            bank = self.pg.take()
            for ui in range(4):
                w, landed, n = self.direct("w_ada", (l,), n_pieces(256 * ui, 2048 + 512 * half))
                for j in range(2):
                    k = 2 * ui + j
                    t = self.PE(lambda e, w=w, k=k, j=j, bank=bank: e.matmul(
                        bank.t[:, :], self.crep[:, k * 128:(k + 1) * 128], w[:, j * 512:(j + 1) * 512],
                        start=k == 0, stop=k == 7), landed, bank.free, t1, signal=j == 1)
                self.release(n, t)
            g = self.gate[:, half * 512:(half + 1) * 512]
            t = self.vtt(g, bank.t[:, :], g, ALU.add, t, kb)
            bank.done(t)
            self.k_gate.append(t)

    def norm_x(self):
        f = self.fence()
        tt = []
        for t in range(4):
            xt, xs = self.x_tile(t), self.xs[:, t * 1024:(t + 1) * 1024]
            tt.append(self.S(lambda e, xt=xt, xs=xs, t=t: e.activation(xs, xt, ACT.Square, accum_out=self.stat[:, t:t + 1]),
                             self.x_ready[t], f, self.k_tab))
        r = self.rstd(self.stat[:, 4:8], self.stat[:, 0:4], 1.0 / D, 1e-6, tt[-1], f)
        k = []
        for t in range(4):
            k.append(self.vts(self.xs[:, t * 1024:(t + 1) * 1024], self.x_tile(t), self.stat[:, 4 + t:5 + t], None,
                              ALU.mult, None, r, tt[t]))
        return k

    def layer_a(self, l, k):
        A = self.A
        f = self.fence()
        self.h_free, self.h_tiles = f, [None] * 4
        self.to_hT(lambda t, d: self.xs[:, t * 1024 + d * 128:t * 1024 + (d + 1) * 128], k + [self.k_mod],
                   lambda d: self.mod[l][:, 16 + d:17 + d], lambda d: self.mod[l][:, d:d + 1])
        self.proj = lambda col, **kw: self.gemm_t("w_in", (l,), col, self.h_rhs, self.l_rhs, self.h_ready, **kw)
        self.proj_steps = lambda col, **kw: self.gemm_steps("w_in", (l,), col, self.h_rhs, self.l_rhs, self.h_ready, **kw)
        f = self.fence()
        self.k_pw = self.load(self.poolw[:, :].rearrange("p (g d) -> p g d", g=4),
                              A["pool_w"][l].rearrange("g c d -> c g d"), f)
        self.k_ic = self.load(self.invcnt[:, :], A["invcnt"], f)
        self.k_dc = self.load(self.decay[:, :], A["decay"], f)
        self.k_rot = [self.load(self.cosr[:, :], A["rot"][0], f, self.k_tab), self.load(self.sinr[:, :], A["rot"][1], f, self.k_tab)]
        k = self.pool(l, f)
        self.pg = self.main2
        side = self.branch(l, 0, k)
        self.ret_ready = []
        mix(self.retention(l, f), side, 19, 96)
        drain(side)
        side = self.branch(l, 1, self.ret_ready)
        self.prepare_rwkv(l)
        mix(self.rwkv(l), side, 38, 88)
        if l + 1 < DEPTH:
            side = itertools.chain(side, self.modulation(l + 1))
        side = itertools.chain(side, self.last_gates(l))
        mix(self.chunks(l), side, 200, 124 if l + 1 < DEPTH else 88)
        drain(side)
        self.pg = self.all4
        f = self.fence()
        self.load_x(A["x"][0] if l == 0 else A["xd"], f, self.k_xd)
        k = self.rwkv_out(l)
        self.gates(l, f)
        self.h_last = [self.PE.last()]
        drain(self.branch(l, 2, k))
        if l == DEPTH - 1:
            self.k_rows = self.rows(A["final_g"], None)
        self.w_out(l)

    def silu(self, out, bank, tok, *free):
        t1 = self.act(out, bank.t[:, :], ACT.Sigmoid, tok, *free)
        t2 = self.vtt(out, bank.t[:, :], out, ALU.mult, t1, tok)
        bank.done(t1, t2)
        return t2

    def pool(self, l, f):
        ready = []
        s = self.pt[:, 0:512], self.pt[:, 512:1024]
        u, sg = self.pt[:, 1024:1536], self.pt[:, 1536:2048]
        td = tz = ts = None
        for g in range(5):
            if g < 4:
                (bank, tu), = self.proj(g * 128)
            if g:
                pb = self.ps.take()
                tp = self.PE(lambda e, pb=pb, dd=dd, g=g: e.matmul(pb.t[:, :], self.poolw[:, (g - 1) * 128:g * 128], dd,
                                                                  start=True, stop=True), td, self.k_pw, pb.free)
                t = self.stt(sg, pb.t[:, :], self.col(("pool_scale", l), g - 1), sg, ALU.mult, ALU.mult, tp, tz, self.k_cols)
                pb.done(t)
                ts = self.split(sg, self.ph[:, (g - 1) * 512:g * 512], self.pl[:, (g - 1) * 512:g * 512], t, f)
                ready += ts
            if g == 4:
                break
            t = self.S(lambda e, b=bank: e.copy(u, b.t[:, :]), tu, td, f)
            bank.done(t)
            src, n, i, w = u, 1, 0, POOLW[g]
            while n < w:
                dst = s[i]
                self.vtt(dst[:, n:512], src[:, n:512], src[:, 0:512 - n], ALU.add, t, f)
                self.V(lambda e, dst=dst, src=src, n=n: e.tensor_copy(dst[:, 0:n], src[:, 0:n]))
                src, n, i = dst, 2 * n, 1 - i
            dd = s[i]
            self.vtt(dd, src, self.invcnt[:, g * 512:(g + 1) * 512], ALU.mult, self.k_ic)
            td = self.vtt(dd, dd, u, ALU.subtract)
            (bank, t), = self.proj(512 + g * 128)
            tz = self.silu(sg, bank, t, f, ts)
        return ready

    def last_gates(self, l):
        f = [self.PE.last()]
        for m in range(8):
            (bank, t), = yield from self.proj_steps(5248 + 2048 + m * 128, rota=self.side2)
            t = self.act(self.sg2[:, m * 512:(m + 1) * 512], bank.t[:, :], ACT.Sigmoid, t, f)
            bank.done(t)
            self.k_sg2 = t

    def branch(self, l, n, ready):
        f = self.fence() if n != 1 else []
        oh, ol = ((self.ph, self.pl), (self.oh, self.ol), (self.o2h, self.o2l))[n]
        rota = self.side2 if n < 2 else self.all4
        self.k_mrg = []
        late = None
        for m2 in range(4):
            sg = []
            for i in range(2):
                m = 2 * m2 + i
                if n == 2:
                    sg.append((self.sg2[:, m * 512:(m + 1) * 512], self.k_sg2, None))
                    continue
                (bank, t), = yield from self.proj_steps(5248 + n * 1024 + m * 128, rota=rota)
                tm = self.tmp.take()
                t = self.act(tm.t[:, :], bank.t[:, :], ACT.Sigmoid, t, tm.free)
                bank.done(t)
                sg.append((tm.t[:, :], t, tm))
            ys = yield from self.gemm_steps("w_branch", (l, n), 256 * m2, lambda k: oh[:, k * 512:(k + 1) * 512],
                             lambda k: ol[:, k * 512:(k + 1) * 512], ready, nk=4, groups=2, rota=rota)
            for i, (bank, t) in enumerate(ys):
                m = 2 * m2 + i
                s, t1, tm = sg[i]
                acc = self.mrg[:, m * 512:(m + 1) * 512]
                t = self.vtt(acc if n == 0 else s, s, bank.t[:, :], ALU.mult, t, t1, f)
                bank.done(t)
                if n:
                    t = self.vtt(acc, acc, s, ALU.add)
                if tm:
                    tm.done(t)
                if n == 2:
                    hi, lo = self.mh[:, m * 512:(m + 1) * 512], self.ml[:, m * 512:(m + 1) * 512]
                    t2 = self.S(lambda e, hi=hi, acc=acc: e.copy(hi, acc), t, f)
                    if late:
                        late()
                    late = lambda acc=acc, hi=hi, lo=lo, t2=t2: self.k_mrg.append(
                        [t2, self.vtt(lo, acc, hi.bitcast(F32), ALU.subtract, t2, f)])
        if late:
            late()

    def rope(self, src, dst, sw, cos, sin, w, *tokens):
        t = None
        for p in range(0, 128, 2 * w):
            for a, b in ((p, p + w), (p + w, p)):
                t = self.G(lambda e, a=a, b=b: e.tensor_copy(sw[a:a + w, :], src[b:b + w, :]), *tokens)
        self.vtt(dst, src, cos, ALU.mult, t, *tokens)
        self.vtt(sw, sw, sin, ALU.mult, t)
        return self.vtt(dst, dst, sw, ALU.add)

    def retention(self, l, f):
        vb = self.gemm_n("w_in", (l,), [0, 256, 512, 768], 2048, self.h_lhs, self.l_lhs, self.h_ready, self.ps)
        kv = []
        for t, (bank, tok) in enumerate(vb):
            kv.append(self.S(lambda e, t=t, bank=bank: e.copy(self.vret[:, t * 512:(t + 1) * 512], bank.t[:, :]), tok, f))
            bank.done(kv[-1])
        yield
        ready = self.ret_ready
        pfree, nfree = f, f
        for s in self.qk.slots:
            s.done(*f)
        for h in range(4):
            rot = []
            for base in (1024, 1536):
                (bank, t), = self.proj(base + h * 128)
                s = self.qk.take()
                src, dst, sw = s.t[:, 0:512], s.t[:, 512:1024], s.t[:, 1024:1536]
                t = self.S(lambda e, src=src, bank=bank: e.copy(src, bank.t[:, :]), t, s.free)
                bank.done(t)
                rot.append((s, dst, self.rope(src, dst, sw, self.cosr[:, :], self.sinr[:, :], 64, t, s.free, self.k_rot)))
                yield
            (bank, tg), = self.proj(2560 + h * 128)
            self.silu(self.sgr[:, :], bank, tg, f)
            yield
            (sq, q, tq), (sk, k, tk) = rot
            tp = []
            for j in range(4):
                pb = self.ps.take()
                n = 512 - 128 * j
                t = self.PE(lambda e, pb=pb, j=j, n=n, q=q, k=k: e.matmul(pb.t[:, 0:n], k[:, j * 128:(j + 1) * 128], q[:, j * 128:512],
                                                                          start=True, stop=True), pb.free, tq, tk)
                t = self.vtt(self.pt[:, j * 512:j * 512 + n], pb.t[:, 0:n], self.decay[:, h * 512:h * 512 + n], ALU.mult,
                             t, pfree, self.k_dc)
                pb.done(t)
                tp.append(t)
            sq.done(t)
            sk.done(t)
            ob = self.ps.take()
            for i in range(4):
                for j in range(i + 1):
                    t = self.PE(lambda e, i=i, j=j, ob=ob, h=h: e.matmul(
                        ob.t[:, i * 128:(i + 1) * 128], self.pt[:, j * 512 + (i - j) * 128:j * 512 + (i - j + 1) * 128],
                        self.vret[:, j * 512 + h * 128:j * 512 + (h + 1) * 128], start=j == 0, stop=j == i, skip_group_check=True),
                        ob.free, tp[j], kv[j], signal=i == j)
            pfree = [t]
            yield
            st = self.stat
            for i in range(4):
                self.V(lambda e, i=i, ob=ob: e.bn_stats(st[:, 16 + 6 * i:22 + 6 * i], ob.t[:, i * 128:(i + 1) * 128]), t)
                ts = self.V(lambda e, i=i: e.bn_aggr(st[:, 2 * i:2 * i + 2], st[:, 16 + 6 * i:22 + 6 * i]))
            r = self.rstd(st[:, 8:12], st[:, 0:8].rearrange("p (i two) -> p i two", two=2)[:, :, 1], 1.0, 1e-5, ts)
            for i in range(4):
                tn = self.vts(self.onat[:, i * 128:(i + 1) * 128], ob.t[:, i * 128:(i + 1) * 128], st[:, 2 * i:2 * i + 1],
                              st[:, 8 + i:9 + i], ALU.subtract, ALU.mult, r, nfree)
            ob.done(tn)
            tb = self.ps.take()
            t = self.transpose4([self.onat[:, i * 128:(i + 1) * 128] for i in range(4)], tb, tn, self.k_id)
            nfree = [t]
            yield
            t = self.stt(self.sgr[:, :], tb.t[:, :], self.col(("ret_g", l), h), self.sgr[:, :], ALU.mult, ALU.mult, t)
            tb.done(t)
            ready += self.split(self.sgr[:, :], self.oh[:, h * 512:(h + 1) * 512], self.ol[:, h * 512:(h + 1) * 512], t, f)
            self.S.wait(ready[-1])
            self.V.wait(ready[-2])

    def shifted(self, bank, tok, mu, out, f):
        t = self.S(lambda e, bank=bank: e.copy(self.PP[:, 1:513], bank.t[:, :]), tok, self.pp_free)
        bank.done(t)
        self.vtt(self.RT[7][:, :], self.PP[:, 0:512], self.PP[:, 1:513], ALU.subtract, t, f)
        t = self.stt(out, self.RT[7][:, :], mu, self.PP[:, 1:513], ALU.mult, ALU.add)
        self.pp_free = [t]
        return t

    def prepare_rwkv(self, l):
        A = self.A
        self.rw_f = f = self.fence()
        self.k_w2 = [self.load(self.w2a2[0:64, :], A["rwkv_w2"][l], f), self.load(self.w2a2[64:128, :], A["rwkv_a2"][l], f)]
        self.k_rs = self.load(self.reset[:, :], A["reset"], f)
        self.k_gm = [self.load(self.gmask[:, :], A["gmask"], f), self.load(self.m1[:, :], A["m1"], f),
                self.load(self.lmask[:, :], A["lmask"], f)]
        self.pp_free = [self.V(lambda e: e.memset(self.PP[:, 0:1], 0.0), f)]

    def rwkv(self, l):
        f, k_rs = self.rw_f, self.k_rs
        pieces = tuple(x for k in range(8) for x in ((128 * k, 3584, 64), (128 * k, 4672, 64)))
        (bank, t), = self.proj(0, pieces=pieces)
        t = self.shifted(bank, t, self.col(("mu_wa", l)), self.wa[:, :], f)
        k_wa = self.act(self.wa[0:64, :], self.wa[0:64, :], ACT.Tanh, t)
        RT = [x[:, :] for x in self.RT]
        yield
        for p in range(4):
            mu = lambda n: self.col((n, l), p)
            pb = self.ps.take()
            t = self.PE(lambda e, pb=pb, p=p: e.matmul(pb.t[:, :], self.w2a2[0:64, p * 128:(p + 1) * 128], self.wa[0:64, :],
                                                       start=True, stop=True), pb.free, k_wa, self.k_w2)
            sg, cum = RT[0], RT[1]
            t = self.act(sg, pb.t[:, :], ACT.Sigmoid, t, f, bias=mu("w0"))
            pb.done(t)
            self.V(lambda e: e.tensor_tensor_scan(cum, self.reset[:, :], sg, 0.0, ALU.mult, ALU.add), t, k_rs)
            c4 = cum.rearrange("p (c n) -> p c n", c=4)
            e4 = self.em[:, 16 * p:16 * p + 16]
            self.V(lambda e, e4=e4: e.tensor_copy(e4[:, 12:16], c4[:, :, 63]))
            tm = self.vtt(e4[:, 8:12], c4[:, :, 127], e4[:, 12:16], ALU.subtract)
            tm = self.V(lambda e, e4=e4: e.tensor_copy(e4[:, 4:8], c4[:, :, 127]))
            self.vtt(c4, c4, e4[:, 12:16].unsqueeze(2).broadcast_to([128, 4, 128]), ALU.subtract)
            td = self.vtt(sg, cum, sg, ALU.subtract)
            te = self.act(e4[:, 0:4], e4[:, 12:16], ACT.Exp, td, scale=-KAPPA)
            te = self.act(e4[:, 4:12], e4[:, 4:12], ACT.Exp, scale=-KAPPA)
            E1, E2, E3 = RT[2], RT[1], RT[0]
            self.act(E1, cum, ACT.Exp, scale=-KAPPA)
            self.act(E3, sg, ACT.Exp, scale=-KAPPA)
            te = self.act(E2, cum, ACT.Exp, scale=KAPPA)
            (bank, t), = self.proj(3072 + p * 128)
            yield
            r = RT[3]
            self.shifted(bank, t, mu("mu_r"), r, f)
            AR = self.AR[:, p * 1024:(p + 1) * 1024]
            self.vtt(AR[:, 512:1024], r, E1, ALU.mult, te)
            (bank, t), = self.proj(3648 + p * 128)
            yield
            k = RT[4]
            tk = self.shifted(bank, t, mu("mu_k"), k, f)
            pb = self.ps.take()
            t = self.PE(lambda e, pb=pb, p=p: e.matmul(pb.t[:, :], self.w2a2[64:128, p * 128:(p + 1) * 128], self.wa[64:128, :],
                                                       start=True, stop=True), pb.free, k_wa, self.k_w2)
            a = RT[5]
            ta = self.act(a, pb.t[:, :], ACT.Sigmoid, t, bias=mu("a0"))
            pb.done(ta)
            kk, q, am = RT[7], RT[6], RT[2]
            t = self.vts(kk, k, mu("k_k"), None, ALU.mult, None)
            t = self.act(q, kk, ACT.Square, t)
            (vb, tv), = self.proj(4160 + p * 128)
            pq = self.ps.take()
            tq = self.PE(lambda e, pq=pq: e.matmul(pq.t[:, :], self.blk64[:, :], q, start=True, stop=True), pq.free, t, *self.k_misc)
            self.vts(am, a, 1.0, mu("k_a"), ALU.subtract, ALU.mult, ta)
            self.stt(k, am, 1.0, k, ALU.add, ALU.mult)
            t = self.stt(r, r, mu("r_k"), k, ALU.mult, ALU.mult)
            self.vtt(self.KH[:, p * 512:(p + 1) * 512], k, E2, ALU.mult)
            yield
            yield
            pb = self.ps.take()
            tb = self.PE(lambda e, pb=pb: e.matmul(pb.t[:, :], self.blk64[:, :], r, start=True, stop=True), pb.free, t)
            t = self.vts(q, pq.t[:, :], 1e-24, None, ALU.max, None, tq)
            pq.done(t)
            t = self.act(q, q, ACT.Sqrt, t)
            self.V(lambda e: e.reciprocal(q, q), t)
            self.vtt(kk, kk, q, ALU.mult)
            self.stt(AR[:, 0:512], kk, -1.0, E3, ALU.mult, ALU.mult)
            self.vtt(kk, kk, a, ALU.mult)
            self.vtt(self.BH[:, p * 512:(p + 1) * 512], kk, E2, ALU.mult)
            v = RT[5]
            tv = self.shifted(vb, tv, mu("mu_v"), v, f)
            for _ in range(5):
                yield
            b2 = self.ps.take()
            t2 = self.transpose4([v[:, c * 128:(c + 1) * 128] for c in range(4)], b2, tv, self.k_id)
            vn = self.VN[:, :].rearrange("p (c q n) -> p c q n", c=4, q=4)[:, :, p, :]
            t3 = self.S(lambda e, b2=b2, vn=vn: e.copy(vn, b2.t[:, :].rearrange("p (c n) -> p c n", c=4)), t2)
            b2.done(t3)
            t = self.vtt(self.VB[:, p * 512:(p + 1) * 512], pb.t[:, :], v, ALU.mult, tb)
            pb.done(t)
            self.S.wait(t)
            self.V.wait(t3, te, t2)

    def rwkv_out(self, l):
        ready = []
        f = self.fence()
        late = None
        for p in range(4):
            (bank, t), = self.proj(4736 + p * 128)
            tm = self.tmp.take()
            y = self.KH[:, p * 512:(p + 1) * 512]
            t1 = self.act(tm.t[:, :], bank.t[:, :], ACT.Sigmoid, t, tm.free)
            self.vtt(y, y, self.VB[:, p * 512:(p + 1) * 512], ALU.add, f)
            if late:
                late()
            t2 = self.vtt(tm.t[:, :], bank.t[:, :], tm.t[:, :], ALU.mult, t1, t)
            bank.done(t2)
            t = self.vtt(y, y, tm.t[:, :], ALU.mult)
            tm.done(t)
            hi, lo = self.o2h[:, p * 512:(p + 1) * 512], self.o2l[:, p * 512:(p + 1) * 512]
            t2 = self.S(lambda e, hi=hi, y=y: e.copy(hi, y), t, f)
            late = lambda y=y, hi=hi, lo=lo, t2=t2: ready.extend([t2, self.vtt(lo, y, hi.bitcast(F32), ALU.subtract, t2, f)])
        late()
        return ready

    def chunks(self, l):
        f = self.fence()
        for z in self.sets:
            z["free"] = z["yfree"] = f
            z["kz"] = self.G(lambda e, z=z: e.memset(z["Y"][:, :], 0.0), f)
        stream = lambda g: itertools.chain.from_iterable(self.chunk(l, c, g) for c in range(4))
        yield from abreast(stream(0), itertools.chain(range(13), stream(1)))

    def chunk(self, l, c, g):
        cs = slice(c * 128, (c + 1) * 128)
        heads = [(4 * g + i, (4 * g + i) // 2, 64 * (i % 2)) for i in range(4)]
        z = self.sets[g]
        free, kz = z["free"], z["kz"]
        G4, X, U, Y = z["G4"], z["X"], z["U"], z["Y"]
        W4, SA, YQ = Y[:, 0:256], Y[:, 256:512], X[:, 0:256]
        v4 = lambda x: x[:, :].rearrange("p (h n) -> p h n", h=4)
        for i, (h, p, q) in enumerate(heads):
            bank = self.ps.take()
            ar = self.AR[q:q + 64, p * 1024:(p + 1) * 1024].rearrange("p (two n) -> p two n", two=2)[:, :, cs]
            for j, KB in enumerate((self.BH, self.KH)):
                o = bank.t[:, 256 * j:256 * j + 256].rearrange("p (two n) -> p two n", two=2)
                t = self.PE(lambda e, o=o, KB=KB, ar=ar, p=p, q=q: e.matmul(
                    o, KB[q:q + 64, p * 512 + c * 128:p * 512 + (c + 1) * 128], ar, start=True, stop=True, skip_group_check=True),
                    bank.free, free, signal=j == 1)
            t = self.vtt(G4[:, i * 512:(i + 1) * 512], bank.t[:, :], self.gmask[:, :], ALU.mult, t, free, self.k_gm)
            bank.done(t)
        yield
        kn = []
        for KB, KN in ((self.BH, z["BN"]), (self.KH, z["KN"])):
            bank = self.ps.take()
            tt = self.transpose4([KB[:, p * 512 + c * 128:p * 512 + (c + 1) * 128] for p in (2 * g, 2 * g + 1)], bank, self.k_id)
            kn.append(self.S(lambda e, KN=KN, bank=bank: e.copy(KN[:, :], bank.t[:, 0:256]), tt, free))
            bank.done(kn[-1])
        ga = G4[:, :].rearrange("p (h n) -> p h n", h=4)[:, :, 0:128]
        self.vtt(v4(U), ga, self.m1[:, :].unsqueeze(1).broadcast_to([128, 4, 128]), ALU.mult)
        tu = self.vtt(v4(U), v4(U), self.ident[:, :].unsqueeze(1).broadcast_to([128, 4, 128]), ALU.add, self.k_id)
        yield

        def four(bank, lhs, rhs, *tokens):
            for i in range(4):
                t = self.PE(lambda e, i=i: e.matmul(bank.t[:, i * 64:(i + 1) * 64], lhs(i), rhs(i), start=True, stop=True,
                                                    skip_group_check=True), bank.free, *tokens, signal=i == 3)
            return t

        blk = lambda x: (lambda i: x[:, i * 128:(i + 1) * 128])
        for lv, n in enumerate((2, 4, 8, 16, 32, 64)):
            bank = self.ps.take()
            t = self.transpose4([U[:, i * 128:(i + 1) * 128] for i in range(4)], bank, tu)
            nb = 64 // n
            part = lambda x, j, n=n: x.rearrange("p (b two n) -> p b two n", two=2, n=n)[:, :, j, :]
            four_part = lambda x, j, n=n: x[:, :].rearrange("p (h b two n) -> p h b two n", h=4, two=2, n=n)[:, :, :, j, :]
            tight = lambda x, n=n: x[:, 0:256].rearrange("p (h b n) -> p h b n", h=4, n=n)
            tx = self.S(lambda e, bank=bank, fp=four_part, ti=tight: e.copy(ti(X), fp(bank.t, 0)), t, free)
            bank.done(tx)
            yield
            yb = self.ps.take()
            t = four(yb, lambda i: G4[:, i * 512:i * 512 + 128], lambda i: X[:, i * 64:(i + 1) * 64], tx, tu)
            ty = self.S(lambda e, yb=yb, fp=four_part, ti=tight: e.copy(fp(Y, 0), ti(yb.t)), t, kz)
            yb.done(ty)
            yield
            wb = self.ps.take()
            tw = four(wb, blk(Y), lambda i, part=part: part(U[:, i * 128:(i + 1) * 128], 1), ty)
            if n < 32:
                m = (self.lmask[:, lv * 64:(lv + 1) * 64].rearrange("p (b n) -> p b n", n=n)
                     .unsqueeze(1).broadcast_to([128, 4, nb, n]))
                tu = self.V(lambda e, m=m, wb=wb, fp=four_part, ti=tight: e.copy_predicated(fp(U, 1), m, ti(wb.t)), tw)
            else:
                for b in range(nb):
                    s = 2 * n * b
                    tu = self.V(lambda e, wb=wb, s=s, b=b, n=n, ti=tight: e.tensor_copy(
                        v4(U)[s:s + n, :, s + n:s + 2 * n], ti(wb.t)[s:s + n, :, b, :]), tw)
            wb.done(tu)
            yield
            if c and lv == 0:
                z["tail"]()
        em = self.em[:, 32 * g:32 * g + 32].rearrange("p (t j c) -> p t j c", t=2, j=4)
        bc = lambda j: em[:, :, j, c].unsqueeze(2).broadcast_to([128, 2, 64])
        st = self.st[:, g * 128:(g + 1) * 128].rearrange("p (t v) -> p t v", t=2)
        S0 = z["SP"]
        spt = S0[:, :].rearrange("p (t j v) -> p t j v", t=2, j=2)
        ts = None
        if c == 0:
            self.V(lambda e: e.memset(S0[:, :], 0.0), free)
        else:
            for j in range(2):
                q = slice(64 * j, 64 * j + 64)
                ts = self.vtt(spt[q, :, j, :], st[q, :, :], bc(0)[q, :, :], ALU.mult, free)
        vn = lambda h: self.VN[:, c * 512 + h * 64:c * 512 + (h + 1) * 64]

        def from_state(bank, j):
            for t in range(2):
                a = self.AR[:, (2 * g + t) * 1024 + j * 512 + c * 128:(2 * g + t) * 1024 + j * 512 + (c + 1) * 128]
                o = bank.t[:, t * 128:(t + 1) * 128]
                self.PE(lambda e, o=o, a=a, t=t: e.matmul(o, a, S0[:, t * 128:(t + 1) * 128], start=t == 0, stop=False,
                                                          skip_group_check=True), ts, bank.free, signal=False)

        wb = self.ps.take()
        if c:
            from_state(wb, 0)
        for i, (h, p, q) in enumerate(heads):
            o = wb.t[:, i * 64:(i + 1) * 64]
            t = self.PE(lambda e, o=o, h=h, i=i: e.matmul(o, G4[:, i * 512 + 256:i * 512 + 384], vn(h), start=c == 0, stop=True,
                                                          skip_group_check=True), wb.free, signal=i == 3)
        t = self.S(lambda e, wb=wb: e.copy(W4, wb.t[:, 0:256]), t)
        wb.done(t)
        yield
        sb = self.ps.take()
        for i, (h, p, q) in enumerate(heads):
            t2 = self.PE(lambda e, i=i, sb=sb: e.matmul(sb.t[:, i * 64:(i + 1) * 64], U[:, i * 128:(i + 1) * 128],
                                                        W4[:, i * 64:(i + 1) * 64], start=True, stop=True, skip_group_check=True),
                         t, tu, sb.free, signal=i == 3)
        tsa = self.S(lambda e, sb=sb: e.copy(SA, sb.t[:, 0:256]), t2)
        sb.done(tsa)
        yield
        if c < 3:
            sb = self.ps.take()
            for i, (h, p, q) in enumerate(heads):
                o = sb.t[q:q + 64, (p - 2 * g) * 64:(p - 2 * g) * 64 + 64]
                for j, (KN, R) in enumerate(((z["BN"], SA[:, i * 64:(i + 1) * 64]), (z["KN"], vn(h)))):
                    t = self.PE(lambda e, o=o, KN=KN, R=R, i=i, j=j: e.matmul(o, KN[:, i * 64:(i + 1) * 64], R, start=j == 0, stop=j == 1,
                                                                              skip_group_check=True), kn, tsa, sb.free, signal=i == 3 and j == 1)
            sv = sb.t[:, 0:128].rearrange("p (t v) -> p t v", t=2)
            if c:
                sq = YQ[:, 0:128].rearrange("p (t v) -> p t v", t=2)
                self.vtt(st, st, bc(1), ALU.mult)
                t = self.vtt(sq, sv, bc(2), ALU.mult, t)
                self.vtt(st, st, sq, ALU.add)
            else:
                t = self.vtt(st, sv, bc(2), ALU.mult, t, free)
            sb.done(t)
        yb = self.ps.take()
        if c:
            from_state(yb, 1)
        for i, (h, p, q) in enumerate(heads):
            o = yb.t[:, i * 64:(i + 1) * 64]
            self.PE(lambda e, o=o, i=i: e.matmul(o, G4[:, i * 512 + 128:i * 512 + 256], SA[:, i * 64:(i + 1) * 64],
                                                 start=c == 0, stop=False, skip_group_check=True), tsa, yb.free, signal=False)
            ty = self.PE(lambda e, o=o, h=h, i=i: e.matmul(o, G4[:, i * 512 + 384:i * 512 + 512], vn(h), start=False, stop=True,
                                                           skip_group_check=True), signal=i == 3)
        y4 = yb.t[:, 0:256].rearrange("p (h n) -> p h n", h=4)
        n4, q4 = z["YN"][:, :].rearrange("p (h n) -> p h n", h=4), YQ.rearrange("p (h n) -> p h n", h=4)
        hs = z["hs"]
        self.V(lambda e: e.tensor_reduce(hs[:, 0:4], y4, AX.X, ALU.add), ty)
        self.vts(hs[:, 0:4], hs[:, 0:4], 1.0 / 64, None, ALU.mult, None)
        t = self.vtt(n4, y4, hs[:, 0:4].unsqueeze(2).broadcast_to([128, 4, 64]), ALU.subtract, z["yfree"])
        yb.done(t)
        self.vtt(q4, n4, n4, ALU.mult)
        t = self.V(lambda e: e.tensor_reduce(hs[:, 4:8], q4, AX.X, ALU.add))
        r = self.rstd(hs[:, 8:12], hs[:, 4:8], 1.0 / 64, 64e-5, t)
        z["free"] = [ty, t]

        def tail():
            t = self.vtt(n4, n4, hs[:, 8:12].unsqueeze(2).broadcast_to([128, 4, 64]), ALU.mult, r)
            bank = self.ps.take()
            t = self.transpose4([z["YN"][:, 0:128], z["YN"][:, 128:256]], bank, t)
            z["yfree"] = [t]
            for j in range(2):
                p = 2 * g + j
                tt = self.act(self.KH[:, p * 512 + c * 128:p * 512 + (c + 1) * 128], bank.t[:, j * 128:(j + 1) * 128],
                              ACT.Identity, t, bias=self.col(("ln_b", l), p), scale=self.col(("ln_w", l), p))
            bank.done(tt)

        if c == 3:
            yield
            tail()
        z["tail"] = tail
        yield

    def w_out(self, l):
        xr = self.x_ready
        self.x_ready = [[] for _ in range(4)]
        for half in range(2):
            rota = (self.all4, self.ps)[half]
            out = self.gemm_n("w_out", (l,), [0, 256, 512, 768], 512 * half,
                              lambda k, t: self.mh[:, k * 512 + t * 128:k * 512 + (t + 1) * 128],
                              lambda k, t: self.ml[:, k * 512 + t * 128:k * 512 + (t + 1) * 128], lambda k: self.k_mrg[k], rota,
                              late=(1, 3)[half])
            for t, (bank, tok) in enumerate(out):
                tm = self.tmp.take()
                a = self.vtt(tm.t[:, :], bank.t[:, :], self.gate[:, half * 512:(half + 1) * 512], ALU.mult, tok, tm.free, self.k_gate)
                bank.done(a)
                x = self.xn[:, t * 1024 + half * 512:t * 1024 + (half + 1) * 512]
                a = self.vtt(x, x, tm.t[:, :], ALU.add, xr[t])
                tm.done(a)
                self.x_ready[t].append(a)
        if l + 1 < DEPTH:
            self.k_xd = [self.load(self.A["xd"][t * 128:(t + 1) * 128, :], self.x_tile(t), *self.x_ready[t]) for t in range(4)]

    def rows(self, g, b):
        f = self.fence()
        k = [self.load(self.bc[:, 0:1024], g.partition_broadcast(128), f)]
        if b is not None:
            k.append(self.load(self.bc[:, 1024:2048], b.partition_broadcast(128), f))
        return k

    def to_hT_tile(self, t, *tokens):
        k = []
        for d4 in range(2):
            bank = self.ps.take()
            a = self.transpose4([self.xn[:, t * 1024 + d * 128:t * 1024 + (d + 1) * 128] for d in range(4 * d4, 4 * d4 + 4)],
                                bank, self.k_id, *tokens)
            o = lambda x: x[:, d4 * 2048:(d4 + 1) * 2048].rearrange("p (d n) -> p d n", d=4)[:, :, t * 128:(t + 1) * 128]
            s = self.split(bank.t[:, :].rearrange("p (d n) -> p d n", d=4), o(self.hh), o(self.hl), a, self.h_free)
            bank.done(*s)
            k += s
        self.h_ready += k
        self.h_tiles[t] = k
        return a

    def final_norm(self):
        kb = self.k_rows
        self.h_free, self.h_ready, self.pending = self.h_last, [], []
        for t in range(4):
            xt, ss, r = self.x_tile(t), self.stat[:, t:t + 1], self.stat[:, 4 + t:5 + t]
            s = self.V(lambda e, xt=xt, ss=ss: e.tensor_tensor_reduce(self.bc[:, 1024:2048], xt, xt, 1.0, 0.0, ALU.mult, ALU.add, ss),
                       self.x_ready[t])
            k = self.rstd(r, ss, 1.0 / D, 1e-6, s)
            k = self.stt(xt, xt, r, self.bc[:, 0:1024], ALU.mult, ALU.mult, k, kb)
            self.pending.append((t, k))
            self.x_ready[t] = [k]
        for p in self.pending[:2]:
            self.to_hT_tile(*p)
        self.pending = self.pending[2:]

    def layer_norm(self, l, name, eps, halves, out=False):
        A = self.A
        st = self.stat
        for t, (xt, k) in enumerate(halves):
            if t == 0:
                self.h_free, self.h_ready, self.pending = self.h_last, [], []
            if t > 1 and not out:
                self.to_hT_tile(*self.pending.pop(0))
            s = self.V(lambda e, t=t: e.bn_aggr(st[:, 4 * t:4 * t + 2], st[:, 16 + 12 * t:28 + 12 * t]), k)
            r = self.rstd(st[:, 4 * t + 2:4 * t + 3], st[:, 4 * t + 1:4 * t + 2], 1.0, eps, s)
            self.stt(xt, xt, st[:, 4 * t:4 * t + 1], self.bc[:, 0:1024], ALU.subtract, ALU.mult, self.k_rows)
            k = self.stt(xt, xt, st[:, 4 * t + 2:4 * t + 3], self.bc[:, 1024:2048], ALU.mult, ALU.add, r)
            self.x_ready[t] = [k]
            if not out:
                self.pending.append((t, k))

    def ffn(self, l, name, ln):
        f = self.fence()
        ready = []
        early = self.gemm_halves(name + "_w_gu_2", (l,), [0, FF])
        for m in range(NFF):
            if m == 0:
                (gb, tg), (ub, tu) = early
            else:
                (gb, tg), = self.gemm_t(name + "_w_gu_2", (l,), m * 128, self.h_rhs, self.l_rhs, self.h_ready)
                (ub, tu), = self.gemm_t(name + "_w_gu_2", (l,), FF + m * 128, self.h_rhs, self.l_rhs, self.h_ready)
            tm = self.tmp.take()
            t = self.act(tm.t[:, :], gb.t[:, :], ACT.Silu, tg, tm.free)
            gb.done(t)
            t = self.vtt(tm.t[:, :], tm.t[:, :], ub.t[:, :], ALU.mult, t, tu)
            ub.done(t)
            k = self.split(tm.t[:, :], self.fh[:, m * 512:(m + 1) * 512], self.fl[:, m * 512:(m + 1) * 512], t, f)
            tm.done(*k)
            ready += k
        return self.project(name + "_w_down_2", l, [256 * i for i in range(11)],
                            self.fh, self.fl, lambda k: ready[2 * k:2 * k + 2], 2 * ALPHA, ln)

    def project(self, name, l, k0s, ah, al, ready, s, ln):
        self.h_last = [self.PE.last()]
        self.k_rows = self.rows(self.A[ln + "_g_2"][l], self.A[ln + "_b_2"][l])
        xr = [[] for _ in range(4)]
        for half in range(2):
            rota = (self.ps, self.all4)[half]
            out = self.gemm_tiles(name, (l,), k0s, 512 * half, lambda k, t: ah[:, k * 512 + t * 128:k * 512 + (t + 1) * 128],
                              lambda k, t: al[:, k * 512 + t * 128:k * 512 + (t + 1) * 128], ready, rota, late=(1, 2)[half])
            for t, (bank, tok) in enumerate(out):
                x = self.xn[:, t * 1024 + half * 512:t * 1024 + (half + 1) * 512]
                a = self.stt(x, x, s, bank.t[:, :], ALU.mult, ALU.add, tok, self.x_ready[t])
                bank.done(a)
                xr[t].append(a)
                st = self.stat[:, 16 + 12 * t + 6 * half:22 + 12 * t + 6 * half]
                self.V(lambda e, x=x, st=st: e.bn_stats(st, x))
                if half:
                    yield self.x_tile(t), xr[t]

    def layer_b(self, l):
        self.layer_norm(l, "ln1", 4e-5, self.ffn(l, "ffn1", "ln1"))
        self.layer_norm(l, "ln2", 1e-5, self.mixer(l))
        self.layer_norm(l, "ln3", 4e-5, self.ffn(l, "ffn2", "ln3"), out=l == DEPTH - 1)

    def mixer(self, l):
        A = self.A
        f = self.fence()
        k_c = [self.load(self.rcos[:, :], A["rcos"], f), self.load(self.rsin[:, :], A["rsin"], f),
               self.load(self.amask[:, :], A["amask"], f), self.load(self.mean256[:, :], A["mean256"], f),
               self.load(self.sink[:, :], A["attn_sink_2"][l].partition_broadcast(128), f)]
        proj = lambda col, rota: self.gemm_t("w_in_2", (l,), col, self.h_rhs, self.l_rhs, self.h_ready, rota=rota)[0]

        def steps(col, rota):
            out = yield from self.gemm_steps("w_in_2", (l,), col, self.h_rhs, self.l_rhs, self.h_ready, rota=rota)
            return out[0]

        z = [x[:, :] for x in self.t3]
        half = lambda x, j: x[:, j * 512:(j + 1) * 512]
        cp = self.ccp[:, :].rearrange("p (j n) -> p j n", j=2)
        self.V(lambda e: e.memset(self.ccp[:, :], 0.0), f)
        self.V(lambda e: e.memset(self.scp[:, :], 0.0), f)
        ready = [None] * 8
        zt = None
        early = self.gemm_halves("w_in_2", (l,), [1536, 1792])
        for j in range(2):
            (ba, ta), (bg, tg) = (proj(1664, self.all4), proj(1920, self.all4)) if j else early
            t = self.act(z[0], bg.t[:, :], ACT.Sigmoid, tg, f, zt)
            bg.done(t)
            zt = t = self.vtt(cp[:, j, 15:527], ba.t[:, :], z[0], ALU.mult, t, ta)
            ba.done(t)
        wide = self.wide_conv(l, cp, half, ready, k_c, f)
        side = abreast(wide, self.short_conv(l, steps, half, ready, zt, f))
        rot, swt = [], None
        for n in range(5):
            b_, t = proj(768 + n * 128, self.main2)
            r = self.rq.take()
            dst = half(self.qT, n) if n < 4 else self.kT[:, :]
            t = self.S(lambda e, b_=b_, r=r: e.copy(r.t[:, 0:512], b_.t[:, :]), t, r.free, f)
            b_.done(t)
            rot.append(self.rope(r.t[:, 0:512], dst, r.t[:, 512:1024], self.rcos[:, :], self.rsin[:, :], 32, t, k_c, f, r.free))
            r.done(rot[-1])
            for _ in range(5):
                next(wide, None)
                next(side, None)
        self.G(lambda e: e.tensor_copy(self.kS[0:64, :], self.kT[64:128, :]), rot, f)
        rot.append(self.G(lambda e: e.tensor_copy(self.kS[64:128, :], self.kT[0:64, :])))
        wh, wl, tok, n = self.unit("w_in_2", (l,), t_pieces(1408))
        vk = self.ps.take()
        for t in range(4):
            for k in range(8):
                tv = self.mm3(vk.t[:, t * 128:(t + 1) * 128], self.h_lhs(k, t), self.l_lhs(k, t), wh[:, k * 128:(k + 1) * 128],
                              wl[:, k * 128:(k + 1) * 128], k == 0, k == 7, tok, vk.free, self.h_ready)
        self.used[n] = tv
        kv = self.S(lambda e: e.copy(self.v2[:, :], vk.t[:, :]), tv, f)
        vk.done(kv)
        mix(self.attention(rot, kv, ready, k_c, f), side, 76, 66)
        drain(side)
        yield from self.project("w_out_2", l, [0, 256, 512, 768], self.xh8, self.xl8, lambda k: ready[k], ALPHA, "ln2")

    def short_conv(self, l, proj, half, ready, zt, f):
        sp = self.scp[:, :].rearrange("p (j n) -> p j n", j=2)
        z = [x[:, :] for x in self.t3]
        for j in range(2):
            b_, t = yield from proj(256 + j * 128, self.side2)
            t = self.S(lambda e, b_=b_: e.copy(z[0], b_.t[:, :]), t, zt)
            b_.done(t)
            b_, th = yield from proj(512 + j * 128, self.side2)
            zt = self.vtt(sp[:, j, 1:513], z[0], b_.t[:, :], ALU.mult, t, th)
            b_.done(zt)
            self.vts(z[1], sp[:, j, 0:512], self.col(("sc", l, 0), j), None, ALU.mult, None)
            for w in (1, 2):
                self.stt(z[1], sp[:, j, w:w + 512], self.col(("sc", l, w), j), z[1], ALU.mult, ALU.add)
            b_, tb = yield from proj(j * 128, self.side2)
            t = self.vtt(z[1], z[1], b_.t[:, :], ALU.mult, tb)
            b_.done(t)
            k = self.split(z[1], half(self.xh8, j), half(self.xl8, j), t, f)
            self.V.wait(*k)
            ready[j] = k

    def wide_conv(self, l, cp, half, ready, k_c, f):
        for j in range(2):
            ac = half(self.acc, j)
            self.vts(ac, cp[:, j, 0:512], self.col(("cc", l, 0), j), self.col(("cc_b", l), j), ALU.mult, ALU.add, f)
            for w in range(1, 31):
                t = self.stt(ac, cp[:, j, w:w + 512], self.col(("cc", l, w), j), ac, ALU.mult, ALU.add)
                yield
        z = self.zc
        mb = self.ps.take()
        for j in range(2):
            t2 = self.PE(lambda e, j=j: e.matmul(mb.t[:, :], self.mean256[:, :], half(self.acc, j), start=j == 0, stop=j == 1),
                         t, mb.free, k_c)
        for j in range(2):
            t = self.vtt(half(self.acc, j), half(self.acc, j), mb.t[:, :], ALU.subtract, t2)
        mb.done(t)
        t3 = self.act(z[:, :], self.acc[:, :], ACT.Square, t, f)
        yield
        vb = self.ps.take()
        for j in range(2):
            t4 = self.PE(lambda e, j=j: e.matmul(vb.t[:, :], self.mean256[:, :], half(z, j), start=j == 0, stop=j == 1), t3, vb.free)
        t = self.vts(z[:, 0:512], vb.t[:, :], 1e-5, None, ALU.add, None, t4)
        vb.done(t)
        t = self.act(z[:, 0:512], z[:, 0:512], ACT.Sqrt, t)
        yield
        self.V(lambda e: e.reciprocal(z[:, 0:512], z[:, 0:512]), t)
        for j in range(2):
            ac = half(self.acc, j)
            t = self.stt(ac, ac, self.col(("cc_lg", l), j), z[:, 0:512], ALU.mult, ALU.mult)
            t = self.act(ac, ac, ACT.Silu, t, bias=self.col(("cc_lb", l), j))
            ready[6 + j] = self.split(ac, half(self.xh8, 6 + j), half(self.xl8, 6 + j), t, f)

    def attention(self, rot, kv, ready, k_c, f):
        outs = {}
        last = None
        parts = []

        def scores(nb, kvh):
            k0, nk = max(nb - 1, 0), min(nb + 2, 4) - max(nb - 1, 0)
            mo = (k0 - nb + 1) * 128
            sm = self.sm.take()
            s = sm.t
            P = []
            for i in range(4):
                h = 4 * kvh + i
                p, q = h // 2, 64 * (h % 2)
                sb, pr = self.ps.take(), self.pr.take()
                kt = self.kT if q == 64 * kvh else self.kS
                t = self.PE(lambda e, sb=sb, p=p, q=q, kt=kt: e.matmul(
                    sb.t[:, 0:nk * 128], self.qT[q:q + 64, p * 512 + nb * 128:p * 512 + (nb + 1) * 128],
                    kt[q:q + 64, k0 * 128:(k0 + nk) * 128], start=True, stop=True), sb.free, rot)
                P.append(pr)
                t = self.V(lambda e, pr=pr, sb=sb, i=i: e.tensor_tensor_reduce(
                    pr.t[:, 0:nk * 128], sb.t[:, 0:nk * 128], self.amask[:, mo:mo + nk * 128], 1.0, -3e38, ALU.add, ALU.max,
                    s[:, i:i + 1]), t, pr.free, sm.free, k_c, f)
                sb.done(t)
                yield
            sk = self.sink[:, 4 * kvh:4 * kvh + 4]
            self.stt(s[:, 0:4], s[:, 0:4], 0.125, sk, ALU.mult, ALU.max)
            self.vts(s[:, 4:8], s[:, 0:4], -1.0, None, ALU.mult, None)
            t = self.vtt(s[:, 8:12], sk, s[:, 0:4], ALU.subtract)
            return nb, kvh, k0, nk, sm, P, t

        def weights(nb, kvh, k0, nk, sm, P, t):
            s = sm.t
            te = []
            for i in range(4):
                x = P[i].t[:, 0:nk * 128]
                te.append(self.S(lambda e, x=x, i=i: e.activation(x, x, ACT.Exp, bias=s[:, 4 + i:5 + i], scale=0.125,
                                                                  accum_out=s[:, 12 + i:13 + i]), t))
            t = self.act(s[:, 8:12], s[:, 8:12], ACT.Exp)
            self.vtt(s[:, 8:12], s[:, 8:12], s[:, 12:16], ALU.add, t)
            t = self.V(lambda e: e.reciprocal(s[:, 16:20], s[:, 8:12]))
            return nb, kvh, k0, nk, sm, P, te, t

        def values(nb, kvh, k0, nk, sm, P, te, td):
            ob = self.main2.take()
            def turned(i):
                tb, pT = self.ps.take(), self.prT.take()
                t = self.transpose4([P[i].t[:, j * 128:(j + 1) * 128] for j in range(nk)], tb, te[i], self.k_id)
                P[i].done(t)
                t = self.S(lambda e, pT=pT, tb=tb: e.copy(pT.t[:, 0:nk * 128], tb.t[:, 0:nk * 128]), t, pT.free)
                tb.done(t)
                return pT, t

            ahead = [turned(0), turned(1)]
            yield
            for i in range(4):
                h = 4 * kvh + i
                pT, t = ahead[i]
                for j in range(nk):
                    to = self.PE(lambda e, h=h, j=j, pT=pT: e.matmul(
                        ob.t[:, h * 64:(h + 1) * 64], pT.t[:, j * 128:(j + 1) * 128],
                        self.v2[:, (k0 + j) * 128 + kvh * 64:(k0 + j) * 128 + kvh * 64 + 64], start=j == 0, stop=j == nk - 1,
                        skip_group_check=True), t, kv, ob.free, signal=j == nk - 1)
                pT.done(to)
                if i < 2:
                    ahead.append(turned(i + 2))
                yield
            ao = self.ao.take() if kvh == 0 else outs["ao"]
            outs["ao"] = ao
            o = slice(kvh * 256, kvh * 256 + 256)
            t = self.vtt(ao.t[:, o].rearrange("p (h n) -> p h n", h=4), ob.t[:, o].rearrange("p (h n) -> p h n", h=4),
                         sm.t[:, 16:20].unsqueeze(2).broadcast_to([128, 4, 64]), ALU.mult, to, ao.free)
            sm.done(t)
            ob.done(t)
            if kvh == 0:
                return
            tb = self.ps.take()
            t = self.transpose4([ao.t[:, i * 128:(i + 1) * 128] for i in range(4)], tb, t)
            ao.done(t)
            v8 = lambda x: x[:, 1024:3072].rearrange("p (j n) -> p j n", j=4)[:, :, nb * 128:(nb + 1) * 128]
            k = self.split(tb.t[:, :].rearrange("p (j n) -> p j n", j=4), v8(self.xh8), v8(self.xl8), t, f)
            tb.done(*k)
            parts.extend(k)

        for nb in range(4):
            for kvh in range(2):
                now = yield from scores(nb, kvh)
                if last:
                    yield from values(*last)
                last = weights(*now)
                yield
        yield from values(*last)
        for j in range(2, 6):
            ready[j] = parts

    def finish(self):
        n = 0
        for t in range(4):
            self.SP.wait(*self.x_ready[t])
            x = self.x_tile(t)
            o = self.A["out"][0, t * 128:(t + 1) * 128, :]
            self.SP.todo.append(lambda e, o=o, x=x: e.dma_start(o, x).then_inc(self.s_out, 16))
            n += 16
        self.SP.todo.append(lambda e: e.wait_ge(self.s_out, n))


def program(nc, A, plan=None):
    p = Program(nc, A, plan)
    if plan is not None:
        p.run()
    return p


_DIRECT = ["x", "positions", "b_ada", "pool_w", "rwkv_w2", "rwkv_a2", "final_g", "attn_sink_2",
           "ln1_g_2", "ln1_b_2", "ln2_g_2", "ln2_b_2", "ln3_g_2", "ln3_b_2"]


def kernel(**inputs):
    import concourse.bacc as bacc
    from concourse.bass_utils import run_bass_kernel_spmd

    inputs = {k: np.asarray(v) for k, v in inputs.items()}
    nc = bacc.Bacc("TRN2", target_bir_lowering=False, num_devices=1)
    spec = columns()
    arrays = {}
    for name in _DIRECT:
        arrays[name] = np.ascontiguousarray(inputs[name])
    cols = np.empty((128, len(spec.pieces)), np.float32)
    flat = {}
    for j, col in enumerate(spec.pieces):
        at = 0
        for name, index, s, n in col:
            v = inputs[name][index].reshape(-1)
            cols[at:at + n, j] = v[s:s + n]
            at += n
    arrays["cols"] = cols
    arrays.update(constants())

    def declare(nc, nu):
        A = {}
        for name, a in arrays.items():
            A[name] = nc.dram_tensor(f"in_{name}", a.shape, mybir.dt.from_np(a.dtype), kind="ExternalInput").ap()
        A["W"] = nc.dram_tensor("in_W", (nu, 128, 1024), F32, kind="ExternalInput").ap()
        A["out"] = nc.dram_tensor("out", (1, T, D), F32, kind="ExternalOutput").ap()
        A["rot"] = nc.dram_tensor("rot", (2, 128, 512), F32, kind="Internal").ap()
        A["xd"] = nc.dram_tensor("xd", (T, D), F32, kind="Internal").ap()
        return A

    draft = bacc.Bacc("TRN2", target_bir_lowering=False, num_devices=1)
    plan = program(draft, declare(draft, 1)).kinds
    prog = program(nc, declare(nc, len(plan)), plan)
    arrays["W"] = pack_units(prog.units, inputs)
    r = run_bass_kernel_spmd(nc, [{f"in_{k}": v for k, v in arrays.items()}], core_ids=[0])
    return r.results[0]["out"]
```
